# Optimizing a Trainium2 kernel written in Bass

```python
import math
import jax, jax.numpy as jnp
from jax import lax
import numpy as np

D_MODEL = 1024
BATCH = 1
SEQ = 1024
DEPTH = 1

GRID_W = 64
CTX_LEN = 256
EPS = 1e-6

GLA_HEADS = 4
GLA_DK = D_MODEL // 16
GLA_DV = D_MODEL // 8
GLA_QK = GLA_HEADS * GLA_DK
GLA_V = GLA_HEADS * GLA_DV
GLA_RANK = 16
GLA_TAU = 16.0
GLA_CHUNK = 16

GDN_HEADS = 4
GDN_DK = D_MODEL // 8
GDN_DV = D_MODEL // 8
GDN_QK = GDN_HEADS * GDN_DK
GDN_V = GDN_HEADS * GDN_DV
GDN_CONV_DIM = 2 * GDN_QK + GDN_V
CONV_W = 3
GDN_CHUNK = 64

D_MIX = GLA_V + GDN_V
D_FF = 4 * D_MODEL
PROJ_WIDTHS = (GLA_QK, GLA_QK, GLA_V, GLA_V, GLA_RANK, GDN_CONV_DIM, GDN_V, 2 * GDN_HEADS, 2 * GDN_HEADS)
PROJ_DIM = GLA_QK * 2 + GLA_V * 2 + GLA_RANK + GDN_CONV_DIM + GDN_V + 4 * GDN_HEADS

kernel_name = "hybrid_gla_gdn_prefix_dit"

def rmsnorm(x, g):
    xf = x.astype(jnp.float32)
    y = xf * lax.rsqrt(jnp.mean(xf * xf, axis=-1, keepdims=True) + EPS)
    return (y * g.astype(jnp.float32)).astype(x.dtype)

def l2norm(x):
    return x * lax.rsqrt(jnp.sum(x * x, axis=-1, keepdims=True) + EPS)

def _heads(u, n_heads):
    B, T, _ = u.shape
    return u.reshape(B, T, n_heads, -1).transpose(0, 2, 1, 3)

def short_conv(u, w, rows):
    B, T, C = u.shape
    if rows is not None:
        u = u.reshape(B, rows, GRID_W, C)
    pad = CONV_W // 2
    up = jnp.pad(u, [(0, 0)] * (u.ndim - 2) + [(pad, pad), (0, 0)])
    L = u.shape[-2]
    y = sum(w[i] * up[..., i:i + L, :] for i in range(CONV_W))
    return y.reshape(B, T, C)

def gla_chunked(q, k, v, log_a, S0):
    B, H, T, DK = q.shape
    DV = v.shape[-1]
    C = GLA_CHUNK
    N = T // C
    q = q.reshape(B, H, N, C, DK)
    k = k.reshape(B, H, N, C, DK)
    v = v.reshape(B, H, N, C, DV)
    b = jnp.cumsum(log_a.reshape(B, H, N, C, DK), axis=3)
    b_last = b[:, :, :, -1:, :]
    causal = jnp.tril(jnp.ones((C, C), dtype=bool))[:, :, None]
    diff = b[:, :, :, :, None, :] - b[:, :, :, None, :, :]
    decay = jnp.exp(jnp.where(causal, diff, -jnp.inf))
    scores = jnp.sum(q[:, :, :, :, None, :] * k[:, :, :, None, :, :] * decay, axis=-1)
    intra = jnp.einsum('bhnij,bhnje->bhnie', scores, v)
    dS = jnp.einsum('bhnjd,bhnje->bhnde', k * jnp.exp(b_last - b), v)
    a_chunk = jnp.exp(b_last[:, :, :, 0, :])

    def step(S, inp):
        a_n, dS_n = inp
        return a_n[..., None] * S + dS_n, S

    S_fin, S_prev = lax.scan(step, S0, (jnp.moveaxis(a_chunk, 2, 0), jnp.moveaxis(dS, 2, 0)))
    S_prev = jnp.moveaxis(S_prev, 0, 2)
    inter = jnp.einsum('bhnid,bhnde->bhnie', q * jnp.exp(b), S_prev)
    return (intra + inter).reshape(B, H, T, DV), S_fin

def gdn_chunked(q, k, v, log_alpha, beta, S0):
    B, H, T, DK = q.shape
    DV = v.shape[-1]
    C = GDN_CHUNK
    N = T // C
    q = q.reshape(B, H, N, C, DK)
    k = k.reshape(B, H, N, C, DK)
    v = v.reshape(B, H, N, C, DV)
    beta = beta.reshape(B, H, N, C)
    g = jnp.cumsum(log_alpha.reshape(B, H, N, C), axis=-1)
    g_last = g[..., -1:]
    strict = jnp.tril(jnp.ones((C, C), dtype=bool), -1)
    incl = jnp.tril(jnp.ones((C, C), dtype=bool))
    gdiff = g[..., :, None] - g[..., None, :]
    kk = jnp.einsum('bhnid,bhnjd->bhnij', k, k)
    L = jnp.where(strict, beta[..., :, None] * kk * jnp.exp(jnp.where(strict, gdiff, 0.0)), 0.0)
    A = jnp.eye(C, dtype=L.dtype) + L
    U = lax.linalg.triangular_solve(A, beta[..., None] * v, left_side=True, lower=True, unit_diagonal=True)
    W = lax.linalg.triangular_solve(A, (beta * jnp.exp(g))[..., None] * k, left_side=True, lower=True,
                                    unit_diagonal=True)
    qk = jnp.einsum('bhnid,bhnjd->bhnij', q, k)
    Aqk = jnp.where(incl, qk * jnp.exp(jnp.where(incl, gdiff, 0.0)), 0.0)
    q_dec = q * jnp.exp(g)[..., None]
    k_dec = k * jnp.exp(g_last - g)[..., None]
    a_chunk = jnp.exp(g_last[..., 0])

    def step(S, inp):
        U_n, W_n, Aqk_n, qd_n, kd_n, a_n = inp
        delta = U_n - jnp.einsum('bhcd,bhde->bhce', W_n, S)
        o = jnp.einsum('bhcd,bhde->bhce', qd_n, S) + jnp.einsum('bhij,bhje->bhie', Aqk_n, delta)
        S_new = a_n[..., None, None] * S + jnp.einsum('bhcd,bhce->bhde', kd_n, delta)
        return S_new, o

    xs = tuple(jnp.moveaxis(t, 2, 0) for t in (U, W, Aqk, q_dec, k_dec, a_chunk))
    S_fin, o = lax.scan(step, S0, xs)
    return jnp.moveaxis(o, 0, 2).reshape(B, H, T, DV), S_fin

def prepare_mixers(h, w_in, w_lr, b_lr, conv_w, a_log, dt_bias, rows):
    f32 = jnp.float32
    B, T, _ = h.shape
    p = h @ w_in
    splits = np.cumsum(PROJ_WIDTHS)[:-1].tolist()
    q_a, k_a, v_a, g_a, r_a, qkv_b, g_b, a_b, beta_b = jnp.split(p, splits, axis=-1)
    gla_q = _heads(q_a.astype(f32), GLA_HEADS) * GLA_DK ** -0.5
    gla_k = _heads(k_a.astype(f32), GLA_HEADS)
    gla_v = _heads(v_a.astype(f32), GLA_HEADS)
    lr = jnp.einsum('btr,zrk->zbtk', r_a, w_lr) + b_lr[:, None, None, :]
    gla_log_a = (jax.nn.log_sigmoid(lr.astype(f32)) / GLA_TAU)
    gla_log_a = gla_log_a.reshape(2, B, T, GLA_HEADS, GLA_DK).transpose(0, 1, 3, 2, 4)
    qkv = jax.nn.silu(short_conv(qkv_b, conv_w, rows)).astype(f32)
    q_b, k_b, v_b = jnp.split(qkv, [GDN_QK, 2 * GDN_QK], axis=-1)
    gdn_q = l2norm(_heads(q_b, GDN_HEADS)) * GDN_DK ** -0.5
    gdn_k = l2norm(_heads(k_b, GDN_HEADS))
    gdn_v = _heads(v_b, GDN_HEADS)
    a = a_b.astype(f32).reshape(B, T, 2, GDN_HEADS)
    log_alpha = -jnp.exp(a_log.astype(f32)) * jax.nn.softplus(a + dt_bias.astype(f32))
    gdn_log_alpha = log_alpha.transpose(2, 0, 3, 1)
    gdn_beta = jax.nn.sigmoid(beta_b.astype(f32).reshape(B, T, 2, GDN_HEADS)).transpose(2, 0, 3, 1)
    return dict(gla_q=gla_q, gla_k=gla_k, gla_v=gla_v, gla_log_a=gla_log_a, gla_g=g_a.astype(f32),
                gdn_q=gdn_q, gdn_k=gdn_k, gdn_v=gdn_v, gdn_log_alpha=gdn_log_alpha, gdn_beta=gdn_beta,
                gdn_g=g_b.astype(f32))

def run_mixers(p, init):
    B = p['gla_q'].shape[0]
    if init is None:
        zg = jnp.zeros((B, GLA_HEADS, GLA_DK, GLA_DV), jnp.float32)
        zd = jnp.zeros((B, GDN_HEADS, GDN_DK, GDN_DV), jnp.float32)
        init = (zg, zg, zd, zd)
    o_gla, o_gdn, fin_gla, fin_gdn = 0.0, 0.0, [], []
    for d in range(2):
        f = (lambda u: jnp.flip(u, axis=2)) if d == 1 else (lambda u: u)
        oa, sa = gla_chunked(f(p['gla_q']), f(p['gla_k']), f(p['gla_v']), f(p['gla_log_a'][d]), init[d])
        ob, sb = gdn_chunked(f(p['gdn_q']), f(p['gdn_k']), f(p['gdn_v']), f(p['gdn_log_alpha'][d]),
                             f(p['gdn_beta'][d]), init[2 + d])
        o_gla = o_gla + f(oa)
        o_gdn = o_gdn + f(ob)
        fin_gla.append(sa)
        fin_gdn.append(sb)
    return o_gla, o_gdn, (fin_gla[0], fin_gla[1], fin_gdn[0], fin_gdn[1])

def merge_heads(o_gla, o_gdn, p, gla_norm_g, gdn_norm_g, w_out, dtype):
    B, _, T, _ = o_gla.shape
    ya = rmsnorm(o_gla, gla_norm_g).transpose(0, 2, 1, 3).reshape(B, T, GLA_V) * jax.nn.silu(p['gla_g'])
    yb = rmsnorm(o_gdn, gdn_norm_g).transpose(0, 2, 1, 3).reshape(B, T, GDN_V) * jax.nn.silu(p['gdn_g'])
    return jnp.concatenate([ya, yb], axis=-1).astype(dtype) @ w_out

def sq_relu_mlp(h, w1, w2):
    return jnp.square(jax.nn.relu(h @ w1)) @ w2

def setup_inputs(seed: int = 0) -> dict:
    key = jax.random.key(seed)
    ks = jax.random.split(key, 20)
    f32 = jnp.float32

    def nrm(k, shape, scale):
        return jax.random.normal(k, shape, f32) * scale

    x = nrm(ks[0], (BATCH, SEQ, D_MODEL), 1.0)
    c = nrm(ks[1], (BATCH, D_MODEL), 1.0)
    ctx = nrm(ks[2], (BATCH, CTX_LEN, D_MODEL), 1.0)
    c_ctx = nrm(ks[3], (D_MODEL,), 1.0)
    w_ada = nrm(ks[4], (DEPTH, D_MODEL, 6 * D_MODEL), 0.5 * D_MODEL ** -0.5)
    b_ada = nrm(ks[5], (DEPTH, 6 * D_MODEL), 0.01)
    norm1_g = 1.0 + nrm(ks[6], (DEPTH, D_MODEL), 0.02)
    norm2_g = 1.0 + nrm(ks[7], (DEPTH, D_MODEL), 0.02)
    w_in = nrm(ks[8], (DEPTH, D_MODEL, PROJ_DIM), D_MODEL ** -0.5)
    gla_w_lr = nrm(ks[9], (DEPTH, 2, GLA_RANK, GLA_QK), GLA_RANK ** -0.5)
    gla_b_lr = nrm(ks[10], (DEPTH, 2, GLA_QK), 0.1)
    gdn_conv_w = nrm(ks[11], (DEPTH, CONV_W, GDN_CONV_DIM), CONV_W ** -0.5)
    gdn_a_log = jnp.log(jax.random.uniform(ks[12], (DEPTH, 2, GDN_HEADS), f32, 1.0, 16.0))
    dt = jnp.exp(jax.random.uniform(ks[13], (DEPTH, 2, GDN_HEADS), f32, math.log(1e-3), math.log(1e-1)))
    gdn_dt_bias = dt + jnp.log(-jnp.expm1(-dt))
    gla_norm_g = 1.0 + nrm(ks[14], (DEPTH, GLA_DV), 0.02)
    gdn_norm_g = 1.0 + nrm(ks[15], (DEPTH, GDN_DV), 0.02)
    w_out = nrm(ks[16], (DEPTH, D_MIX, D_MODEL), D_MIX ** -0.5)
    w_ff1 = nrm(ks[17], (DEPTH, D_MODEL, D_FF), D_MODEL ** -0.5)
    w_ff2 = nrm(ks[18], (DEPTH, D_FF, D_MODEL), D_FF ** -0.5)
    final_norm_g = 1.0 + nrm(ks[19], (D_MODEL,), 0.02)
    return {"x": x, "c": c, "ctx": ctx, "c_ctx": c_ctx, "w_ada": w_ada, "b_ada": b_ada,
            "norm1_g": norm1_g, "norm2_g": norm2_g, "w_in": w_in, "gla_w_lr": gla_w_lr,
            "gla_b_lr": gla_b_lr, "gdn_conv_w": gdn_conv_w, "gdn_a_log": gdn_a_log,
            "gdn_dt_bias": gdn_dt_bias, "gla_norm_g": gla_norm_g, "gdn_norm_g": gdn_norm_g,
            "w_out": w_out, "w_ff1": w_ff1, "w_ff2": w_ff2, "final_norm_g": final_norm_g}

def reference(x, c, ctx, c_ctx, w_ada, b_ada, norm1_g, norm2_g, w_in, gla_w_lr, gla_b_lr, gdn_conv_w,
              gdn_a_log, gdn_dt_bias, gla_norm_g, gdn_norm_g, w_out, w_ff1, w_ff2, final_norm_g):
    B, T, _ = x.shape
    rows = T // GRID_W
    xc = ctx
    silu_c = jax.nn.silu(c)
    silu_cc = jax.nn.silu(c_ctx)
    for l in range(DEPTH):
        last = l == DEPTH - 1
        mod_x = (silu_c @ w_ada[l] + b_ada[l])[:, None, :]
        mod_c = silu_cc @ w_ada[l] + b_ada[l]
        sh1x, sc1x, gt1x, sh2x, sc2x, gt2x = jnp.split(mod_x, 6, axis=-1)
        sh1c, sc1c, gt1c, sh2c, sc2c, gt2c = jnp.split(mod_c, 6, axis=-1)
        hx = rmsnorm(x, norm1_g[l]) * (1.0 + sc1x) + sh1x
        hc = rmsnorm(xc, norm1_g[l]) * (1.0 + sc1c) + sh1c
        args = (w_in[l], gla_w_lr[l], gla_b_lr[l], gdn_conv_w[l], gdn_a_log[l], gdn_dt_bias[l])
        p_c = prepare_mixers(hc, *args, None)
        p_x = prepare_mixers(hx, *args, rows)
        oc_gla, oc_gdn, ctx_states = run_mixers(p_c, None)
        ox_gla, ox_gdn, _ = run_mixers(p_x, ctx_states)
        x = x + gt1x * merge_heads(ox_gla, ox_gdn, p_x, gla_norm_g[l], gdn_norm_g[l], w_out[l], x.dtype)
        hx2 = rmsnorm(x, norm2_g[l]) * (1.0 + sc2x) + sh2x
        x = x + gt2x * sq_relu_mlp(hx2, w_ff1[l], w_ff2[l])
        if not last:
            xc = xc + gt1c * merge_heads(oc_gla, oc_gdn, p_c, gla_norm_g[l], gdn_norm_g[l], w_out[l], xc.dtype)
            hc2 = rmsnorm(xc, norm2_g[l]) * (1.0 + sc2c) + sh2c
            xc = xc + gt2c * sq_relu_mlp(hc2, w_ff1[l], w_ff2[l])
    return rmsnorm(x, final_norm_g)


_drawn_inputs = setup_inputs


def setup_inputs(seed=0):
    import zlib

    import numpy as np

    out = dict(_drawn_inputs(seed))
    spreads = {}
    factors = {'ctx': 3.652,
     'c_ctx': 5.712,
     'b_ada': 3.335,
     'norm1_g': 7.681,
     'norm2_g': 19.709,
     'gla_b_lr': 8.0,
     'gla_norm_g': 29.598,
     'gdn_norm_g': 29.979,
     'final_norm_g': 8.16}
    for name, (base, spread) in spreads.items():
        noise = np.random.default_rng([zlib.crc32(name.encode()), seed]).standard_normal(out[name].shape)
        drawn = base * np.exp(spread * noise) if base else spread * noise
        out[name] = __import__('jax').numpy.asarray(drawn.astype(out[name].dtype))
    for name, factor in factors.items():
        out[name] = (out[name] * factor).astype(out[name].dtype)
    return out
```

```python
from contextlib import ExitStack

import numpy as np

import concourse.bass as bass
from concourse import mybir

F32 = mybir.dt.float32
F32R = mybir.dt.float32r
ALU = mybir.AluOpType
ACT = mybir.ActivationFunctionType
AX = mybir.AxisListType

P = 128
D = 1024
KT = D // P
NLAT, NCTX = 1024, 256
NTOK = NLAT + NCTX
TL, TC = NLAT // P, NCTX // P
NT = TL + TC
C = 64
NH = 4
GRID_W = 64
EPS = 1e-6
QK_A, V_A = 256, 512
OFF_QA, OFF_KA, OFF_VA, OFF_GA, OFF_R, OFF_QKV, OFF_GB, OFF_AB = 0, 256, 512, 1024, 1536, 1552, 3088, 3600
RANK = 16
LEVELS = 6
NADA = 6 * D
FF = 4 * D
SCRATCH = "Internal"
GLA_SCALE = (QK_A // NH) ** -0.5
GLA_DECAY = 1.0 / 16.0
GDN_SCALE = P ** -0.5
DEBUG = ()


def pos_of(tile):
    return (tile + TC) % NT


class Alloc:

    def __init__(self, nc, ctx, tag=""):
        self.nc, self.ctx, self.tag, self.sems = nc, ctx, tag, []

    def sb(self, name, shape, dt=F32):
        return self.ctx.enter_context(self.nc.sbuf_tensor(name, shape, dt))

    def ps(self, name, shape, dt=F32):
        return self.ctx.enter_context(self.nc.psum_tensor(name, shape, dt))

    def sem(self, name):
        if not self.sems:
            self.ctx.callback(self.clear_sems)
        self.sems.append(self.nc.alloc_semaphore(name=self.tag + name))
        return self.sems[-1]

    def clear_sems(self):
        self.nc.clear_and_free_semaphores(self.sems)
        self.nc.all_engine_barrier()


def mm3(pe, out, lhi, llo, rhi, rlo, start, stop):
    pe.matmul(out, lhi, rhi, start=start, stop=False)
    pe.matmul(out, lhi, rlo, start=False, stop=False)
    return pe.matmul(out, llo, rhi, start=False, stop=stop)


def modulate_phase(nc, A, K, S):
    with ExitStack() as ctx:
        m = Alloc(nc, ctx, "mod_")
        NCH = NADA // 512
        RING = 2
        xs = m.sb("xs", [P, NT, D])
        junk = m.sb("square", [P, D])
        wa = m.sb("wa", [P, RING, KT, 512])
        rows = m.sb("rows", [P, P])
        craw = m.sb("craw", [P, 2, KT])
        csil = m.sb("csil", [P, KT, 2])
        modrow = m.sb("modrow", [2, NADA])
        ss = m.sb("ss", [P, NT])
        var = m.sb("var", [P, NT])
        lnv = m.sb("lnv", [P, NT])
        rstd = m.sb("rstd", [P, NT])
        sc1 = m.sb("sc1", [P, KT, 2])
        hf = m.sb("hf", [P, 3, 512])
        ps_row = m.ps("ps_row", [2, 2, 512])
        ps_mod = m.ps("ps_mod", [P, 512])
        ps_cols = m.ps("ps_cols", [P, 512])
        ps_t = m.ps("ps_t", [P, 4, 512])
        ld_const, ld_rows, ld_c = m.sem("ld_const"), m.sem("ld_rows"), m.sem("ld_c")
        ld_x = [m.sem(f"ld_x{t}") for t in range(NT)]
        ld_w = [m.sem(f"ld_w{r}") for r in range(RING)]
        cols_ready, cols_done = m.sem("cols_ready"), m.sem("cols_done")
        c_silu, row_ready, row_done = m.sem("c_silu"), m.sem("row_ready"), m.sem("row_done")
        mod_ready, mod_done, sc1_done = m.sem("mod_ready"), m.sem("mod_done"), m.sem("sc1_done")
        ss_done, var_done, ln_done, rstd_done = m.sem("ss_done"), m.sem("var_done"), m.sem("ln_done"), m.sem("rstd_done")
        xn_done, t_ready = m.sem("xn_done"), m.sem("t_ready")
        hi_done, hf_done, lo_done = m.sem("hi_done"), m.sem("hf_done"), m.sem("lo_done")
        segs = [(0, 4), (4, 4), (8, 2)]
        units = [(k, s) for s in range(3) for k in range(KT)]
        block = ctx.enter_context(nc.Block())

        @block.sync
        def _(sp):
            sp.dma_start(craw[:, 0, :], A["c"].rearrange("a (p k) -> p (a k)", k=KT)).then_inc(ld_c, 16)
            sp.dma_start(craw[:, 1, :], A["c_ctx"].rearrange("(p k) -> p k", k=KT)).then_inc(ld_c, 16)
            for dst, name in ((K.ident, "k_ident"), (K.tri, "k_tri"), (K.trix, "k_trix"), (K.negmask, "k_negmask"),
                              (K.levmask, "k_levmask"), (K.smask, "k_smask"), (K.ident64, "k_ident64")):
                sp.dma_start(dst[:], A[name]).then_inc(ld_const, 16)
            r = 0
            for name, n in (("b_ada", 48), ("norm1_g", 8), ("norm2_g", 8), ("gdn_conv_w", 36)):
                sp.dma_start(rows[r:r + n, :], A[name].rearrange("a n -> (a n)").rearrange("(r p) -> r p", p=P)
                             if len(A[name].shape) == 2 else
                             A[name].rearrange("a w n -> (a w n)").rearrange("(r p) -> r p", p=P)).then_inc(ld_rows, 16)
                r += n
            wv = A["w_ada"].rearrange("(p k) n -> p k n", k=KT)
            xt = [A["x"][t * P:(t + 1) * P, :] for t in range(TL)] + [A["ctx"][t * P:(t + 1) * P, :] for t in range(TC)]
            for n in range(NCH):
                if n >= RING:
                    sp.wait_ge(row_ready, n - RING + 1)
                sp.dma_start(wa[:, n % RING], wv[:, :, n * 512:(n + 1) * 512]).then_inc(ld_w[n % RING], 16)
                for t in range(4 * n, min(4 * n + 4, NT)):
                    sp.dma_start(xs[:, t], xt[t]).then_inc(ld_x[t], 16)

        @block.scalar
        def _(act):
            act.wait_ge(ld_c, 32)
            act.activation(csil[:].rearrange("p k v -> p v k"), craw[:], ACT.Silu).then_inc(c_silu, 1)
            for t in range(NT):
                act.wait_ge(ld_x[t], 16)
                if t:
                    act.wait_ge(ss_done, t)
                act.activation(junk[:], xs[:, t], ACT.Square, accum_out=ss[:, t:t + 1]).then_inc(ss_done, 1)
            act.wait_ge(var_done, 1)
            act.activation(lnv[:], var[:], ACT.Ln).then_inc(ln_done, 1)
            act.wait_ge(ln_done, 1)
            act.activation(rstd[:], lnv[:], ACT.Exp, scale=-0.5).then_inc(rstd_done, 1)
            for u, (k, s) in enumerate(units):
                t0, n = segs[s]
                act.wait_ge(hf_done, u + 1)
                act.activation(K.hhi[:, k, t0 * P:(t0 + n) * P], hf[:, u % 3, :n * P], ACT.Copy).then_inc(hi_done, 1)

        @block.vector
        def _(dve):
            dve.wait_ge(cols_ready, 1)
            dve.tensor_copy(K.cols[:], ps_cols[:, :100]).then_inc(cols_done, 1)
            for n in range(NCH):
                dve.wait_ge(row_ready, n + 1)
                dve.tensor_copy(modrow[:, n * 512:(n + 1) * 512], ps_row[:, n % 2]).then_inc(row_done, 1)
                if n == 2:
                    dve.wait_ge(ss_done, NT)
                    dve.tensor_scalar(var[:], ss[:], 1.0 / D, EPS, ALU.mult, ALU.add).then_inc(var_done, 1)
                    dve.wait_ge(rstd_done, 1)
                    for t in range(NT):
                        dve.tensor_scalar(xs[:, t], xs[:, t], rstd[:, t:t + 1], None, ALU.mult).then_inc(xn_done, 1)
            dve.wait_ge(mod_ready, 1)
            dve.wait_ge(cols_done, 1)
            dve.tensor_tensor(K.mod[:], ps_mod[:, :96].rearrange("p (j v) -> p j v", v=2),
                              K.cols[:, 0:48].unsqueeze(2).broadcast_to([P, 48, 2]), ALU.add).then_inc(mod_done, 1)
            dve.wait_ge(mod_done, 1)
            dve.tensor_scalar(sc1[:], K.mod[:, 8:16], 1.0, None, ALU.add).then_inc(sc1_done, 1)
            dve.wait_ge(sc1_done, 1)
            dve.tensor_tensor(sc1[:], sc1[:], K.cols[:, 48:56].unsqueeze(2).broadcast_to([P, KT, 2]),
                              ALU.mult).then_inc(sc1_done, 1)
            dve.wait_ge(sc1_done, 2)
            for u, (k, s) in enumerate(units):
                t0, n = segs[s]
                v = int(s == 2)
                dve.wait_ge(t_ready, u + 1)
                if u >= 3:
                    dve.wait_ge(lo_done, u - 2)
                dve.tensor_scalar(hf[:, u % 3, :n * P], ps_t[:, u % 4, :n * P], sc1[:, k, v:v + 1],
                                  K.mod[:, k, v:v + 1], ALU.mult, ALU.add).then_inc(hf_done, 1)

        @block.gpsimd
        def _(pool):
            pool.memset(K.ones[:], 1.0)
            for u, (k, s) in enumerate(units):
                t0, n = segs[s]
                pool.wait_ge(hi_done, u + 1)
                pool.tensor_tensor(K.hlo[:, k, t0 * P:(t0 + n) * P], hf[:, u % 3, :n * P],
                                   K.hhi[:, k, t0 * P:(t0 + n) * P].bitcast(F32), ALU.subtract).then_inc(lo_done, 1)

        @block.tensor
        def _(pe):
            pe.wait_ge(ld_const, 7 * 16)
            pe.wait_ge(ld_rows, 4 * 16)
            pe.transpose(ps_cols[:, :100], rows[:100, :], K.ident[:100, :100]).then_inc(cols_ready, 1)
            pe.wait_ge(c_silu, 1)
            for n in range(NCH):
                pe.wait_ge(ld_w[n % RING], 16 * (n // RING + 1))
                if n >= 2:
                    pe.wait_ge(row_done, n - 1)
                for k in range(KT):
                    last = pe.matmul(ps_row[:, n % 2], csil[:, k, :], wa[:, n % RING, k, :],
                                     start=(k == 0), stop=(k == KT - 1))
                last.then_inc(row_ready, 1)
            pe.wait_ge(row_done, NCH)
            for j in range(48):
                last = pe.transpose(ps_mod[:, 2 * j:2 * j + 2], modrow[:, j * P:(j + 1) * P], K.ident[0:2, 0:2])
            last.then_inc(mod_ready, 1)
            for u, (k, s) in enumerate(units):
                t0, n = segs[s]
                pe.wait_ge(xn_done, t0 + n)
                if u >= 4:
                    pe.wait_ge(hf_done, u - 3)
                for i in range(n):
                    last = pe.transpose(ps_t[:, u % 4, i * P:(i + 1) * P], xs[:, t0 + i, k * P:(k + 1) * P], K.ident[:])
                last.then_inc(t_ready, 1)


def project_phase(nc, A, K, S):
    with ExitStack() as ctx:
        m = Alloc(nc, ctx, "proj_")
        W = 256
        UNITS = [("small", 0, 32, 0),
                 ("k", OFF_QKV + 512, W, 0), ("k", OFF_QKV + 768, W, 2),
                 ("v", OFF_QKV + 1024, W, 0), ("v", OFF_QKV + 1280, W, 2),
                 ("q", OFF_QKV, W, 0), ("q", OFF_QKV + 256, W, 2),
                 ("ka", OFF_KA, W, 0), ("qa", OFF_QA, W, 0),
                 ("va", OFF_VA, W, 0), ("va", OFF_VA + W, W, 2),
                 ("gate", OFF_GA, W, 0), ("gate", OFF_GA + W, W, 1),
                 ("gate", OFF_GB, W, 2), ("gate", OFF_GB + W, W, 3)]
        NU = len(UNITS)
        raw = m.sb("raw", [P, 2, KT, W])
        whi = m.sb("whi", [P, 2, KT, W], F32R)
        wlo = m.sb("wlo", [P, 2, KT, W], F32R)
        u_sb = m.sb("u_sb", [P, NTOK])
        y_sb = m.sb("y_sb", [P, NTOK])
        z_sb = m.sb("z_sb", [P, 2, NTOK])
        sq_sb = m.sb("sq_sb", [P, NTOK])
        n_sb = m.sb("n_sb", [P, 2, NTOK])
        tok_sb = m.sb("tok_sb", [P, NT, P])
        a_sb = m.sb("a_sb", [P, NTOK])
        t_sb = m.sb("t_sb", [P, 4, W])
        small = m.sb("small", [P, NT, 32])
        eps = m.sb("eps", [P, 1])
        wlr = m.sb("wlr", [RANK + 1, 512])
        raT = m.sb("raT", [32, NTOK])
        lr_e = m.sb("lr_e", [P, 512])
        lr_x = m.sb("lr_x", [P, 2, 512])
        alog = m.sb("alog", [P, 8])
        dtb = m.sb("dtb", [P, 8])
        nea = m.sb("nea", [P, 8])
        za = m.sb("za", [P, NT, 8])
        zb = m.sb("zb", [P, NT, 8])
        zc = m.sb("zc", [P, NT, 8])
        ps_main = m.ps("ps_main", [P, 3, 512])
        ps_sq = m.ps("ps_sq", [P, 3, 512])
        ps_tr = m.ps("ps_tr", [P, 2, 512])
        ld_w = [m.sem("ld_w0"), m.sem("ld_w1")]
        ld_s = m.sem("ld_s")
        hi_done, lo_done = m.sem("p_hi_done"), m.sem("p_lo_done")
        main_ready, main_out = m.sem("main_ready"), m.sem("main_out")
        conv_done, z_done, sq_done = m.sem("conv_done"), m.sem("z_done"), m.sem("sq_done")
        ss_ready, lnss_done, rs_done, n_done = m.sem("ss_ready"), m.sem("lnss_done"), m.sem("rs_done"), m.sem("n_done")
        tr_ready, tr_out = m.sem("tr_ready"), m.sem("tr_out")
        st_n = [m.sem("st_n0"), m.sem("st_n1")]
        st_tok, st_a = m.sem("st_tok"), m.sem("st_a")
        st_t = [m.sem(f"st_t{i}") for i in range(4)]
        conv_step = m.sem("conv_step")
        init_done, rt_ready, rt_out = m.sem("init_done"), m.sem("rt_ready"), m.sem("rt_out")
        lr_abs, lr_exp, lr_ln, lr_done = m.sem("lr_abs"), m.sem("lr_exp"), m.sem("lr_ln"), m.sem("lr_done")
        st_lr = [m.sem("st_lr0"), m.sem("st_lr1")]
        ab_act, ab_dve = m.sem("ab_act"), m.sem("ab_dve")
        SEG = [(0, 512), (512, 512), (1024, 256)]

        outs = []
        for u, (kind, _, width, h0) in enumerate(UNITS):
            if kind in ("k", "v", "q", "ka", "qa"):
                for j in range(2):
                    for s in range(2 if kind in ("q", "qa") else 3):
                        outs.append((u, kind, j, s))
                        n_lr = sum(o[1] == "lr" for o in outs)
                        if n_lr < NT:
                            outs.append((u, "lr", n_lr, 0))
            else:
                for t in range(TL if kind == "gate" else NT):
                    outs.append((u, kind, t, 0))
        out_by = {}
        for i, (u, kind, j, _) in enumerate(outs):
            out_by[(u, kind, j)] = i + 1
            out_by[u] = i + 1
        conv_tiles = [(u, j) for u, un in enumerate(UNITS) if un[0] in ("k", "v", "q") for j in range(2)]
        conv_no = {x: i for i, x in enumerate(conv_tiles)}
        kinds = [UNITS[u][0] for u, _ in conv_tiles]

        def n_norm(i):
            return sum(k != "v" for k in kinds[:i])

        def n_turn(i):
            return sum(k != "q" for k in kinds[:i])

        NTR = 3

        block = ctx.enter_context(nc.Block())

        def turned_store(i):
            u, j = conv_tiles[i]
            return (S["kt"] if kinds[i] == "k" else S["vt"]), UNITS[u][3] + j

        @block.sync
        def _(sp):
            wv = A["w_in"].rearrange("(k p) n -> p k n", p=P)
            sp.dma_start(wlr[0:RANK, :], A["gla_w_lr"].rearrange("z r n -> r z n")).then_inc(ld_s, 16)
            sp.dma_start(wlr[RANK:RANK + 1, :], A["gla_b_lr"].rearrange("(a z) n -> a (z n)", a=1)).then_inc(ld_s, 16)
            sp.dma_start(alog[:], A["gdn_a_log"].rearrange("z h -> (z h)").partition_broadcast(P)).then_inc(ld_s, 16)
            sp.dma_start(dtb[:], A["gdn_dt_bias"].rearrange("z h -> (z h)").partition_broadcast(P)).then_inc(ld_s, 16)

            def load_unit(u):
                kind, col, width, _ = UNITS[u]
                if u >= 2:
                    sp.wait_ge(lo_done, u - 1)
                if kind == "small":
                    sp.dma_start(raw[:, u % 2, :, 0:16], wv[:, :, OFF_R:OFF_R + 16]).then_inc(ld_w[u % 2], 16)
                    sp.dma_start(raw[:, u % 2, :, 16:32], wv[:, :, OFF_AB:OFF_AB + 16]).then_inc(ld_w[u % 2], 16)
                else:
                    sp.dma_start(raw[:, u % 2], wv[:, :, col:col + width]).then_inc(ld_w[u % 2], 16)

            for u in range(NU):
                load_unit(u)

        @block.gpsimd
        def _(pool):
            pool.memset(eps[:], EPS).then_inc(init_done, 1)
            pool.memset(raT[:], 1.0).then_inc(init_done, 1)
            def store_conv(i):
                u, j = conv_tiles[i]
                head = UNITS[u][3] + j
                if kinds[i] != "v":
                    n = n_norm(i)
                    pool.wait_ge(n_done, n + 1)
                    dst = S["k"] if kinds[i] == "k" else S["q"]
                    pool.dma_start(dst[TC:NT, :, head, :].rearrange("t p n -> p t n"),
                                   n_sb[:, n % 2, :NLAT].rearrange("p (t n) -> p t n", n=P)).then_inc(st_n[n % 2], 16)
                    if kinds[i] == "k":
                        pool.dma_start(dst[0:TC, :, head, :].rearrange("t p n -> p t n"),
                                       n_sb[:, n % 2, NLAT:].rearrange("p (t n) -> p t n", n=P)).then_inc(st_n[n % 2], 16)
                if kinds[i] != "q":
                    dst, head = turned_store(i)
                    n = n_turn(i)
                    pool.wait_ge(tr_out, NTR * (n + 1))
                    pool.dma_start(dst[TC:NT, :, head, :].rearrange("t p n -> p t n"),
                                   tok_sb[:, 0:TL, :]).then_inc(st_tok, 16)
                    pool.dma_start(dst[0:TC, :, head, :].rearrange("t p n -> p t n"),
                                   tok_sb[:, TL:NT, :]).then_inc(st_tok, 16)

            for t in range(NT):
                pool.wait_ge(lr_done, t + 1)
                pool.dma_start(S["la"][pos_of(t)], lr_x[:, t % 2]).then_inc(st_lr[t % 2], 16)
                if t == 4:
                    store_conv(0)
                if t == 7:
                    store_conv(1)
            for i in range(2, len(conv_tiles)):
                store_conv(i)
            for u, (kind, _, _, h0) in enumerate(UNITS):
                if kind in ("ka", "qa"):
                    for j in range(2):
                        pool.wait_ge(main_out, out_by[(u, kind, j)])
                        dst = S["ga_k"] if kind == "ka" else S["ga_q"]
                        pool.dma_start(dst[TC:NT, :, j, :].rearrange("t p n -> p t n"),
                                       a_sb[:, :NLAT].rearrange("p (t n) -> p t n", n=P)).then_inc(st_a, 16)
                        if kind == "ka":
                            pool.dma_start(dst[0:TC, :, j, :].rearrange("t p n -> p t n"),
                                           a_sb[:, NLAT:].rearrange("p (t n) -> p t n", n=P)).then_inc(st_a, 16)
            nt = 0
            for u, (kind, _, _, h0) in enumerate(UNITS):
                if kind in ("va", "gate"):
                    for t in range(TL if kind == "gate" else NT):
                        pool.wait_ge(main_out, out_by[(u, kind, t)])
                        dst = (S["va"][pos_of(t), :, h0 * P:h0 * P + W] if kind == "va"
                               else S["gate"][t, :, h0 * W:(h0 + 1) * W])
                        pool.dma_start(dst, t_sb[:, nt % 4]).then_inc(st_t[nt % 4], 16)
                        nt += 1
            for s, n in ((st_n[0], 4 * 16 + 2 * 16), (st_n[1], 4 * 16 + 2 * 16), (st_tok, 16 * 16), (st_lr[0], 80),
                         (st_lr[1], 80), (st_a, 96)):
                pool.wait_ge(s, n)
            for i in range(4):
                pool.wait_ge(st_t[i], 16 * ((nt + 3 - i) // 4))

        def stored_n(n):
            nk = 4
            return 16 * sum(2 if i < nk else 1 for i in range(n % 2, n - 1, 2))

        @block.scalar
        def _(act):
            def split(u):
                act.wait_ge(ld_w[u % 2], 16 * (u // 2 + 1) + (16 if u % 2 == 0 else 0))
                if u >= 2:
                    act.wait_ge(main_ready, out_by[u - 2])
                w = UNITS[u][2]
                act.activation(whi[:, u % 2, :, :w], raw[:, u % 2, :, :w], ACT.Copy).then_inc(hi_done, 1)

            def finish_conv(i):
                kind = kinds[i]
                act.wait_ge(conv_done, i + 1)
                if i >= 2:
                    act.wait_ge(n_done, n_norm(i - 1))
                    if n_turn(i - 1):
                        act.wait_ge(tr_ready, NTR * n_turn(i - 1))
                n = NLAT if kind == "q" else NTOK
                act.activation(z_sb[:, i % 2, :n], y_sb[:, :n], ACT.Silu).then_inc(z_done, 1)
                if kind != "v":
                    act.wait_ge(z_done, i + 1)
                    if n_norm(i):
                        act.wait_ge(ss_ready, n_norm(i))
                        act.wait_ge(n_done, n_norm(i))
                    act.activation(sq_sb[:, :n], z_sb[:, i % 2, :n], ACT.Square).then_inc(sq_done, 1)

            def finish_norm(i):
                kind = kinds[i]
                if kind == "v":
                    return
                k = n_norm(i)
                n = NLAT if kind == "q" else NTOK
                act.wait_ge(ss_ready, k + 1)
                act.activation(sq_sb[:, :n], ps_sq[:, :, :].rearrange("p s n -> p (s n)")[:, :n], ACT.Ln,
                               bias=eps[:]).then_inc(lnss_done, 1)
                act.wait_ge(lnss_done, k + 1)
                act.activation(sq_sb[:, :n], sq_sb[:, :n], ACT.Exp, scale=-0.5).then_inc(rs_done, 1)

            act.wait_ge(init_done, 2)
            split(0)
            split(1)
            na = nt = 0
            for i, (u, kind, j, s) in enumerate(outs):
                act.wait_ge(main_ready, i + 1)
                if kind == "small":
                    act.activation(small[:, j, :], ps_main[:, i % 3, :32], ACT.Copy).then_inc(main_out, 1)
                    if j == NT - 1:
                        act.wait_ge(ab_dve, 1)
                        act.activation(zb[:], za[:], ACT.Abs).then_inc(ab_act, 1)
                        act.activation(nea[:], alog[:], ACT.Exp).then_inc(ab_act, 1)
                        act.wait_ge(ab_act, 2)
                        act.activation(zb[:], zb[:], ACT.Exp, scale=-1.0).then_inc(ab_act, 1)
                        act.wait_ge(ab_act, 3)
                        act.activation(zb[:], zb[:], ACT.Ln, bias=1.0).then_inc(ab_act, 1)
                        act.activation(zc[:], small[:, :, 24:32], ACT.Exp, scale=-1.0).then_inc(ab_act, 1)
                elif kind == "lr":
                    if j >= 2:
                        act.wait_ge(st_lr[j % 2], 16 * (j // 2))
                    act.activation(lr_x[:, j % 2], ps_main[:, i % 3, :], ACT.Copy).then_inc(main_out, 1)
                    act.wait_ge(main_out, i + 1)
                    if j:
                        act.wait_ge(lr_done, j)
                    act.activation(lr_e[:], lr_x[:, j % 2], ACT.Abs).then_inc(lr_abs, 1)
                    act.wait_ge(lr_abs, j + 1)
                    act.activation(lr_e[:], lr_e[:], ACT.Exp, scale=-1.0).then_inc(lr_exp, 1)
                    act.wait_ge(lr_exp, j + 1)
                    act.activation(lr_e[:], lr_e[:], ACT.Ln, bias=1.0).then_inc(lr_ln, 1)
                elif kind in ("k", "v", "q"):
                    cn = conv_no[(u, j)]
                    t0, n = SEG[s]
                    if s == 0 and cn >= 1:
                        act.wait_ge(conv_done, cn)
                    act.activation(u_sb[:, t0:t0 + n], ps_main[:, i % 3, :n], ACT.Copy).then_inc(main_out, 1)
                    if s == 0 and cn >= 1:
                        finish_norm(cn - 1)
                    if s == (1 if kind == "q" else 2):
                        finish_conv(cn)
                elif kind in ("ka", "qa"):
                    t0, n = SEG[s]
                    if s == 0 and na >= 1:
                        act.wait_ge(st_a, (0, 32, 64, 80)[na])
                    act.activation(a_sb[:, t0:t0 + n], ps_main[:, i % 3, :n], ACT.Copy,
                                   scale=(GLA_SCALE if kind == "qa" else 1.0)).then_inc(main_out, 1)
                    if na == 0 and s == 0:
                        finish_norm(len(conv_tiles) - 1)
                    if s == (1 if kind == "qa" else 2):
                        na += 1
                else:
                    if nt >= 4:
                        act.wait_ge(st_t[nt % 4], 16 * (nt // 4))
                    act.activation(t_sb[:, nt % 4], ps_main[:, i % 3, :W],
                                   ACT.Silu if kind == "gate" else ACT.Copy).then_inc(main_out, 1)
                    nt += 1
                if u >= 1 and i + 1 == out_by[u - 1] + 1 and u + 1 < NU:
                    split(u + 1)

        @block.vector
        def _(dve):
            step = [0]

            def then_step(ins):
                step[0] += 1
                ins.then_inc(conv_step, 1)
                dve.wait_ge(conv_step, step[0])

            def split(u):
                dve.wait_ge(hi_done, u + 1)
                w = UNITS[u][2]
                dve.tensor_tensor(wlo[:, u % 2, :, :w], raw[:, u % 2, :, :w], whi[:, u % 2, :, :w].bitcast(F32),
                                  ALU.subtract).then_inc(lo_done, 1)

            def conv(cn):
                u, j = conv_tiles[cn]
                kind = kinds[cn]
                dve.wait_ge(main_out, out_by[(u, kind, j)])
                if cn >= 1:
                    dve.wait_ge(z_done, cn)
                ch = {"q": 0, "k": 4, "v": 8}[kind] + UNITS[u][3] + j
                w = [K.cols[:, 64 + tap * 12 + ch:65 + tap * 12 + ch] for tap in range(3)]
                n = NLAT if kind == "q" else NTOK
                then_step(dve.tensor_scalar(y_sb[:, :n], u_sb[:, :n], w[1], None, ALU.mult))
                for lo, hi, row in ((0, NLAT, GRID_W), (NLAT, NTOK, NCTX)):
                    if lo >= n:
                        continue
                    uu = u_sb[:, lo:hi].rearrange("p (r w) -> p r w", w=row)
                    yy = y_sb[:, lo:hi].rearrange("p (r w) -> p r w", w=row)
                    then_step(dve.scalar_tensor_tensor(yy[:, :, 1:], uu[:, :, :row - 1], w[0], yy[:, :, 1:],
                                                       ALU.mult, ALU.add))
                    last = dve.scalar_tensor_tensor(yy[:, :, :row - 1], uu[:, :, 1:], w[2], yy[:, :, :row - 1],
                                                    ALU.mult, ALU.add)
                    if hi < n:
                        then_step(last)
                last.then_inc(conv_done, 1)

            def norm(cn):
                kind = kinds[cn]
                if kind == "v":
                    return
                k = n_norm(cn)
                n = NLAT if kind == "q" else NTOK
                dve.wait_ge(rs_done, k + 1)
                if k >= 2:
                    dve.wait_ge(st_n[k % 2], stored_n(k))
                if 2 <= k < 6:
                    dve.wait_ge(tr_ready, NTR * (k - 1))
                dve.scalar_tensor_tensor(n_sb[:, k % 2, :n], z_sb[:, cn % 2, :n], GDN_SCALE if kind == "q" else 1.0,
                                         sq_sb[:, :n], ALU.mult, ALU.mult).then_inc(n_done, 1)

            def turn_out(cn):
                if kinds[cn] == "q":
                    return
                k = n_turn(cn)
                if k:
                    dve.wait_ge(st_tok, 32 * k)
                for r, (t0, n) in enumerate(((0, 4), (4, 4), (8, 2))):
                    f = NTR * k + r
                    dve.wait_ge(tr_ready, f + 1)
                    dve.tensor_copy(tok_sb[:, t0:t0 + n, :].rearrange("p t n -> p (t n)"),
                                    ps_tr[:, f % 2, :n * P]).then_inc(tr_out, 1)

            dve.wait_ge(init_done, 2)
            split(0)
            split(1)
            for r, (t0, n) in enumerate(SEG):
                dve.wait_ge(rt_ready, r + 1)
                dve.tensor_copy(raT[0:RANK, t0:t0 + n], ps_sq[0:RANK, r, :n]).then_inc(rt_out, 1)
            dve.wait_ge(ld_s, 64)
            dve.wait_ge(main_out, NT)
            dve.tensor_tensor(za[:], small[:, :, 16:24], dtb[:].unsqueeze(1).broadcast_to([P, NT, 8]),
                              ALU.add).then_inc(ab_dve, 1)
            dve.wait_ge(ab_act, 4)
            dve.wait_ge(ab_dve, 1)
            then_step(dve.scalar_tensor_tensor(za[:], za[:], 0.0, zb[:], ALU.max, ALU.add))
            then_step(dve.scalar_tensor_tensor(za[:], za[:], -1.0, nea[:].unsqueeze(1).broadcast_to([P, NT, 8]),
                                               ALU.mult, ALU.mult))
            for t in range(NT):
                dve.tensor_copy(K.gdn_la[:, :, pos_of(t), :], za[:, t, :].rearrange("p (z h) -> p z h", z=2))
            dve.wait_ge(ab_act, 5)
            then_step(dve.tensor_scalar(zc[:], zc[:], 1.0, None, ALU.add))
            then_step(dve.reciprocal(zc[:], zc[:]))
            for t in range(NT):
                dve.tensor_copy(K.beta[:, :, pos_of(t), :], zc[:, t, :].rearrange("p (z h) -> p z h", z=2))
            for i, (u, kind, j, s) in enumerate(outs):
                if kind == "lr":
                    dve.wait_ge(lr_ln, j + 1)
                    dve.scalar_tensor_tensor(lr_x[:, j % 2], lr_x[:, j % 2], 0.0, lr_e[:],
                                             ALU.min, ALU.subtract).then_inc(lr_done, 1)
                if (u, j) in conv_no and kind != "lr" and i + 1 == out_by[(u, kind, j)]:
                    cn = conv_no[(u, j)]
                    if cn >= 1:
                        norm(cn - 1)
                    conv(cn)
                    if cn >= 1:
                        turn_out(cn - 1)
                if kind == "ka" and j == 0 and s == 0:
                    norm(len(conv_tiles) - 1)
                if u >= 1 and i + 1 == out_by[u - 1] + 1 and u + 1 < NU:
                    split(u + 1)

        @block.tensor
        def _(pe):
            pe.wait_ge(init_done, 2)

            def ranks():
                for r, (t0, n) in enumerate(SEG):
                    pe.wait_ge(main_out, (t0 + n) // P)
                    for i in range(n // P):
                        last = pe.transpose(ps_sq[0:RANK, r, i * P:(i + 1) * P], small[:, t0 // P + i, 0:RANK], K.ident[:])
                    last.then_inc(rt_ready, 1)

            def sums(cn):
                if kinds[cn] == "v":
                    return
                k = n_norm(cn)
                pe.wait_ge(sq_done, k + 1)
                if k:
                    pe.wait_ge(lnss_done, k)
                else:
                    pe.wait_ge(rt_out, 3)
                for s in range(2 if kinds[cn] == "q" else 3):
                    t0, n = SEG[s]
                    last = pe.matmul(ps_sq[:, s, :n], K.ones[:], sq_sb[:, t0:t0 + n], start=True, stop=True)
                last.then_inc(ss_ready, 1)

            def turn(cn):
                if kinds[cn] == "q":
                    return
                k = n_turn(cn)
                if kinds[cn] == "k":
                    pe.wait_ge(n_done, n_norm(cn) + 1)
                    src = n_sb[:, n_norm(cn) % 2]
                else:
                    pe.wait_ge(z_done, cn + 1)
                    src = z_sb[:, cn % 2]
                for r, (t0, n) in enumerate(((0, 4), (4, 4), (8, 2))):
                    f = NTR * k + r
                    if f >= 2:
                        pe.wait_ge(tr_out, f - 1)
                    for i in range(n):
                        last = pe.transpose(ps_tr[:, f % 2, i * P:(i + 1) * P], src[:, (t0 + i) * P:(t0 + i + 1) * P],
                                            K.ident[:])
                    last.then_inc(tr_ready, 1)

            for i, (u, kind, j, s) in enumerate(outs):
                b, width = u % 2, UNITS[u][2]
                pe.wait_ge(lo_done, u + 1)
                if i >= 3:
                    pe.wait_ge(main_out, i - 2)
                if kind == "lr":
                    if j == 0:
                        pe.wait_ge(rt_out, 3)
                        pe.wait_ge(ld_s, 64)
                    pe.matmul(ps_main[:, i % 3, :], raT[0:RANK + 1, j * P:(j + 1) * P], wlr[:], start=True,
                              stop=True).then_inc(main_ready, 1)
                elif kind in ("small", "va", "gate"):
                    ts = slice(j * P, (j + 1) * P)
                    for k in range(KT):
                        last = mm3(pe, ps_main[:, i % 3, :width], K.hhi[:, k, ts], K.hlo[:, k, ts],
                                   whi[:, b, k, :width], wlo[:, b, k, :width], k == 0, k == KT - 1)
                    last.then_inc(main_ready, 1)
                    if kind == "small" and j == NT - 1:
                        ranks()
                else:
                    t0, n = SEG[s]
                    cs = slice(j * P, (j + 1) * P)
                    for k in range(KT):
                        last = mm3(pe, ps_main[:, i % 3, :n], whi[:, b, k, cs], wlo[:, b, k, cs],
                                   K.hhi[:, k, t0:t0 + n], K.hlo[:, k, t0:t0 + n], k == 0, k == KT - 1)
                    last.then_inc(main_ready, 1)
                    cn = conv_no.get((u, j), len(conv_tiles) if (kind, j) == ("ka", 0) else 0)
                    if cn >= 1 and s == 0:
                        sums(cn - 1)
                    if cn >= 1 and s == (1 if kind == "q" else 2):
                        turn(cn - 1)


def mix_phase(nc, A, K, S):
    LAST_LEVEL = LEVELS - 1
    SM_STEPS = 5
    with ExitStack() as ctx:
        m = Alloc(nc, ctx, "mix_")
        R2 = range(2)
        both = lambda name, shape: [m.sb(f"{name}{d}", shape) for d in R2]
        kc, qc = both("kc", [P, NH, P]), both("qc", [P, NH, P])
        kt, vt = both("kt", [P, NH, P]), both("vt", [P, NH, P])
        coef = both("coef", [P, 5, NH])
        rows = both("rows", [P, 2, NH, C])
        lmat = both("lmat", [P, NH, C])
        dec = both("dec", [P, 2, NH, C])
        loff = both("loff", [P, LEVELS, NH, C])
        xx = both("xx", [P, 2, NH, C])
        yy = both("yy", [P, NH, C])
        xtp, atp = both("xtp", [P, NH, P]), both("atp", [P, NH, P])
        bv, bk, kd, qd = (both(n, [P, NH, P]) for n in ("bv", "bk", "kd", "qd"))
        wtn, delta = both("wtn", [P, NH, P]), both("delta", [P, NH, P])
        st, sta = both("st", [P, NH, P]), both("sta", [P, NH, P])
        sm = m.sb("sm", [P, 2, NT, 5, NH])
        gqk = m.sb("gqk", [P, 2, 2, P])
        gva, gla = m.sb("gva", [P, NH, P]), m.sb("gla", [P, 512])
        bs = m.sb("bs", [P, 2, 2, P])
        wl = m.sb("wl", [P, LEVELS, 2, 2, P])
        kin, qin = m.sb("kin", [P, 2, 2, P]), m.sb("qin", [P, 2, 2, P])
        msc = m.sb("msc", [P, 2, LEVELS + 1, C])
        atg = m.sb("atg", [P, NH, P])
        kint = m.sb("kint", [P, 2, 2, P])
        pa = [m.ps(f"pa{d}", [P, 512]) for d in R2]
        pb = [m.ps(f"pb{d}", [P, 512]) for d in R2]
        pc = [m.ps(f"pc{d}", [P, 512]) for d in R2]
        px = [m.ps(f"px{d}", [P, 512]) for d in R2]

        two = lambda name: [m.sem(f"{name}{d}") for d in R2]
        init_done, g_ready, sm_step = m.sem("mx_init"), m.sem("g_ready"), m.sem("sm_step")
        ld_k, ld_q, ld_t = two("ld_k"), two("ld_q"), two("ld_t")
        coef_done, tri_la_done = two("coef_done"), two("tri_la_done")
        gr_ready, kq_ready = two("gr_ready"), two("kq_ready")
        diff_done, dec_in, dec_done, eg_done = two("diff_done"), two("dec_in"), two("dec_done"), two("eg_done")
        kkd_done, l_done, at_done = two("kkd_done"), two("l_done"), two("at_done")
        loff_done, x_done, y_ready, y_done, p_ready = (two("loff_done"), two("x_done"), two("y_ready"),
                                                       two("y_done"), two("p_ready"))
        xtp_done, scaled_done, qd_done = two("xtp_done"), two("scaled_done"), two("qd_done")
        uw_ready, wt_done, ws_ready, delta_done = two("uw_ready"), two("wt_done"), two("ws_ready"), two("delta_done")
        ds_ready, sta_done, st_done = two("ds_ready"), two("sta_done"), two("st_done")
        o_ready, o_done = two("o_ready"), two("o_done")
        ld_g, ld_gq, st_qin, qin_done = m.sem("ld_g"), m.sem("ld_gq"), m.sem("st_qin"), m.sem("qin_done")
        b_ready, b_done, sub_done, exp_done = m.sem("b_ready"), m.sem("b_done"), m.sem("sub_done"), m.sem("exp_done")
        wl_done, io_done = m.sem("wl_done"), m.sem("io_done")
        sc_ready, msc_done, atg_done = m.sem("sc_ready"), m.sem("msc_done"), m.sem("atg_done")
        kt_ready, kt_out, gs_ready, gs_out = m.sem("kt_ready"), m.sem("kt_out"), m.sem("gs_ready"), m.sem("gs_out")
        og_ready, og_out, scan = m.sem("og_ready"), m.sem("og_out"), m.sem("gla_scan")

        def after(eng, sem, n):
            if not isinstance(n, int) or n > 0:
                eng.wait_ge(sem, n)

        def pos(d, s, lat):
            if d == 0:
                return s
            return 11 - s if lat else 1 - s

        def steps(eng, body):
            body(0, False)
            body(1, False)
            for i in range(TL):
                body(i + TC, True)

        def chunk_order(d):
            return ((0, 1), (1, 0))[d]

        half = lambda c: slice(c * C, (c + 1) * C)
        block = ctx.enter_context(nc.Block())

        @block.sync
        def _(sp):
            def step(s, lat):
                for d in R2:
                    p = pos(d, s, lat)
                    after(sp, kq_ready[d], s)
                    sp.dma_start(kc[d][:], S["k"][p]).then_inc(ld_k[d], 16)
                    if lat:
                        sp.wait_ge(sta_done[d], 2 * s)
                        sp.dma_start(qc[d][:], S["q"][p]).then_inc(ld_q[d], 16)
                    if not isinstance(s, int) or s > 0:
                        sp.wait_ge(scaled_done[d], s * 3)
                    sp.dma_start(kt[d][:], S["kt"][p]).then_inc(ld_t[d], 16)
                    sp.dma_start(vt[d][:], S["vt"][p]).then_inc(ld_t[d], 16)
                    if d == 0:
                        after(sp, gs_ready, 2 * s)
                        if lat:
                            sp.wait_ge(og_out, s - TC + 1)
                        sp.dma_start(gqk[:, 1], S["ga_k"][s]).then_inc(ld_g, 16)
                        sp.dma_start(gva[:], S["va"][s].rearrange("p (h n) -> p h n", h=NH)).then_inc(ld_g, 16)
                        sp.dma_start(gla[:], S["la"][s]).then_inc(ld_g, 16)
                        if lat:
                            sp.dma_start(gqk[:, 0], S["ga_q"][s]).then_inc(ld_gq, 16)
                if lat:
                    sp.wait_ge(qin_done, s - TC + 1)
                    sp.dma_start(S["qin"][s - TC], qin[:]).then_inc(st_qin, 16)
            sp.sem_inc(st_qin, 16)
            steps(sp, step)
            sp.wait_ge(st_qin, 16 * (TL + 1))

        @block.gpsimd
        def _(pool):
            for d in R2:
                for t in (xtp[d], atp[d], st[d]):
                    pool.memset(t[:], 0.0)
            pool.memset(K.xo[:, :, V_A:], 0.0)
            pool.memset(atg[:], 0.0).then_inc(init_done, 1)

            def step(s, lat):
                for d in R2:
                    after(pool, l_done[d], s)
                    after(pool, diff_done[d], 2 * s)
                    if isinstance(s, int) and s == 0:
                        pool.wait_ge(sm_step, SM_STEPS)
                    pool.tensor_copy(coef[d][:], sm[:, d, pos(d, s, lat)]).then_inc(coef_done[d], 1)
                    pool.wait_ge(coef_done[d], s + 1)
                    after(pool, sta_done[d], 2 * s)
                    pool.tensor_tensor(rows[d][:], K.tri[:, d].rearrange("p (c j) -> p c j", c=2).unsqueeze(2)
                                       .broadcast_to([P, 2, NH, C]),
                                       coef[d][:, 0].unsqueeze(1).unsqueeze(3).broadcast_to([P, 2, NH, C]),
                                       ALU.mult).then_inc(tri_la_done[d], 1)
                for d in R2:
                    pool.wait_ge(l_done[d], s + 1)
                    pool.tensor_tensor(loff[d][:, 0], lmat[d][:],
                                       K.levmask[:, d, 0].unsqueeze(1).broadcast_to([P, NH, C]),
                                       ALU.mult).then_inc(loff_done[d], 1)
                    pool.tensor_tensor(loff[d][:, 1:].rearrange("p l h j -> p l h j"),
                                       lmat[d][:].unsqueeze(1).broadcast_to([P, LEVELS - 1, NH, C]),
                                       K.levmask[:, d, 1:].unsqueeze(2).broadcast_to([P, LEVELS - 1, NH, C]),
                                       ALU.mult).then_inc(loff_done[d], 1)
                if lat:
                    pool.wait_ge(exp_done, 3 * s - 3)
                    pool.wait_ge(ld_gq, 16 * (s - TC + 1))
                    pool.tensor_tensor(qin[:].rearrange("p z a n -> p z (a n)"), qin[:].rearrange("p z a n -> p z (a n)"),
                                       gqk[:, 0].rearrange("p a n -> p (a n)").unsqueeze(1).broadcast_to([P, 2, 256]),
                                       ALU.mult).then_inc(qin_done, 1)
                for d in R2:
                    pool.wait_ge(ld_t[d], 32 * (s + 1))
                    after(pool, ds_ready[d], 2 * s)
                    for out_, in_, kind in ((bv, vt, 2), (bk, kt, 3), (kd, kt, 4)):
                        pool.tensor_tensor(out_[d][:], in_[d][:],
                                           coef[d][:, kind].unsqueeze(2).broadcast_to([P, NH, P]),
                                           ALU.mult).then_inc(scaled_done[d], 1)
                for d in R2:
                    pool.wait_ge(eg_done[d], s + 1)
                    if lat:
                        pool.wait_ge(ld_q[d], 16 * (s - TC + 1))
                        pool.tensor_tensor(qd[d][:].rearrange("p h (c j) -> p c h j", c=2),
                                           qc[d][:].rearrange("p h (c j) -> p c h j", c=2), rows[d][:],
                                           ALU.mult).then_inc(qd_done[d], 1)
                for n in R2:
                    for d in R2:
                        c = chunk_order(d)[n]
                        last = (C - 1, 0)[d]
                        after(pool, st_done[d], 2 * s + n)
                        pool.tensor_tensor(sta[d][:], st[d][:], rows[d][:, c, :, last:last + 1]
                                           .broadcast_to([P, NH, P]), ALU.mult).then_inc(sta_done[d], 1)
            steps(pool, step)

        @block.scalar
        def _(act):
            act.wait_ge(g_ready, 1)
            act.activation(sm[:, :, :, 1, :], px[0][:, 0:80].rearrange("p (d t h) -> p d t h", d=2, t=NT),
                           ACT.Copy).then_inc(sm_step, 1)
            act.activation(sm[:, :, :, 3, :], px[0][:, 0:80].rearrange("p (d t h) -> p d t h", d=2, t=NT),
                           ACT.Exp).then_inc(sm_step, 1)
            act.activation(sm[:, :, :, 4, :], px[0][:, 80:160].rearrange("p (d t h) -> p d t h", d=2, t=NT),
                           ACT.Exp).then_inc(og_out, 1)

            def step(s, lat):
                act.wait_ge(b_ready, s + 1)
                after(act, sub_done, s)
                act.activation(bs[:].rearrange("p z a n -> p (z a n)"), px[0][:], ACT.Copy,
                               scale=GLA_DECAY).then_inc(b_done, 1)
                act.wait_ge(b_done, s + 1)
                for z in R2:
                    end = (C - 1, 0)[z]
                    act.activation(K.ga_a[:, bass.ds(2 * s, 2), z, :].rearrange("p c a -> p a c"),
                                   bs[:, z].rearrange("p a (c j) -> p a c j", c=2)[:, :, :, end], ACT.Exp)
                if lat:
                    act.wait_ge(st_qin, 16 * (s - TC + 1))
                    act.activation(qin[:], bs[:], ACT.Exp).then_inc(exp_done, 1)
                for d in R2:
                    act.wait_ge(dec_in[d], 2 * (s + 1))
                    act.activation(dec[d][:], dec[d][:], ACT.Exp).then_inc(dec_done[d], 1)
                    act.activation(rows[d][:].rearrange("p c h j -> p (c h j)"), pa[d][:], ACT.Exp).then_inc(eg_done[d], 1)
                act.wait_ge(sub_done, s + 1)
                act.activation(kin[:], kin[:], ACT.Exp).then_inc(exp_done, 1)
                if lat:
                    act.activation(wl[:], wl[:], ACT.Exp).then_inc(exp_done, 1)
                for lev in range(1, LEVELS):
                    for d in R2:
                        act.wait_ge(y_ready[d], s * (LEVELS - 1) + lev)
                        act.activation(yy[d][:].rearrange("p h j -> p (h j)"), pa[d][:, :NH * C], ACT.Copy).then_inc(y_done[d], 1)
                    if lev == 2:
                        act.wait_ge(kt_ready, s + 1)
                        act.activation(kint[:].rearrange("p z a n -> p (z a n)"), px[0][:], ACT.Copy).then_inc(kt_out, 1)
                    if lev == LAST_LEVEL:
                        for c in R2:
                            act.wait_ge(gs_ready, 2 * s + c + 1)
                            act.activation(K.ga_st[:, bass.ds(2 * s + c, 1)].rearrange("p o z a n -> p (o z a n)"), px[c][:],
                                           ACT.Copy).then_inc(gs_out, 1)
                for d in R2:
                    act.wait_ge(uw_ready[d], s + 1)
                    act.activation(wtn[d][:].rearrange("p h j -> p (h j)"), pa[d][:], ACT.Copy, scale=-1.0).then_inc(wt_done[d], 1)
                if lat:
                    act.wait_ge(og_ready, s - TC + 1)
                    act.activation(K.xo[:, bass.ds(s - TC, 1), 0:V_A].rearrange("p o n -> p (o n)"), px[0][:],
                                   ACT.Copy).then_inc(og_out, 1)
            steps(act, step)

        @block.vector
        def _(dve):
            dve.tensor_copy(sm[:, :, :, 0, :], K.gdn_la[:]).then_inc(sm_step, 1)
            dve.tensor_copy(sm[:, :, :, 2, :], K.beta[:]).then_inc(sm_step, 1)
            dve.wait_ge(sm_step, SM_STEPS - 1)
            dve.wait_ge(og_out, 1)
            dve.tensor_tensor(sm[:, :, :, 3, :], sm[:, :, :, 3, :], K.beta[:], ALU.mult).then_inc(sm_step, 1)
            dve.wait_ge(init_done, 1)
            for d in R2:
                dve.sem_inc(o_done[d], 1)

            def step(s, lat):
                for d in R2:
                    dve.wait_ge(gr_ready[d], s + 1)
                    for c in R2:
                        dve.tensor_tensor(lmat[d][half(c)], pa[d][half(c)].rearrange("p (c h j) -> p c h j", c=2, h=NH)[:, c],
                                          coef[d][half(c), 1].unsqueeze(2).broadcast_to([C, NH, C]),
                                          ALU.subtract).then_inc(diff_done[d], 1)
                    dve.wait_ge(diff_done[d], 2 * (s + 1))
                    dve.scalar_tensor_tensor(dec[d][:, 0], lmat[d][:], -1.0,
                                             K.negmask[:, d, 0].unsqueeze(1).broadcast_to([P, NH, C]),
                                             ALU.mult, ALU.min).then_inc(dec_in[d], 1)
                    dve.tensor_tensor(dec[d][:, 1], lmat[d][:], K.negmask[:, d, 1].unsqueeze(1).broadcast_to([P, NH, C]),
                                      ALU.min).then_inc(dec_in[d], 1)
                dve.wait_ge(b_done, s + 1)
                bf = bs[:, 0].rearrange("p a n -> p (a n)")
                br = bs[:, 1].rearrange("p a n -> p (a n)")
                for z, (b, end) in enumerate(((bf, C - 1), (br, 0))):
                    bb = b.rearrange("p (m j) -> p m j", j=C)
                    last = dve.tensor_tensor(kin[:, z].rearrange("p a (c j) -> p (a c) j", j=C),
                                             bb[:, :, end:end + 1].broadcast_to([P, 4, C]), bb, ALU.subtract)
                if lat:
                    for lev in range(LEVELS):
                        h = 1 << lev
                        n = 256 // (2 * h)
                        f, r = (b.rearrange("p (m u j) -> p m u j", u=2, j=h) for b in (bf, br))
                        wq, wk = (wl[:, lev, x].rearrange("p a (m u j) -> p (a m) u j", u=2, j=h) for x in R2)
                        mid_f = f[:, :, 0, h - 1:h].broadcast_to([P, n, h])
                        mid_r = r[:, :, 1, 0:1].broadcast_to([P, n, h])
                        dve.tensor_tensor(wq[:, :, 1, :], f[:, :, 1, :], mid_f, ALU.subtract)
                        dve.tensor_tensor(wq[:, :, 0, :], r[:, :, 0, :], mid_r, ALU.subtract)
                        dve.tensor_tensor(wk[:, :, 0, :], mid_f, f[:, :, 0, :], ALU.subtract)
                        last = dve.tensor_tensor(wk[:, :, 1, :], mid_r, r[:, :, 1, :], ALU.subtract)
                last.then_inc(sub_done, 1)
                for d in R2:
                    dve.wait_ge(kq_ready[d], s + 1)
                    dve.wait_ge(dec_done[d], s + 1)
                    kq = pb[d][:].rearrange("p (h x j) -> p h x j", h=NH, x=2)
                    dve.tensor_tensor(lmat[d][:], dec[d][:, 0], kq[:, :, 0, :], ALU.mult).then_inc(kkd_done[d], 1)
                    if lat:
                        for c in R2:
                            dve.tensor_tensor(atp[d][half(c), :, half(c)], dec[d][half(c), 1], kq[half(c), :, 1, :],
                                              ALU.mult).then_inc(at_done[d], 1)
                    dve.wait_ge(kkd_done[d], s + 1)
                    dve.tensor_tensor(lmat[d][:], lmat[d][:], coef[d][:, 2].unsqueeze(2).broadcast_to([P, NH, C]),
                                      ALU.mult).then_inc(l_done[d], 1)
                dve.wait_ge(exp_done, 3 * s - 2 if lat else s + 1)
                dve.wait_ge(ld_g, 48 * (s + 1))
                dve.tensor_tensor(kin[:].rearrange("p z a n -> p z (a n)"), kin[:].rearrange("p z a n -> p z (a n)"),
                                  gqk[:, 1].rearrange("p a n -> p (a n)").unsqueeze(1).broadcast_to([P, 2, 256]),
                                  ALU.mult).then_inc(io_done, 1)
                id4 = K.ident64[:].unsqueeze(1).broadcast_to([P, NH, C])
                for d in R2:
                    dve.wait_ge(loff_done[d], 2 * s + 1)
                    dve.tensor_tensor(xx[d][:, 1], id4, loff[d][:, 0], ALU.subtract).then_inc(x_done[d], 1)
                if lat:
                    dve.wait_ge(exp_done, 3 * s - 1)
                    dve.wait_ge(ld_gq, 16 * (s - TC + 1))
                    dve.tensor_tensor(wl[:].rearrange("p l x a n -> p l (x a n)"),
                                      wl[:].rearrange("p l x a n -> p l (x a n)"),
                                      gqk[:].rearrange("p x a n -> p (x a n)").unsqueeze(1).broadcast_to([P, LEVELS, 512]),
                                      ALU.mult).then_inc(wl_done, 1)
                for d in R2:
                    dve.wait_ge(p_ready[d], s * LEVELS + 1)
                    dve.tensor_tensor(xx[d][:, 0], id4, pa[d][:, :NH * C].rearrange("p (h j) -> p h j", h=NH),
                                      ALU.subtract).then_inc(x_done[d], 1)
                for lev in range(1, LEVELS):
                    for d in R2:
                        dve.wait_ge(p_ready[d], s * LEVELS + lev + 1)
                        if lev < LAST_LEVEL:
                            dve.tensor_tensor(xx[d][:].rearrange("p x h j -> p (x h j)"),
                                              xx[d][:].rearrange("p x h j -> p (x h j)"), pb[d][:],
                                              ALU.subtract).then_inc(x_done[d], 1)
                        else:
                            for c in R2:
                                dve.tensor_tensor(xtp[d][half(c), :, half(c)], xx[d][half(c), 0],
                                                  pb[d][half(c), :NH * C].rearrange("p (h j) -> p h j", h=NH),
                                                  ALU.subtract).then_inc(xtp_done[d], 1)
                    if lat and lev <= NH:
                        hd = lev - 1
                        dve.wait_ge(sc_ready, NH * (s - TC) + hd + 1)
                        dve.tensor_tensor(msc[:, hd % 2].rearrange("p l j -> p (l j)"), px[1][:, :(LEVELS + 1) * C],
                                          K.smask[:].rearrange("p l j -> p (l j)"), ALU.mult).then_inc(msc_done, 1)
                        dve.wait_ge(msc_done, NH * (s - TC) + hd + 1)
                        for c in R2:
                            dve.tensor_reduce(atg[half(c), hd, half(c)], msc[half(c), hd % 2].rearrange("p l j -> p j l"),
                                              AX.X, ALU.add).then_inc(atg_done, 1)
                for n in R2:
                    for d in R2:
                        c = chunk_order(d)[n]
                        dve.wait_ge(ws_ready[d], 2 * s + n + 1)
                        dve.tensor_copy(delta[d][half(c)].rearrange("p h j -> p (h j)"), pc[d][half(c)]).then_inc(delta_done[d], 1)
                    for d in R2:
                        dve.wait_ge(ds_ready[d], 2 * s + n + 1)
                        dve.wait_ge(sta_done[d], 2 * s + n + 1)
                        dve.tensor_tensor(st[d][:].rearrange("p h j -> p (h j)"), sta[d][:].rearrange("p h j -> p (h j)"),
                                          pa[d][:], ALU.add).then_inc(st_done[d], 1)
                if lat:
                    for d in R2:
                        o = K.xo[:, bass.ds(s - TC if d == 0 else 9 - s, 1), V_A:].rearrange("p o n -> p (o n)")
                        dve.wait_ge(o_ready[d], s - TC + 1)
                        dve.wait_ge(o_done[1 - d], s - TC + 1 + d)
                        dve.tensor_tensor(o, o, pb[d][:], ALU.add).then_inc(o_done[d], 1)
            steps(dve, step)

            def advance(z, to, frm):
                for a in R2:
                    dve.scalar_tensor_tensor(K.ga_st[:, bass.ds(to, 1), z, a].rearrange("p o n -> p (o n)"),
                                             K.ga_st[:, bass.ds(frm, 1), z, a].rearrange("p o n -> p (o n)"),
                                             K.ga_a[:, bass.ds(to, 1), z, a],
                                             K.ga_st[:, bass.ds(to, 1), z, a].rearrange("p o n -> p (o n)"),
                                             ALU.mult, ALU.add).then_inc(scan, 1)

            dve.wait_ge(gs_out, 2 * NT)
            for i in range(1, 2 * TC):
                advance(0, i, i - 1)
                advance(1, 2 * TC - 1 - i, 2 * TC - i)
                dve.wait_ge(scan, 4 * i)
            dve.tensor_copy(K.ga_st[:, 2 * NT, 1], K.ga_st[:, 0, 1]).then_inc(scan, 1)
            dve.wait_ge(scan, 4 * (2 * TC - 1) + 1)
            for i in range(2 * TL):
                advance(0, i + 4, i + 3)
                advance(1, 19 - i, 20 - i)
                dve.wait_ge(scan, 4 * (i + 2 * TC) + 1)

        @block.tensor
        def _(pe):
            for x, tri in enumerate((K.tri, K.trix)):
                for d in R2:
                    last = pe.matmul(px[0][:, 80 * x + 40 * d:80 * x + 40 * d + 40], tri[:, d],
                                     K.gdn_la[:, d].rearrange("p t h -> p (t h)"), start=True, stop=True)
            last.then_inc(g_ready, 1)
            pe.wait_ge(init_done, 1)

            def level_y(d, s, lev):
                if lev == 1:
                    pe.wait_ge(x_done[d], (LEVELS) * s + 2)
                else:
                    pe.wait_ge(x_done[d], LEVELS * s + lev + 1)
                    pe.wait_ge(y_done[d], (LEVELS - 1) * s + lev - 1)
                pe.wait_ge(loff_done[d], 2 * s + 2)
                for h in range(NH):
                    for c in R2:
                        last = pe.matmul(pa[d][half(c), h * C:(h + 1) * C], loff[d][half(c), lev, h],
                                         xx[d][half(c), 0, h], start=True, stop=True)
                last.then_inc(y_ready[d], 1)

            def level_p(d, s, lev, lat):
                pe.wait_ge(y_done[d], (LEVELS - 1) * s + lev)
                if lat and lev == 1:
                    pe.wait_ge(at_done[d], 2 * (s - TC + 1))
                for h in range(NH):
                    for c in R2:
                        last = pe.matmul(pb[d][half(c), h * C:(h + 1) * C], xx[d][half(c), 1, h],
                                         yy[d][half(c), h], start=True, stop=True)
                        if lev < LAST_LEVEL:
                            last = pe.matmul(pb[d][half(c), (NH + h) * C:(NH + h + 1) * C], yy[d][half(c), h],
                                             xx[d][half(c), 1, h], start=True, stop=True)
                last.then_inc(p_ready[d], 1)

            def scores(s, hd):
                a, r = hd // 2, half(hd % 2)
                if hd == 0:
                    pe.wait_ge(wl_done, s - TC + 1)
                    after(pe, gs_out, 2 * s)
                else:
                    pe.wait_ge(msc_done, NH * (s - TC) + hd)
                for c in R2:
                    for lev in range(LEVELS + 1):
                        kk, qq = ((wl[r, lev, 1, a, half(c)], wl[r, lev, 0, a, half(c)]) if lev < LEVELS
                                  else (gqk[r, 1, a, half(c)], gqk[r, 0, a, half(c)]))
                        last = pe.matmul(px[1][half(c), lev * C:(lev + 1) * C], kk, qq, start=True, stop=True)
                last.then_inc(sc_ready, 1)

            def step(s, lat):
                for d in R2:
                    pe.wait_ge(tri_la_done[d], s + 1)
                    after(pe, st_done[d], 2 * s)
                    pe.matmul(pa[d][:], K.ones[:], rows[d][:].rearrange("p c h j -> p (c h j)"), start=True,
                              stop=True).then_inc(gr_ready[d], 1)
                pe.wait_ge(ld_g, 48 * (s + 1))
                after(pe, gs_out, 2 * s)
                pe.wait_ge(og_out, s - TC + 1 if lat else 1)
                for z in R2:
                    for a in R2:
                        last = pe.matmul(px[0][:, (2 * z + a) * P:(2 * z + a + 1) * P],
                                         gla[:, (2 * z + a) * P:(2 * z + a + 1) * P], K.tri[:, z], start=True, stop=True)
                last.then_inc(b_ready, 1)
                for d in R2:
                    pe.wait_ge(ld_k[d], 16 * (s + 1))
                    if lat:
                        pe.wait_ge(ld_q[d], 16 * (s - TC + 1))
                        pe.wait_ge(o_done[d], s - TC + 1)
                    after(pe, xtp_done[d], 2 * s)
                    for h in range(NH):
                        for c in R2:
                            kk = kc[d][:, h, half(c)]
                            last = pe.matmul(pb[d][half(c), 2 * h * C:(2 * h + 1) * C], kk, kk, start=True, stop=True)
                            if lat:
                                last = pe.matmul(pb[d][half(c), (2 * h + 1) * C:(2 * h + 2) * C], kk,
                                                 qc[d][:, h, half(c)], start=True, stop=True)
                    last.then_inc(kq_ready[d], 1)
                for d in R2:
                    pe.wait_ge(loff_done[d], 2 * s + 1)
                    pe.wait_ge(eg_done[d], s + 1)
                    for h in range(NH):
                        for c in R2:
                            last = pe.matmul(pa[d][half(c), h * C:(h + 1) * C], loff[d][half(c), 0, h],
                                             K.ident64[half(c)], start=True, stop=True)
                    last.then_inc(p_ready[d], 1)
                for lev in range(1, LEVELS):
                    for d in R2:
                        level_y(d, s, lev)
                    if lat and lev <= NH:
                        scores(s, lev - 1)
                    if lev == 2:
                        pe.wait_ge(io_done, s + 1)
                        pe.wait_ge(b_done, s + 1)
                        for z in R2:
                            for a in R2:
                                last = pe.transpose(px[0][:, (2 * z + a) * P:(2 * z + a + 1) * P], kin[:, z, a], K.ident[:])
                        last.then_inc(kt_ready, 1)
                    if lev == LAST_LEVEL:
                        for c in R2:
                            pe.wait_ge(kt_out, s + 1)
                            if lat and c == 1:
                                pe.wait_ge(msc_done, NH * (s - TC + 1))
                            for z in R2:
                                for hd in range(NH):
                                    a, x = hd // 2, hd % 2
                                    last = pe.matmul(px[c][half(x), (2 * z + a) * P:(2 * z + a + 1) * P],
                                                     kint[half(c), z, a, half(x)], gva[half(c), hd], start=True, stop=True)
                            last.then_inc(gs_ready, 1)
                    for d in R2:
                        level_p(d, s, lev, lat)
                for d in R2:
                    pe.wait_ge(xtp_done[d], 2 * (s + 1))
                    pe.wait_ge(scaled_done[d], 3 * (s + 1))
                    after(pe, delta_done[d], 2 * s)
                    for h in range(NH):
                        pe.matmul(pc[d][:, h * P:(h + 1) * P], xtp[d][:, h], bv[d][:, h], start=(h == 0), stop=False,
                                  skip_group_check=True)
                    for h in range(NH):
                        last = pe.matmul(pa[d][:, h * P:(h + 1) * P], bk[d][:, h], xtp[d][:, h], start=True, stop=True)
                    last.then_inc(uw_ready[d], 1)
                for n in R2:
                    for d in R2:
                        c = chunk_order(d)[n]
                        pe.wait_ge(wt_done[d], s + 1)
                        after(pe, st_done[d], 2 * s + n)
                        for h in range(NH):
                            last = pe.matmul(pc[d][half(c), h * P:(h + 1) * P], wtn[d][:, h, half(c)], st[d][:, h],
                                             start=False, stop=True, skip_group_check=True)
                        last.then_inc(ws_ready[d], 1)
                        if lat:
                            pe.wait_ge(qd_done[d], s - TC + 1)
                            for h in range(NH):
                                pe.matmul(pb[d][half(c), h * P:(h + 1) * P], qd[d][:, h, half(c)], st[d][:, h],
                                          start=(h == 0), stop=False, skip_group_check=True)
                    for d in R2:
                        c = chunk_order(d)[n]
                        pe.wait_ge(delta_done[d], 2 * s + n + 1)
                        if n == 1:
                            pe.wait_ge(st_done[d], 2 * s + 1)
                        for h in range(NH):
                            last = pe.matmul(pa[d][:, h * P:(h + 1) * P], kd[d][half(c), h], delta[d][half(c), h],
                                             start=True, stop=True)
                        last.then_inc(ds_ready[d], 1)
                if lat:
                    for d in R2:
                        pe.wait_ge(at_done[d], 2 * (s - TC + 1))
                        for h in range(NH):
                            last = pe.matmul(pb[d][:, h * P:(h + 1) * P], atp[d][:, h], delta[d][:, h],
                                             start=False, stop=True, skip_group_check=True)
                        last.then_inc(o_ready[d], 1)
                    pe.wait_ge(atg_done, 2 * NH * (s - TC + 1))
                    pe.wait_ge(gs_out, 2 * s + 1)
                    for hd in range(NH):
                        last = pe.matmul(px[0][:, hd * P:(hd + 1) * P], atg[:, hd], gva[:, hd], start=True, stop=True)
                    last.then_inc(og_ready, 1)
            steps(pe, step)


def merge_phase(nc, A, K, S):
    with ExitStack() as ctx:
        m = Alloc(nc, ctx, "merge_")
        wraw = m.sb("wraw", [P, 2, D])
        whi, wlo = m.sb("wohi", [P, KT, D], F32R), m.sb("wolo", [P, KT, D], F32R)
        gt1 = m.sb("gt1", [P, D])
        diag = m.sb("diag", [P, 2, P])
        gains = m.sb("gains", [P, 2, P])
        qs = m.sb("qs", [P, 2, 2, 2, P])
        gates = m.sb("gates", [P, 2, D])
        xs = m.sb("mxs", [P, 2, D])
        sq = m.sb("msq", [P, D])
        ss, var, lnv, rs = (m.sb(n, [P, 8]) for n in ("mss", "mvar", "mlnv", "mrs"))
        yhi, ylo = m.sb("yhi", [P, KT, P], F32R), m.sb("ylo", [P, KT, P], F32R)
        ps_o = m.ps("mps_o", [P, 2, 2, 512])
        ps_t = m.ps("mps_t", [P, 2, 512])
        ps_p = m.ps("mps_p", [P, 2, 512])
        row_bank = [ps_p[:, 0], ps_p[:, 1], ps_o[:, 1, 0], ps_o[:, 1, 1]]
        ld_wo, ld_gain = [m.sem("ld_wo0"), m.sem("ld_wo1")], m.sem("ld_gain")
        ld_qs, ld_gates, ld_xs = ([m.sem(f"{n}{b}") for b in range(2)] for n in ("ld_qs", "ld_gates", "ld_xs"))
        diag_done, diag_used, row_out = m.sem("diag_done"), m.sem("diag_used"), m.sem("mrow_out")
        wo_scaled, wo_hi, wo_lo = m.sem("wo_scaled"), m.sem("wo_hi"), m.sem("wo_lo")
        inter_ready, o_done, sq_done, ss_done = m.sem("inter_ready"), m.sem("mo_done"), m.sem("msq_done"), m.sem("mss_done")
        var_done, ln_done, rs_done = m.sem("mvar_done"), m.sem("mln_done"), m.sem("mrs_done")
        gain_done, norm_done, y_done = m.sem("gain_done"), m.sem("norm_done"), m.sem("my_done")
        t_ready, hi_done, lo_done = m.sem("mt_ready"), m.sem("mhi_done"), m.sem("mlo_done")
        p_ready, x1_done = m.sem("mp_ready"), m.sem("x1_done")
        block = ctx.enter_context(nc.Block())

        @block.sync
        def _(sp):
            for i, n in enumerate(("gla_norm_g", "gdn_norm_g")):
                sp.dma_start(gains[:, i], A[n].partition_broadcast(P).rearrange("p a n -> p (a n)")).then_inc(ld_gain, 16)

            def states_query(t):
                b = t % 2
                if t >= 2:
                    sp.wait_ge(inter_ready, t - 1)
                sp.dma_start(qs[:, b], S["qin"][t]).then_inc(ld_qs[b], 16)

            def tile_inputs(t):
                b = t % 2
                if t >= 2:
                    sp.wait_ge(y_done, t - 1)
                sp.dma_start(gates[:, b], S["gate"][t]).then_inc(ld_gates[b], 16)
                if t >= 2:
                    sp.wait_ge(x1_done, 2 * (t - 1))
                sp.dma_start(xs[:, b], A["x"][t * P:(t + 1) * P]).then_inc(ld_xs[b], 16)

            states_query(0)
            tile_inputs(0)
            for k in range(KT):
                if k >= 2:
                    sp.wait_ge(wo_lo, k - 1)
                sp.dma_start(wraw[:, k % 2], A["w_out"][k * P:(k + 1) * P]).then_inc(ld_wo[k % 2], 16)
            states_query(1)
            for t in range(1, TL):
                if t + 1 < TL:
                    states_query(t + 1)
                tile_inputs(t)

        @block.gpsimd
        def _(pool):
            def gain(t):
                pool.wait_ge(ld_gates[t % 2], 16 * (t // 2 + 1))
                g = gates[:, t % 2].rearrange("p (g h n) -> p g h n", g=2, h=NH)
                pool.tensor_tensor(g, g, gains[:].unsqueeze(2).broadcast_to([P, 2, NH, P]), ALU.mult).then_inc(gain_done, 1)

            pool.wait_ge(ld_gain, 32)
            gain(0)
            for k in range(KT):
                pool.wait_ge(wo_hi, k + 1)
                pool.tensor_tensor(wlo[:, k], wraw[:, k % 2], whi[:, k].bitcast(F32), ALU.subtract).then_inc(wo_lo, 1)
            for t in range(TL):
                pool.wait_ge(o_done, 2 * (t + 1))
                if t:
                    pool.wait_ge(ss_done, t)
                pool.tensor_tensor(sq[:], K.xo[:, t], K.xo[:, t], ALU.mult).then_inc(sq_done, 1)
                pool.wait_ge(norm_done, t + 1)
                pool.wait_ge(gain_done, t + 1)
                pool.tensor_tensor(K.xo[:, t], K.xo[:, t], gates[:, t % 2], ALU.mult).then_inc(y_done, 1)
                if t + 1 < TL:
                    gain(t + 1)

        @block.scalar
        def _(act):
            for r in range(4):
                act.wait_ge(diag_used, 4 * (r + 1))
                dst = gt1 if r < 2 else K.gt2
                act.activation(dst[:, (r % 2) * 512:(r % 2 + 1) * 512], row_bank[r], ACT.Copy).then_inc(row_out, 1)
            for k in range(KT):
                act.wait_ge(wo_scaled, k + 1)
                act.activation(whi[:, k], wraw[:, k % 2], ACT.Copy).then_inc(wo_hi, 1)
            for t in range(TL):
                act.wait_ge(var_done, t + 1)
                act.activation(lnv[:], var[:], ACT.Ln).then_inc(ln_done, 1)
                act.wait_ge(ln_done, t + 1)
                act.activation(rs[:], lnv[:], ACT.Exp, scale=-0.5).then_inc(rs_done, 1)
                for i in range(2):
                    act.wait_ge(t_ready, 2 * t + i + 1)
                    if t:
                        act.wait_ge(p_ready, 2 * t)
                    act.activation(yhi[:, 4 * i:4 * i + 4].rearrange("p k n -> p (k n)"), ps_t[:, i],
                                   ACT.Copy).then_inc(hi_done, 1)

        @block.vector
        def _(dve):
            for i in range(2 * KT):
                if i >= 2:
                    dve.wait_ge(diag_used, i - 1)
                dve.tensor_scalar(diag[:, i % 2], K.ident[:], K.mod[:, (16 if i < KT else 40) + i % KT, 0:1], None,
                                  ALU.mult).then_inc(diag_done, 1)

            def outputs(t):
                for i in range(2):
                    cs = slice(i * 512, (i + 1) * 512)
                    dve.wait_ge(p_ready, 2 * t + i + 1)
                    dve.wait_ge(ld_xs[t % 2], 16 * (t // 2 + 1))
                    dve.tensor_tensor(K.xo[:, t, cs], xs[:, t % 2, cs], ps_p[:, i], ALU.add).then_inc(x1_done, 1)

            def norms(t):
                dve.wait_ge(inter_ready, t + 1)
                for x in range(2):
                    o = K.xo[:, t, 0:V_A].rearrange("p (a x n) -> p a x n", a=2, x=2)[:, :, x]
                    dve.tensor_tensor(o, o, ps_o[:, t % 2, x, 0:2 * P].rearrange("p (a n) -> p a n", a=2),
                                      ALU.add).then_inc(o_done, 1)
                dve.wait_ge(sq_done, t + 1)
                dve.tensor_reduce(ss[:], sq[:].rearrange("p (h n) -> p h n", n=P), AX.X, ALU.add).then_inc(ss_done, 1)
                dve.wait_ge(ss_done, t + 1)
                dve.tensor_scalar(var[:], ss[:], 1.0 / P, EPS, ALU.mult, ALU.add).then_inc(var_done, 1)
                dve.wait_ge(rs_done, t + 1)
                o = K.xo[:, t].rearrange("p (h n) -> p h n", n=P)
                dve.tensor_tensor(o, o, rs[:].unsqueeze(2).broadcast_to([P, 8, P]), ALU.mult).then_inc(norm_done, 1)

            def low(t):
                for i in range(2):
                    dve.wait_ge(hi_done, 2 * t + i + 1)
                    hi = yhi[:, 4 * i:4 * i + 4].rearrange("p k n -> p (k n)")
                    dve.tensor_tensor(ylo[:, 4 * i:4 * i + 4].rearrange("p k n -> p (k n)"), ps_t[:, i], hi.bitcast(F32),
                                      ALU.subtract).then_inc(lo_done, 1)

            dve.wait_ge(row_out, 2)
            for k in range(KT):
                dve.wait_ge(ld_wo[k % 2], 16 * (k // 2 + 1))
                dve.tensor_tensor(wraw[:, k % 2], wraw[:, k % 2], gt1[:], ALU.mult).then_inc(wo_scaled, 1)
            for t in range(TL):
                norms(t)
                if t:
                    outputs(t - 1)
                low(t)
            outputs(TL - 1)

        @block.tensor
        def _(pe):
            for i in range(2 * KT):
                pe.wait_ge(diag_done, i + 1)
                last = pe.matmul(row_bank[i // 4][:, (i % 4) * P:(i % 4 + 1) * P], K.ones[:], diag[:, i % 2],
                                 start=True, stop=True)
                last.then_inc(diag_used, 1)

            def inter(t):
                pe.wait_ge(ld_qs[t % 2], 16 * (t // 2 + 1))
                if t == 1:
                    pe.wait_ge(row_out, 4)
                if t >= 2:
                    pe.wait_ge(o_done, 2 * (t - 1))
                for c in range(2):
                    cc, toks = 2 * (t + TC) + c, slice(c * C, (c + 1) * C)
                    for hd in range(NH):
                        a, x = hd // 2, hd % 2
                        r = slice(x * C, (x + 1) * C)
                        for z in range(2):
                            last = pe.matmul(ps_o[toks, t % 2, x, a * P:(a + 1) * P], qs[r, t % 2, z, a, toks],
                                             K.ga_st[r, cc - 1 if z == 0 else cc + 1, z, a], start=(z == 0), stop=(z == 1))
                last.then_inc(inter_ready, 1)

            inter(0)
            for t in range(TL):
                if t + 1 < TL:
                    inter(t + 1)
                pe.wait_ge(y_done, t + 1)
                if t:
                    pe.wait_ge(lo_done, 2 * t)
                for i in range(2):
                    for j in range(4):
                        last = pe.transpose(ps_t[:, i, j * P:(j + 1) * P],
                                            K.xo[:, t, (4 * i + j) * P:(4 * i + j + 1) * P], K.ident[:])
                    last.then_inc(t_ready, 1)
                pe.wait_ge(lo_done, 2 * (t + 1))
                if t == 0:
                    pe.wait_ge(wo_lo, KT)
                    pe.wait_ge(row_out, 2)
                if t:
                    pe.wait_ge(x1_done, 2 * t)
                for i in range(2):
                    cs = slice(i * 512, (i + 1) * 512)
                    for k in range(KT):
                        last = mm3(pe, ps_p[:, i], yhi[:, k], ylo[:, k], whi[:, k, cs], wlo[:, k, cs],
                                   k == 0, k == KT - 1)
                    last.then_inc(p_ready, 1)


def mlp_phase(nc, A, K, S, out):
    GJ = 4
    NG = FF // (GJ * P)
    with ExitStack() as ctx:
        m = Alloc(nc, ctx, "mlp_")
        h2hi, h2lo = m.sb("h2hi", [P, KT, NLAT], F32R), m.sb("h2lo", [P, KT, NLAT], F32R)
        ss, var, lnv, rstd = (m.sb(n, [P, TL]) for n in ("fss", "fvar", "flnv", "frstd"))
        sc2 = m.sb("sc2", [P, KT])
        tmp = m.sb("ftmp", [P, 2, 512])
        with ExitStack() as ctx_in:
            mi = Alloc(nc, ctx_in, "mlp_in_")
            xn = mi.sb("fxn", [P, TL, D])
            junk = mi.sb("fjunk", [P, D])
            ps = mi.ps("fps_t", [P, 4, 512])
            ss_done, var_done, ln_done, rstd_done = (mi.sem(n) for n in ("fss_done", "fvar_done", "fln_done", "frstd_done"))
            sc_done, xn_done, t_ready = mi.sem("fsc_done"), mi.sem("fxn_done"), mi.sem("ft_ready")
            hf_done, hi_done, lo_done = mi.sem("fhf_done"), mi.sem("fhi_done"), mi.sem("flo_done")
            units = [(k, s) for s in range(2) for k in range(KT)]
            block = ctx_in.enter_context(nc.Block())

            @block.scalar
            def _(act):
                for t in range(TL):
                    if t:
                        act.wait_ge(ss_done, t)
                    act.activation(junk[:], K.xo[:, t], ACT.Square, accum_out=ss[:, t:t + 1]).then_inc(ss_done, 1)
                    if t % 4 == 3:
                        hs = slice(t - 3, t + 1)
                        act.wait_ge(var_done, t // 4 + 1)
                        act.activation(lnv[:, hs], var[:, hs], ACT.Ln).then_inc(ln_done, 1)
                        act.wait_ge(ln_done, t // 4 + 1)
                        act.activation(rstd[:, hs], lnv[:, hs], ACT.Exp, scale=-0.5).then_inc(rstd_done, 1)
                for u, (k, s) in enumerate(units):
                    act.wait_ge(hf_done, u + 1)
                    act.activation(h2hi[:, k, s * 512:(s + 1) * 512], tmp[:, u % 2], ACT.Copy).then_inc(hi_done, 1)

            @block.vector
            def _(dve):
                dve.tensor_scalar(sc2[:], K.mod[:, 32:40, 0], 1.0, None, ALU.add).then_inc(sc_done, 1)
                dve.wait_ge(sc_done, 1)
                dve.tensor_tensor(sc2[:], sc2[:], K.cols[:, 56:64], ALU.mult).then_inc(sc_done, 1)
                for hlf in range(2):
                    hs = slice(4 * hlf, 4 * hlf + 4)
                    dve.wait_ge(ss_done, 4 * hlf + 4)
                    dve.tensor_scalar(var[:, hs], ss[:, hs], 1.0 / D, EPS, ALU.mult, ALU.add).then_inc(var_done, 1)
                    dve.wait_ge(rstd_done, hlf + 1)
                    for t in range(4 * hlf, 4 * hlf + 4):
                        dve.tensor_scalar(xn[:, t], K.xo[:, t], rstd[:, t:t + 1], None, ALU.mult).then_inc(xn_done, 1)
                dve.wait_ge(sc_done, 2)
                for u, (k, s) in enumerate(units):
                    dve.wait_ge(t_ready, u + 1)
                    if u >= 2:
                        dve.wait_ge(lo_done, u - 1)
                    dve.tensor_scalar(tmp[:, u % 2], ps[:, u % 4], sc2[:, k:k + 1], K.mod[:, 24 + k, 0:1],
                                      ALU.mult, ALU.add).then_inc(hf_done, 1)

            @block.gpsimd
            def _(pool):
                for u, (k, s) in enumerate(units):
                    cs = slice(s * 512, (s + 1) * 512)
                    pool.wait_ge(hi_done, u + 1)
                    pool.tensor_tensor(h2lo[:, k, cs], tmp[:, u % 2], h2hi[:, k, cs].bitcast(F32),
                                       ALU.subtract).then_inc(lo_done, 1)

            @block.tensor
            def _(pe):
                for u, (k, s) in enumerate(units):
                    pe.wait_ge(xn_done, 4 * s + 4)
                    if u >= 4:
                        pe.wait_ge(hf_done, u - 3)
                    for i in range(4):
                        last = pe.transpose(ps[:, u % 4, i * P:(i + 1) * P], xn[:, 4 * s + i, k * P:(k + 1) * P], K.ident[:])
                    last.then_inc(t_ready, 1)

        hhi, hlo = m.sb("hidhi", [P, GJ, NLAT], F32R), m.sb("hidlo", [P, GJ, NLAT], F32R)
        w1raw = m.sb("w1raw", [P, 2, KT, P])
        w1hi, w1lo = m.sb("w1hi", [P, 2, KT, P], F32R), m.sb("w1lo", [P, 2, KT, P], F32R)
        w2raw = m.sb("w2raw", [P, D])
        w2hi, w2lo = m.sb("w2hi", [P, GJ, D], F32R), m.sb("w2lo", [P, GJ, D], F32R)
        ps_a = m.ps("fps_a", [P, 4, 512])
        ps_b = m.ps("fps_b", [P, 4, 512])
        ld_w1, ld_w2 = [m.sem("ld_w1_0"), m.sem("ld_w1_1")], m.sem("ld_w2")
        w1_hi, w1_lo, w2_scaled, w2_hi, w2_lo = (m.sem(n) for n in ("w1_hi", "w1_lo", "w2_scaled", "w2_hi", "w2_lo"))
        a_ready, relu_done, sq_done, hid_hi, hid_lo = (m.sem(n) for n in ("a_ready", "relu_done", "fsq_done", "hid_hi", "hid_lo"))
        b_ready, x2_done = m.sem("b_ready"), m.sem("x2_done")
        NO = 2 * TL

        def after(eng, sem, n):
            if not isinstance(n, int) or n > 0:
                eng.wait_ge(sem, n)

        def groups(eng, body):
            for g in range(NG):
                body(g, g == NG - 1)

        block = ctx.enter_context(nc.Block())

        @block.sync
        def _(sp):
            w1v = A["w_ff1"].rearrange("(k p) f -> p k f", p=P)

            def load_w1(g, j):
                f = GJ * g + j
                after(sp, w1_lo, f - 1)
                sp.dma_start(w1raw[:, j % 2], w1v[:, :, bass.ds(f * P, P)]).then_inc(ld_w1[j % 2], 16)

            def group(g, last):
                for j in range(GJ):
                    f = GJ * g + j
                    after(sp, w2_lo, f)
                    sp.dma_start(w2raw[:], A["w_ff2"][bass.ds(f * P, P)]).then_inc(ld_w2, 16)
                    if not (last and j == GJ - 1):
                        load_w1(g if j < GJ - 1 else g + 1, (j + 1) % GJ)

            load_w1(0, 0)
            groups(sp, group)

        @block.gpsimd
        def _(pool):
            def low_w1(g, j):
                f = GJ * g + j
                pool.wait_ge(w1_hi, f + 1)
                pool.tensor_tensor(w1lo[:, j % 2], w1raw[:, j % 2], w1hi[:, j % 2].bitcast(F32),
                                   ALU.subtract).then_inc(w1_lo, 1)

            def group(g, last):
                for j in range(GJ):
                    f = GJ * g + j
                    if not (last and j == GJ - 1):
                        low_w1(g if j < GJ - 1 else g + 1, (j + 1) % GJ)
                    pool.wait_ge(ld_w2, 16 * (f + 1))
                    pool.tensor_tensor(w2raw[:], w2raw[:], K.gt2[:], ALU.mult).then_inc(w2_scaled, 1)
                    for i in range(2):
                        cs = slice(i * 512, (i + 1) * 512)
                        pool.wait_ge(hid_hi, 2 * f + i + 1)
                        pool.tensor_tensor(hlo[:, j, cs], tmp[:, i], hhi[:, j, cs].bitcast(F32),
                                           ALU.subtract).then_inc(hid_lo, 1)

            low_w1(0, 0)
            groups(pool, group)

        @block.scalar
        def _(act):
            def high_w1(g, j):
                f = GJ * g + j
                after(act, a_ready, 2 * (f - 1))
                act.wait_ge(ld_w1[j % 2], 16 * (2 * g + j // 2 + 1))
                act.activation(w1hi[:, j % 2], w1raw[:, j % 2], ACT.Copy).then_inc(w1_hi, 1)

            def group(g, last):
                for j in range(GJ):
                    f = GJ * g + j
                    if not (last and j == GJ - 1):
                        high_w1(g if j < GJ - 1 else g + 1, (j + 1) % GJ)
                    for i in range(2):
                        after(act, hid_lo, 2 * f + i - 1)
                        act.wait_ge(a_ready, 2 * f + i + 1)
                        act.activation(tmp[:, i], ps_a[:, (2 * j + i) % 4], ACT.Relu).then_inc(relu_done, 1)
                    for i in range(2):
                        act.wait_ge(sq_done, 2 * f + i + 1)
                        if j == 0 and i == 0:
                            after(act, b_ready, NO * g)
                        act.activation(hhi[:, j, i * 512:(i + 1) * 512], tmp[:, i], ACT.Copy).then_inc(hid_hi, 1)
                    act.wait_ge(w2_scaled, f + 1)
                    act.activation(w2hi[:, j], w2raw[:], ACT.Copy).then_inc(w2_hi, 1)

            high_w1(0, 0)
            groups(act, group)

        @block.vector
        def _(dve):
            def group(g, last):
                for j in range(GJ):
                    f = GJ * g + j
                    for i in range(2):
                        dve.wait_ge(relu_done, 2 * f + i + 1)
                        dve.tensor_tensor(tmp[:, i], tmp[:, i], tmp[:, i], ALU.mult).then_inc(sq_done, 1)
                    dve.wait_ge(w2_hi, f + 1)
                    dve.tensor_tensor(w2lo[:, j], w2raw[:], w2hi[:, j].bitcast(F32), ALU.subtract).then_inc(w2_lo, 1)
                for o in range(NO):
                    x = K.xo[:, o // 2, (o % 2) * 512:(o % 2 + 1) * 512]
                    dve.wait_ge(b_ready, NO * g + o + 1)
                    if o == 0:
                        after(dve, x2_done, NO * g)
                    dve.tensor_tensor(x, x, ps_b[:, o % 4], ALU.add).then_inc(x2_done, 1)
            groups(dve, group)

        @block.tensor
        def _(pe):
            def group(g, last):
                for j in range(GJ):
                    f = GJ * g + j
                    pe.wait_ge(w1_lo, f + 1)
                    for i in range(2):
                        after(pe, relu_done, 2 * f + i - 3)
                        for k in range(KT):
                            done = mm3(pe, ps_a[:, (2 * j + i) % 4], w1hi[:, j % 2, k], w1lo[:, j % 2, k],
                                       h2hi[:, k, i * 512:(i + 1) * 512], h2lo[:, k, i * 512:(i + 1) * 512],
                                       k == 0, k == KT - 1)
                        done.then_inc(a_ready, 1)
                for q in range(NO // 4):
                    for part in (range(GJ - 1), range(GJ - 1, GJ)):
                        for o in range(4 * q, 4 * q + 4):
                            t, cs = o // 2, slice((o % 2) * 512, (o % 2 + 1) * 512)
                            if part[0] == 0:
                                after(pe, x2_done, NO * g + o - 3)
                            for j in part:
                                f = GJ * g + j
                                if o == 4 * q:
                                    pe.wait_ge(w2_lo, f + 1)
                                    pe.wait_ge(hid_lo, 2 * f + (1 if t < 4 else 2))
                                done = mm3(pe, ps_b[:, o % 4], hhi[:, j, t * P:(t + 1) * P], hlo[:, j, t * P:(t + 1) * P],
                                           w2hi[:, j, cs], w2lo[:, j, cs], j == 0, j == GJ - 1)
                            if part[0]:
                                done.then_inc(b_ready, 1)
            groups(pe, group)


def final_phase(nc, A, K, out):
    with ExitStack() as ctx:
        m = Alloc(nc, ctx, "final_")
        gain, junk, y = m.sb("fgain", [P, D]), m.sb("gjunk", [P, D]), m.sb("fy", [P, TL, D])
        ss, var, lnv, rstd = (m.sb(n, [P, TL]) for n in ("gss", "gvar", "glnv", "grstd"))
        ld_gain, ss_done, var_done, ln_done, rstd_done, norm_done, y_done = (
            m.sem(n) for n in ("ld_fgain", "gss_done", "gvar_done", "gln_done", "grstd_done", "gnorm_done", "gy_done"))
        block = ctx.enter_context(nc.Block())

        @block.sync
        def _(sp):
            sp.dma_start(gain[:], A["final_norm_g"].partition_broadcast(P)).then_inc(ld_gain, 16)
            for t in range(TL):
                sp.wait_ge(y_done, t + 1)
                sp.dma_start(out[t * P:(t + 1) * P], y[:, t]).then_inc(K.stored, 16)
            sp.wait_ge(K.stored, 16 * TL)

        @block.scalar
        def _(act):
            for t in range(TL):
                if t:
                    act.wait_ge(ss_done, t)
                act.activation(junk[:], K.xo[:, t], ACT.Square, accum_out=ss[:, t:t + 1]).then_inc(ss_done, 1)
                if t % 4 == 3:
                    hs = slice(t - 3, t + 1)
                    act.wait_ge(var_done, t // 4 + 1)
                    act.activation(lnv[:, hs], var[:, hs], ACT.Ln).then_inc(ln_done, 1)
                    act.wait_ge(ln_done, t // 4 + 1)
                    act.activation(rstd[:, hs], lnv[:, hs], ACT.Exp, scale=-0.5).then_inc(rstd_done, 1)

        @block.vector
        def _(dve):
            for hlf in range(2):
                hs = slice(4 * hlf, 4 * hlf + 4)
                dve.wait_ge(ss_done, 4 * hlf + 4)
                dve.tensor_scalar(var[:, hs], ss[:, hs], 1.0 / D, EPS, ALU.mult, ALU.add).then_inc(var_done, 1)
                dve.wait_ge(rstd_done, hlf + 1)
                dve.wait_ge(ld_gain, 16)
                for t in range(4 * hlf, 4 * hlf + 4):
                    dve.scalar_tensor_tensor(y[:, t], K.xo[:, t], rstd[:, t:t + 1], gain[:], ALU.mult,
                                             ALU.mult).then_inc(y_done, 1)


def masks():
    t = np.arange(P)
    same = t[:, None] // C == t[None, :] // C
    tri = np.stack([same & (t[:, None] <= t[None, :]), same & (t[:, None] >= t[None, :])], 1)
    trix = np.stack([same & (t[:, None] > t[None, :]), same & (t[:, None] < t[None, :])], 1)
    p, f = (t % C)[:, None], np.arange(C)[None, :]
    neg = np.float32(-1e30)
    valid = np.stack([np.stack([f <= p, f >= p], 1), np.stack([f >= p, f <= p], 1)], 1)
    lev, smask = [], []
    for h in (1, 2, 4, 8, 16, 32):
        block = p // (2 * h) == f // (2 * h)
        up_p, up_f = p % (2 * h) >= h, f % (2 * h) >= h
        lev.append(np.stack([block & up_p & ~up_f, block & ~up_p & up_f], 1))
        smask.append(block & (up_p != up_f))
    smask = [x.astype(np.float32) for x in smask] + [2.0 * (p == f).astype(np.float32)]
    f32 = lambda x: np.ascontiguousarray(x, dtype=np.float32)
    return {"k_ident": np.eye(P, dtype=np.float32), "k_tri": f32(tri), "k_trix": f32(trix),
            "k_negmask": f32(np.where(valid, np.float32(0), neg)),
            "k_levmask": f32(np.stack(lev, 2)), "k_smask": f32(np.stack(smask, 1)),
            "k_ident64": f32(p == f)}


class Kept:
    pass


def hybrid_block(nc, A, out):
    dram = {"k": [NT, P, NH, P], "q": [NT, P, NH, P], "kt": [NT, P, NH, P], "vt": [NT, P, NH, P],
            "ga_k": [NT, P, 2, P], "ga_q": [NT, P, 2, P], "va": [NT, P, V_A], "la": [NT, P, 512],
            "gate": [TL, P, 2 * V_A], "qin": [TL, P, 2, 2, P]}
    S = {n: nc.dram_tensor("s_" + n, s, F32, kind=SCRATCH).ap() for n, s in dram.items()}
    K = Kept()
    with ExitStack() as ctx:
        m = Alloc(nc, ctx)
        K.stored = ctx.enter_context(nc.semaphore("stored"))
        K.ident = m.sb("ident", [P, P])
        K.tri = m.sb("tri", [P, 2, P])
        K.trix = m.sb("trix", [P, 2, P])
        K.negmask = m.sb("negmask", [P, 2, 2, C])
        K.levmask = m.sb("levmask", [P, 2, LEVELS, C])
        K.smask = m.sb("smask", [P, LEVELS + 1, C])
        K.ident64 = m.sb("ident64", [P, C])
        K.ones = m.sb("ones", [P, P])
        K.cols = m.sb("cols", [P, 100])
        K.mod = m.sb("mod", [P, 48, 2])
        K.gdn_la = m.sb("gdn_la", [P, 2, NT, NH])
        K.beta = m.sb("beta", [P, 2, NT, NH])
        with ExitStack() as ctx_h:
            mh = Alloc(nc, ctx_h)
            K.hhi = mh.sb("hhi", [P, KT, NTOK], F32R)
            K.hlo = mh.sb("hlo", [P, KT, NTOK], F32R)
            modulate_phase(nc, A, K, S)
            project_phase(nc, A, K, S)
        K.xo = m.sb("xo", [P, TL, D])
        K.gt2 = m.sb("gt2", [P, D])
        with ExitStack() as ctx_s:
            ms = Alloc(nc, ctx_s)
            K.ga_st = ms.sb("ga_st", [P, 2 * NT + 1, 2, 2, P])
            K.ga_a = ms.sb("ga_a", [P, 2 * NT, 2, 2])
            mix_phase(nc, A, K, S)
            merge_phase(nc, A, K, S)
        mlp_phase(nc, A, K, S, out)
        final_phase(nc, A, K, out)


def kernel(**inputs):
    import concourse.bacc as bacc
    from concourse.bass_utils import run_bass_kernel_spmd

    nc = bacc.Bacc("TRN2", target_bir_lowering=False, num_devices=1)
    arrays = {n: np.ascontiguousarray(a) for n, a in inputs.items()}
    arrays["x"] = arrays["x"].reshape(NLAT, D)
    arrays["ctx"] = arrays["ctx"].reshape(NCTX, D)
    for n in ("w_ada", "w_in", "gla_w_lr", "gla_b_lr", "gdn_a_log", "gdn_dt_bias", "w_out", "w_ff1", "w_ff2"):
        arrays[n] = arrays[n].reshape(arrays[n].shape[1:])
    arrays.update(masks())
    A = {n: nc.dram_tensor("in_" + n, a.shape, F32, kind="ExternalInput").ap() for n, a in arrays.items()}
    out = nc.dram_tensor("out", (NLAT, D), F32, kind="ExternalOutput").ap()
    hybrid_block(nc, A, out)
    got = run_bass_kernel_spmd(nc, [{"in_" + n: a for n, a in arrays.items()}], core_ids=[0])
    res = got.results[0]
    y = res["out"].reshape(1, NLAT, D)
    return y
```

```python
from contextlib import ExitStack

import numpy as np

import concourse.bass as bass
from concourse import mybir

F32 = mybir.dt.float32
F32R = mybir.dt.float32r
ALU = mybir.AluOpType
ACT = mybir.ActivationFunctionType
AX = mybir.AxisListType

P = 128
D = 1024
KT = D // P
NLAT, NCTX = 1024, 256
NTOK = NLAT + NCTX
TL, TC = NLAT // P, NCTX // P
NT = TL + TC
C = 64
NH = 4
GRID_W = 64
EPS = 1e-6
QK_A, V_A = 256, 512
OFF_QA, OFF_KA, OFF_VA, OFF_GA, OFF_R, OFF_QKV, OFF_GB, OFF_AB = 0, 256, 512, 1024, 1536, 1552, 3088, 3600
RANK = 16
LEVELS = 6
NADA = 6 * D
FF = 4 * D
SCRATCH = "Internal"
GLA_SCALE = (QK_A // NH) ** -0.5
GLA_DECAY = 1.0 / 16.0
GDN_SCALE = P ** -0.5
DEBUG = ()


def pos_of(tile):
    return (tile + TC) % NT


class Alloc:

    def __init__(self, nc, ctx, tag=""):
        self.nc, self.ctx, self.tag, self.sems = nc, ctx, tag, []

    def sb(self, name, shape, dt=F32):
        return self.ctx.enter_context(self.nc.sbuf_tensor(name, shape, dt))

    def ps(self, name, shape, dt=F32):
        return self.ctx.enter_context(self.nc.psum_tensor(name, shape, dt))

    def sem(self, name):
        if not self.sems:
            self.ctx.callback(self.clear_sems)
        self.sems.append(self.nc.alloc_semaphore(name=self.tag + name))
        return self.sems[-1]

    def clear_sems(self):
        self.nc.clear_and_free_semaphores(self.sems)
        self.nc.all_engine_barrier()


def mm3(pe, out, lhi, llo, rhi, rlo, start, stop):
    pe.matmul(out, lhi, rhi, start=start, stop=False)
    pe.matmul(out, lhi, rlo, start=False, stop=False)
    return pe.matmul(out, llo, rhi, start=False, stop=stop)


def modulate_phase(nc, A, K, S):
    with ExitStack() as ctx:
        m = Alloc(nc, ctx, "mod_")
        NCH = NADA // 512
        RING = 2
        xs = m.sb("xs", [P, NT, D])
        junk = m.sb("square", [P, D])
        wa = m.sb("wa", [P, RING, KT, 512])
        rows = m.sb("rows", [P, P])
        craw = m.sb("craw", [P, 2, KT])
        csil = m.sb("csil", [P, KT, 2])
        modrow = m.sb("modrow", [2, NADA])
        ss = m.sb("ss", [P, NT])
        var = m.sb("var", [P, NT])
        lnv = m.sb("lnv", [P, NT])
        rstd = m.sb("rstd", [P, NT])
        sc1 = m.sb("sc1", [P, KT, 2])
        hf = m.sb("hf", [P, 3, 512])
        ps_row = m.ps("ps_row", [2, 2, 512])
        ps_mod = m.ps("ps_mod", [P, 512])
        ps_cols = m.ps("ps_cols", [P, 512])
        ps_t = m.ps("ps_t", [P, 4, 512])
        ld_const, ld_rows, ld_c = m.sem("ld_const"), m.sem("ld_rows"), m.sem("ld_c")
        ld_x = [m.sem(f"ld_x{t}") for t in range(NT)]
        ld_w = [m.sem(f"ld_w{r}") for r in range(RING)]
        cols_ready, cols_done = m.sem("cols_ready"), m.sem("cols_done")
        c_silu, row_ready, row_done = m.sem("c_silu"), m.sem("row_ready"), m.sem("row_done")
        mod_ready, mod_done, sc1_done = m.sem("mod_ready"), m.sem("mod_done"), m.sem("sc1_done")
        ss_done, var_done, ln_done, rstd_done = m.sem("ss_done"), m.sem("var_done"), m.sem("ln_done"), m.sem("rstd_done")
        xn_done, t_ready = m.sem("xn_done"), m.sem("t_ready")
        hi_done, hf_done, lo_done = m.sem("hi_done"), m.sem("hf_done"), m.sem("lo_done")
        segs = [(0, 4), (4, 4), (8, 2)]
        units = [(k, s) for s in range(3) for k in range(KT)]
        block = ctx.enter_context(nc.Block())

        @block.sync
        def _(sp):
            sp.dma_start(craw[:, 0, :], A["c"].rearrange("a (p k) -> p (a k)", k=KT)).then_inc(ld_c, 16)
            sp.dma_start(craw[:, 1, :], A["c_ctx"].rearrange("(p k) -> p k", k=KT)).then_inc(ld_c, 16)
            sp.dma_start(K.ident[:], A["k_ident"]).then_inc(ld_const, 16)
            r = 0
            for name, n in (("b_ada", 48), ("norm1_g", 8), ("norm2_g", 8), ("gdn_conv_w", 36)):
                sp.dma_start(rows[r:r + n, :], A[name].rearrange("a n -> (a n)").rearrange("(r p) -> r p", p=P)
                             if len(A[name].shape) == 2 else
                             A[name].rearrange("a w n -> (a w n)").rearrange("(r p) -> r p", p=P)).then_inc(ld_rows, 16)
                r += n
            wv = A["w_ada"].rearrange("(p k) n -> p k n", k=KT)
            xt = [A["x"][t * P:(t + 1) * P, :] for t in range(TL)] + [A["ctx"][t * P:(t + 1) * P, :] for t in range(TC)]
            for n in range(NCH):
                if n >= RING:
                    sp.wait_ge(row_ready, n - RING + 1)
                sp.dma_start(wa[:, n % RING], wv[:, :, n * 512:(n + 1) * 512]).then_inc(ld_w[n % RING], 16)
                for t in range(4 * n, min(4 * n + 4, NT)):
                    sp.dma_start(xs[:, t], xt[t]).then_inc(ld_x[t], 16)

        @block.scalar
        def _(act):
            act.wait_ge(ld_c, 32)
            act.activation(csil[:].rearrange("p k v -> p v k"), craw[:], ACT.Silu).then_inc(c_silu, 1)
            for t in range(NT):
                act.wait_ge(ld_x[t], 16)
                if t:
                    act.wait_ge(ss_done, t)
                act.activation(junk[:], xs[:, t], ACT.Square, accum_out=ss[:, t:t + 1]).then_inc(ss_done, 1)
            act.wait_ge(var_done, 1)
            act.activation(lnv[:], var[:], ACT.Ln).then_inc(ln_done, 1)
            act.wait_ge(ln_done, 1)
            act.activation(rstd[:], lnv[:], ACT.Exp, scale=-0.5).then_inc(rstd_done, 1)
            for u, (k, s) in enumerate(units):
                t0, n = segs[s]
                act.wait_ge(hf_done, u + 1)
                act.activation(K.hhi[:, k, t0 * P:(t0 + n) * P], hf[:, u % 3, :n * P], ACT.Copy).then_inc(hi_done, 1)

        @block.vector
        def _(dve):
            dve.wait_ge(cols_ready, 1)
            dve.tensor_copy(K.cols[:], ps_cols[:, :100]).then_inc(cols_done, 1)
            for n in range(NCH):
                dve.wait_ge(row_ready, n + 1)
                dve.tensor_copy(modrow[:, n * 512:(n + 1) * 512], ps_row[:, n % 2]).then_inc(row_done, 1)
                if n == 2:
                    dve.wait_ge(ss_done, NT)
                    dve.tensor_scalar(var[:], ss[:], 1.0 / D, EPS, ALU.mult, ALU.add).then_inc(var_done, 1)
                    dve.wait_ge(rstd_done, 1)
                    for t in range(NT):
                        dve.tensor_scalar(xs[:, t], xs[:, t], rstd[:, t:t + 1], None, ALU.mult).then_inc(xn_done, 1)
            dve.wait_ge(mod_ready, 1)
            dve.wait_ge(cols_done, 1)
            dve.tensor_tensor(K.mod[:], ps_mod[:, :96].rearrange("p (j v) -> p j v", v=2),
                              K.cols[:, 0:48].unsqueeze(2).broadcast_to([P, 48, 2]), ALU.add).then_inc(mod_done, 1)
            dve.wait_ge(mod_done, 1)
            dve.tensor_scalar(sc1[:], K.mod[:, 8:16], 1.0, None, ALU.add).then_inc(sc1_done, 1)
            dve.wait_ge(sc1_done, 1)
            dve.tensor_tensor(sc1[:], sc1[:], K.cols[:, 48:56].unsqueeze(2).broadcast_to([P, KT, 2]),
                              ALU.mult).then_inc(sc1_done, 1)
            dve.wait_ge(sc1_done, 2)
            for u, (k, s) in enumerate(units):
                t0, n = segs[s]
                v = int(s == 2)
                dve.wait_ge(t_ready, u + 1)
                if u >= 3:
                    dve.wait_ge(lo_done, u - 2)
                dve.tensor_scalar(hf[:, u % 3, :n * P], ps_t[:, u % 4, :n * P], sc1[:, k, v:v + 1],
                                  K.mod[:, k, v:v + 1], ALU.mult, ALU.add).then_inc(hf_done, 1)

        @block.gpsimd
        def _(pool):
            pool.memset(K.ones[:], 1.0)
            for u, (k, s) in enumerate(units):
                t0, n = segs[s]
                pool.wait_ge(hi_done, u + 1)
                pool.tensor_tensor(K.hlo[:, k, t0 * P:(t0 + n) * P], hf[:, u % 3, :n * P],
                                   K.hhi[:, k, t0 * P:(t0 + n) * P].bitcast(F32), ALU.subtract).then_inc(lo_done, 1)

        @block.tensor
        def _(pe):
            pe.wait_ge(ld_const, 16)
            pe.wait_ge(ld_rows, 4 * 16)
            pe.transpose(ps_cols[:, :100], rows[:100, :], K.ident[:100, :100]).then_inc(cols_ready, 1)
            pe.wait_ge(c_silu, 1)
            for n in range(NCH):
                pe.wait_ge(ld_w[n % RING], 16 * (n // RING + 1))
                if n >= 2:
                    pe.wait_ge(row_done, n - 1)
                for k in range(KT):
                    last = pe.matmul(ps_row[:, n % 2], csil[:, k, :], wa[:, n % RING, k, :],
                                     start=(k == 0), stop=(k == KT - 1))
                last.then_inc(row_ready, 1)
            pe.wait_ge(row_done, NCH)
            for j in range(48):
                last = pe.transpose(ps_mod[:, 2 * j:2 * j + 2], modrow[:, j * P:(j + 1) * P], K.ident[0:2, 0:2])
            last.then_inc(mod_ready, 1)
            for u, (k, s) in enumerate(units):
                t0, n = segs[s]
                pe.wait_ge(xn_done, t0 + n)
                if u >= 4:
                    pe.wait_ge(hf_done, u - 3)
                for i in range(n):
                    last = pe.transpose(ps_t[:, u % 4, i * P:(i + 1) * P], xs[:, t0 + i, k * P:(k + 1) * P], K.ident[:])
                last.then_inc(t_ready, 1)


def project_phase(nc, A, K, S):
    with ExitStack() as ctx:
        m = Alloc(nc, ctx, "proj_")
        W = 256
        UNITS = [("small", 0, 32, 0),
                 ("k", OFF_QKV + 512, W, 0), ("k", OFF_QKV + 768, W, 2),
                 ("v", OFF_QKV + 1024, W, 0), ("v", OFF_QKV + 1280, W, 2),
                 ("q", OFF_QKV, W, 0), ("q", OFF_QKV + 256, W, 2),
                 ("ka", OFF_KA, W, 0), ("qa", OFF_QA, W, 0),
                 ("va", OFF_VA, W, 0), ("va", OFF_VA + W, W, 2),
                 ("gate", OFF_GA, W, 0), ("gate", OFF_GA + W, W, 1),
                 ("gate", OFF_GB, W, 2), ("gate", OFF_GB + W, W, 3)]
        NU = len(UNITS)
        raw = m.sb("raw", [P, 2, KT, W])
        whi = m.sb("whi", [P, 2, KT, W], F32R)
        wlo = m.sb("wlo", [P, 2, KT, W], F32R)
        u_sb = m.sb("u_sb", [P, NTOK])
        y_sb = m.sb("y_sb", [P, NTOK])
        z_sb = m.sb("z_sb", [P, 2, NTOK])
        sq_sb = m.sb("sq_sb", [P, NTOK])
        n_sb = m.sb("n_sb", [P, 2, NTOK])
        tok_sb = m.sb("tok_sb", [P, NT, P])
        a_sb = m.sb("a_sb", [P, NTOK])
        t_sb = m.sb("t_sb", [P, 4, W])
        small = m.sb("small", [P, NT, 32])
        eps = m.sb("eps", [P, 1])
        wlr = m.sb("wlr", [RANK + 1, 512])
        raT = m.sb("raT", [32, NTOK])
        lr_e = m.sb("lr_e", [P, 512])
        lr_x = m.sb("lr_x", [P, 2, 512])
        alog = m.sb("alog", [P, 8])
        dtb = m.sb("dtb", [P, 8])
        nea = m.sb("nea", [P, 8])
        za = m.sb("za", [P, NT, 8])
        zb = m.sb("zb", [P, NT, 8])
        zc = m.sb("zc", [P, NT, 8])
        ps_main = m.ps("ps_main", [P, 3, 512])
        ps_sq = m.ps("ps_sq", [P, 3, 512])
        ps_tr = m.ps("ps_tr", [P, 2, 512])
        ld_w = [m.sem("ld_w0"), m.sem("ld_w1")]
        ld_s = m.sem("ld_s")
        hi_done, lo_done = m.sem("p_hi_done"), m.sem("p_lo_done")
        main_ready, main_out = m.sem("main_ready"), m.sem("main_out")
        conv_done, z_done, sq_done = m.sem("conv_done"), m.sem("z_done"), m.sem("sq_done")
        ss_ready, lnss_done, rs_done, n_done = m.sem("ss_ready"), m.sem("lnss_done"), m.sem("rs_done"), m.sem("n_done")
        tr_ready, tr_out = m.sem("tr_ready"), m.sem("tr_out")
        st_n = [m.sem("st_n0"), m.sem("st_n1")]
        st_tok, st_a = m.sem("st_tok"), m.sem("st_a")
        st_t = [m.sem(f"st_t{i}") for i in range(4)]
        conv_step = m.sem("conv_step")
        init_done, rt_ready, rt_out = m.sem("init_done"), m.sem("rt_ready"), m.sem("rt_out")
        lr_abs, lr_exp, lr_ln, lr_done = m.sem("lr_abs"), m.sem("lr_exp"), m.sem("lr_ln"), m.sem("lr_done")
        st_lr = [m.sem("st_lr0"), m.sem("st_lr1")]
        ab_act, ab_dve = m.sem("ab_act"), m.sem("ab_dve")
        SEG = [(0, 512), (512, 512), (1024, 256)]

        outs = []
        for u, (kind, _, width, h0) in enumerate(UNITS):
            if kind in ("k", "v", "q", "ka", "qa"):
                for j in range(2):
                    for s in range(2 if kind in ("q", "qa") else 3):
                        outs.append((u, kind, j, s))
                        n_lr = sum(o[1] == "lr" for o in outs)
                        if n_lr < NT:
                            outs.append((u, "lr", n_lr, 0))
            else:
                for t in range(TL if kind == "gate" else NT):
                    outs.append((u, kind, t, 0))
        out_by = {}
        for i, (u, kind, j, _) in enumerate(outs):
            out_by[(u, kind, j)] = i + 1
            out_by[u] = i + 1
        conv_tiles = [(u, j) for u, un in enumerate(UNITS) if un[0] in ("k", "v", "q") for j in range(2)]
        conv_no = {x: i for i, x in enumerate(conv_tiles)}
        kinds = [UNITS[u][0] for u, _ in conv_tiles]

        def n_norm(i):
            return sum(k != "v" for k in kinds[:i])

        def n_turn(i):
            return sum(k != "q" for k in kinds[:i])

        NTR = 3

        block = ctx.enter_context(nc.Block())

        def turned_store(i):
            u, j = conv_tiles[i]
            return (S["kt"] if kinds[i] == "k" else S["vt"]), UNITS[u][3] + j

        @block.sync
        def _(sp):
            wv = A["w_in"].rearrange("(k p) n -> p k n", p=P)
            sp.dma_start(wlr[0:RANK, :], A["gla_w_lr"].rearrange("z r n -> r z n")).then_inc(ld_s, 16)
            sp.dma_start(wlr[RANK:RANK + 1, :], A["gla_b_lr"].rearrange("(a z) n -> a (z n)", a=1)).then_inc(ld_s, 16)
            sp.dma_start(alog[:], A["gdn_a_log"].rearrange("z h -> (z h)").partition_broadcast(P)).then_inc(ld_s, 16)
            sp.dma_start(dtb[:], A["gdn_dt_bias"].rearrange("z h -> (z h)").partition_broadcast(P)).then_inc(ld_s, 16)

            def load_unit(u):
                kind, col, width, _ = UNITS[u]
                if u >= 2:
                    sp.wait_ge(lo_done, u - 1)
                if kind == "small":
                    sp.dma_start(raw[:, u % 2, :, 0:16], wv[:, :, OFF_R:OFF_R + 16]).then_inc(ld_w[u % 2], 16)
                    sp.dma_start(raw[:, u % 2, :, 16:32], wv[:, :, OFF_AB:OFF_AB + 16]).then_inc(ld_w[u % 2], 16)
                else:
                    sp.dma_start(raw[:, u % 2], wv[:, :, col:col + width]).then_inc(ld_w[u % 2], 16)

            for u in range(NU):
                load_unit(u)

        @block.gpsimd
        def _(pool):
            pool.memset(eps[:], EPS).then_inc(init_done, 1)
            pool.memset(raT[:], 1.0).then_inc(init_done, 1)
            def store_conv(i):
                u, j = conv_tiles[i]
                head = UNITS[u][3] + j
                if kinds[i] != "v":
                    n = n_norm(i)
                    pool.wait_ge(n_done, n + 1)
                    dst = S["k"] if kinds[i] == "k" else S["q"]
                    pool.dma_start(dst[TC:NT, :, head, :].rearrange("t p n -> p t n"),
                                   n_sb[:, n % 2, :NLAT].rearrange("p (t n) -> p t n", n=P)).then_inc(st_n[n % 2], 16)
                    if kinds[i] == "k":
                        pool.dma_start(dst[0:TC, :, head, :].rearrange("t p n -> p t n"),
                                       n_sb[:, n % 2, NLAT:].rearrange("p (t n) -> p t n", n=P)).then_inc(st_n[n % 2], 16)
                if kinds[i] != "q":
                    dst, head = turned_store(i)
                    n = n_turn(i)
                    pool.wait_ge(tr_out, NTR * (n + 1))
                    pool.dma_start(dst[TC:NT, :, head, :].rearrange("t p n -> p t n"),
                                   tok_sb[:, 0:TL, :]).then_inc(st_tok, 16)
                    pool.dma_start(dst[0:TC, :, head, :].rearrange("t p n -> p t n"),
                                   tok_sb[:, TL:NT, :]).then_inc(st_tok, 16)

            for t in range(NT):
                pool.wait_ge(lr_done, t + 1)
                pool.dma_start(S["la"][pos_of(t)], lr_x[:, t % 2]).then_inc(st_lr[t % 2], 16)
                if t == 4:
                    store_conv(0)
                if t == 7:
                    store_conv(1)
            for i in range(2, len(conv_tiles)):
                store_conv(i)
            for u, (kind, _, _, h0) in enumerate(UNITS):
                if kind in ("ka", "qa"):
                    for j in range(2):
                        pool.wait_ge(main_out, out_by[(u, kind, j)])
                        dst = S["ga_k"] if kind == "ka" else S["ga_q"]
                        pool.dma_start(dst[TC:NT, :, j, :].rearrange("t p n -> p t n"),
                                       a_sb[:, :NLAT].rearrange("p (t n) -> p t n", n=P)).then_inc(st_a, 16)
                        if kind == "ka":
                            pool.dma_start(dst[0:TC, :, j, :].rearrange("t p n -> p t n"),
                                           a_sb[:, NLAT:].rearrange("p (t n) -> p t n", n=P)).then_inc(st_a, 16)
            nt = 0
            for u, (kind, _, _, h0) in enumerate(UNITS):
                if kind in ("va", "gate"):
                    for t in range(TL if kind == "gate" else NT):
                        pool.wait_ge(main_out, out_by[(u, kind, t)])
                        dst = (S["va"][pos_of(t), :, h0 * P:h0 * P + W] if kind == "va"
                               else S["gate"][t, :, h0 * W:(h0 + 1) * W])
                        pool.dma_start(dst, t_sb[:, nt % 4]).then_inc(st_t[nt % 4], 16)
                        nt += 1
            for s, n in ((st_n[0], 4 * 16 + 2 * 16), (st_n[1], 4 * 16 + 2 * 16), (st_tok, 16 * 16), (st_lr[0], 80),
                         (st_lr[1], 80), (st_a, 96)):
                pool.wait_ge(s, n)
            for i in range(4):
                pool.wait_ge(st_t[i], 16 * ((nt + 3 - i) // 4))

        def stored_n(n):
            nk = 4
            return 16 * sum(2 if i < nk else 1 for i in range(n % 2, n - 1, 2))

        @block.scalar
        def _(act):
            def split(u):
                act.wait_ge(ld_w[u % 2], 16 * (u // 2 + 1) + (16 if u % 2 == 0 else 0))
                if u >= 2:
                    act.wait_ge(main_ready, out_by[u - 2])
                w = UNITS[u][2]
                act.activation(whi[:, u % 2, :, :w], raw[:, u % 2, :, :w], ACT.Copy).then_inc(hi_done, 1)

            def finish_conv(i):
                kind = kinds[i]
                act.wait_ge(conv_done, i + 1)
                if i >= 2:
                    act.wait_ge(n_done, n_norm(i - 1))
                    if n_turn(i - 1):
                        act.wait_ge(tr_ready, NTR * n_turn(i - 1))
                n = NLAT if kind == "q" else NTOK
                act.activation(z_sb[:, i % 2, :n], y_sb[:, :n], ACT.Silu).then_inc(z_done, 1)
                if kind != "v":
                    act.wait_ge(z_done, i + 1)
                    if n_norm(i):
                        act.wait_ge(ss_ready, n_norm(i))
                        act.wait_ge(n_done, n_norm(i))
                    act.activation(sq_sb[:, :n], z_sb[:, i % 2, :n], ACT.Square).then_inc(sq_done, 1)

            def finish_norm(i):
                kind = kinds[i]
                if kind == "v":
                    return
                k = n_norm(i)
                n = NLAT if kind == "q" else NTOK
                act.wait_ge(ss_ready, k + 1)
                act.activation(sq_sb[:, :n], ps_sq[:, :, :].rearrange("p s n -> p (s n)")[:, :n], ACT.Ln,
                               bias=eps[:]).then_inc(lnss_done, 1)
                act.wait_ge(lnss_done, k + 1)
                act.activation(sq_sb[:, :n], sq_sb[:, :n], ACT.Exp, scale=-0.5).then_inc(rs_done, 1)

            act.wait_ge(init_done, 2)
            split(0)
            split(1)
            na = nt = 0
            for i, (u, kind, j, s) in enumerate(outs):
                act.wait_ge(main_ready, i + 1)
                if kind == "small":
                    act.activation(small[:, j, :], ps_main[:, i % 3, :32], ACT.Copy).then_inc(main_out, 1)
                    if j == NT - 1:
                        act.wait_ge(ab_dve, 1)
                        act.activation(zb[:], za[:], ACT.Abs).then_inc(ab_act, 1)
                        act.activation(nea[:], alog[:], ACT.Exp).then_inc(ab_act, 1)
                        act.wait_ge(ab_act, 2)
                        act.activation(zb[:], zb[:], ACT.Exp, scale=-1.0).then_inc(ab_act, 1)
                        act.wait_ge(ab_act, 3)
                        act.activation(zb[:], zb[:], ACT.Ln, bias=1.0).then_inc(ab_act, 1)
                        act.activation(zc[:], small[:, :, 24:32], ACT.Exp, scale=-1.0).then_inc(ab_act, 1)
                elif kind == "lr":
                    if j >= 2:
                        act.wait_ge(st_lr[j % 2], 16 * (j // 2))
                    act.activation(lr_x[:, j % 2], ps_main[:, i % 3, :], ACT.Copy).then_inc(main_out, 1)
                    act.wait_ge(main_out, i + 1)
                    if j:
                        act.wait_ge(lr_done, j)
                    act.activation(lr_e[:], lr_x[:, j % 2], ACT.Abs).then_inc(lr_abs, 1)
                    act.wait_ge(lr_abs, j + 1)
                    act.activation(lr_e[:], lr_e[:], ACT.Exp, scale=-1.0).then_inc(lr_exp, 1)
                    act.wait_ge(lr_exp, j + 1)
                    act.activation(lr_e[:], lr_e[:], ACT.Ln, bias=1.0).then_inc(lr_ln, 1)
                elif kind in ("k", "v", "q"):
                    cn = conv_no[(u, j)]
                    t0, n = SEG[s]
                    if s == 0 and cn >= 1:
                        act.wait_ge(conv_done, cn)
                    act.activation(u_sb[:, t0:t0 + n], ps_main[:, i % 3, :n], ACT.Copy).then_inc(main_out, 1)
                    if s == 0 and cn >= 1:
                        finish_norm(cn - 1)
                    if s == (1 if kind == "q" else 2):
                        finish_conv(cn)
                elif kind in ("ka", "qa"):
                    t0, n = SEG[s]
                    if s == 0 and na >= 1:
                        act.wait_ge(st_a, (0, 32, 64, 80)[na])
                    act.activation(a_sb[:, t0:t0 + n], ps_main[:, i % 3, :n], ACT.Copy,
                                   scale=(GLA_SCALE if kind == "qa" else 1.0)).then_inc(main_out, 1)
                    if na == 0 and s == 0:
                        finish_norm(len(conv_tiles) - 1)
                    if s == (1 if kind == "qa" else 2):
                        na += 1
                else:
                    if nt >= 4:
                        act.wait_ge(st_t[nt % 4], 16 * (nt // 4))
                    act.activation(t_sb[:, nt % 4], ps_main[:, i % 3, :W],
                                   ACT.Silu if kind == "gate" else ACT.Copy).then_inc(main_out, 1)
                    nt += 1
                if u >= 1 and i + 1 == out_by[u - 1] + 1 and u + 1 < NU:
                    split(u + 1)

        @block.vector
        def _(dve):
            step = [0]

            def then_step(ins):
                step[0] += 1
                ins.then_inc(conv_step, 1)
                dve.wait_ge(conv_step, step[0])

            def split(u):
                dve.wait_ge(hi_done, u + 1)
                w = UNITS[u][2]
                dve.tensor_tensor(wlo[:, u % 2, :, :w], raw[:, u % 2, :, :w], whi[:, u % 2, :, :w].bitcast(F32),
                                  ALU.subtract).then_inc(lo_done, 1)

            def conv(cn):
                u, j = conv_tiles[cn]
                kind = kinds[cn]
                dve.wait_ge(main_out, out_by[(u, kind, j)])
                if cn >= 1:
                    dve.wait_ge(z_done, cn)
                ch = {"q": 0, "k": 4, "v": 8}[kind] + UNITS[u][3] + j
                w = [K.cols[:, 64 + tap * 12 + ch:65 + tap * 12 + ch] for tap in range(3)]
                n = NLAT if kind == "q" else NTOK
                then_step(dve.tensor_scalar(y_sb[:, :n], u_sb[:, :n], w[1], None, ALU.mult))
                for lo, hi, row in ((0, NLAT, GRID_W), (NLAT, NTOK, NCTX)):
                    if lo >= n:
                        continue
                    uu = u_sb[:, lo:hi].rearrange("p (r w) -> p r w", w=row)
                    yy = y_sb[:, lo:hi].rearrange("p (r w) -> p r w", w=row)
                    then_step(dve.scalar_tensor_tensor(yy[:, :, 1:], uu[:, :, :row - 1], w[0], yy[:, :, 1:],
                                                       ALU.mult, ALU.add))
                    last = dve.scalar_tensor_tensor(yy[:, :, :row - 1], uu[:, :, 1:], w[2], yy[:, :, :row - 1],
                                                    ALU.mult, ALU.add)
                    if hi < n:
                        then_step(last)
                last.then_inc(conv_done, 1)

            def norm(cn):
                kind = kinds[cn]
                if kind == "v":
                    return
                k = n_norm(cn)
                n = NLAT if kind == "q" else NTOK
                dve.wait_ge(rs_done, k + 1)
                if k >= 2:
                    dve.wait_ge(st_n[k % 2], stored_n(k))
                if 2 <= k < 6:
                    dve.wait_ge(tr_ready, NTR * (k - 1))
                dve.scalar_tensor_tensor(n_sb[:, k % 2, :n], z_sb[:, cn % 2, :n], GDN_SCALE if kind == "q" else 1.0,
                                         sq_sb[:, :n], ALU.mult, ALU.mult).then_inc(n_done, 1)

            def turn_out(cn):
                if kinds[cn] == "q":
                    return
                k = n_turn(cn)
                if k:
                    dve.wait_ge(st_tok, 32 * k)
                for r, (t0, n) in enumerate(((0, 4), (4, 4), (8, 2))):
                    f = NTR * k + r
                    dve.wait_ge(tr_ready, f + 1)
                    dve.tensor_copy(tok_sb[:, t0:t0 + n, :].rearrange("p t n -> p (t n)"),
                                    ps_tr[:, f % 2, :n * P]).then_inc(tr_out, 1)

            dve.wait_ge(init_done, 2)
            split(0)
            split(1)
            for r, (t0, n) in enumerate(SEG):
                dve.wait_ge(rt_ready, r + 1)
                dve.tensor_copy(raT[0:RANK, t0:t0 + n], ps_sq[0:RANK, r, :n]).then_inc(rt_out, 1)
            dve.wait_ge(ld_s, 64)
            dve.wait_ge(main_out, NT)
            dve.tensor_tensor(za[:], small[:, :, 16:24], dtb[:].unsqueeze(1).broadcast_to([P, NT, 8]),
                              ALU.add).then_inc(ab_dve, 1)
            dve.wait_ge(ab_act, 4)
            dve.wait_ge(ab_dve, 1)
            then_step(dve.scalar_tensor_tensor(za[:], za[:], 0.0, zb[:], ALU.max, ALU.add))
            then_step(dve.scalar_tensor_tensor(za[:], za[:], -1.0, nea[:].unsqueeze(1).broadcast_to([P, NT, 8]),
                                               ALU.mult, ALU.mult))
            for t in range(NT):
                dve.tensor_copy(K.gdn_la[:, :, pos_of(t), :], za[:, t, :].rearrange("p (z h) -> p z h", z=2))
            dve.wait_ge(ab_act, 5)
            then_step(dve.tensor_scalar(zc[:], zc[:], 1.0, None, ALU.add))
            then_step(dve.reciprocal(zc[:], zc[:]))
            for t in range(NT):
                dve.tensor_copy(K.beta[:, :, pos_of(t), :], zc[:, t, :].rearrange("p (z h) -> p z h", z=2))
            for i, (u, kind, j, s) in enumerate(outs):
                if kind == "lr":
                    dve.wait_ge(lr_ln, j + 1)
                    dve.scalar_tensor_tensor(lr_x[:, j % 2], lr_x[:, j % 2], 0.0, lr_e[:],
                                             ALU.min, ALU.subtract).then_inc(lr_done, 1)
                if (u, j) in conv_no and kind != "lr" and i + 1 == out_by[(u, kind, j)]:
                    cn = conv_no[(u, j)]
                    if cn >= 1:
                        norm(cn - 1)
                    conv(cn)
                    if cn >= 1:
                        turn_out(cn - 1)
                if kind == "ka" and j == 0 and s == 0:
                    norm(len(conv_tiles) - 1)
                if u >= 1 and i + 1 == out_by[u - 1] + 1 and u + 1 < NU:
                    split(u + 1)

        @block.tensor
        def _(pe):
            pe.wait_ge(init_done, 2)

            def ranks():
                for r, (t0, n) in enumerate(SEG):
                    pe.wait_ge(main_out, (t0 + n) // P)
                    for i in range(n // P):
                        last = pe.transpose(ps_sq[0:RANK, r, i * P:(i + 1) * P], small[:, t0 // P + i, 0:RANK], K.ident[:])
                    last.then_inc(rt_ready, 1)

            def sums(cn):
                if kinds[cn] == "v":
                    return
                k = n_norm(cn)
                pe.wait_ge(sq_done, k + 1)
                if k:
                    pe.wait_ge(lnss_done, k)
                else:
                    pe.wait_ge(rt_out, 3)
                for s in range(2 if kinds[cn] == "q" else 3):
                    t0, n = SEG[s]
                    last = pe.matmul(ps_sq[:, s, :n], K.ones[:], sq_sb[:, t0:t0 + n], start=True, stop=True)
                last.then_inc(ss_ready, 1)

            def turn(cn):
                if kinds[cn] == "q":
                    return
                k = n_turn(cn)
                if kinds[cn] == "k":
                    pe.wait_ge(n_done, n_norm(cn) + 1)
                    src = n_sb[:, n_norm(cn) % 2]
                else:
                    pe.wait_ge(z_done, cn + 1)
                    src = z_sb[:, cn % 2]
                for r, (t0, n) in enumerate(((0, 4), (4, 4), (8, 2))):
                    f = NTR * k + r
                    if f >= 2:
                        pe.wait_ge(tr_out, f - 1)
                    for i in range(n):
                        last = pe.transpose(ps_tr[:, f % 2, i * P:(i + 1) * P], src[:, (t0 + i) * P:(t0 + i + 1) * P],
                                            K.ident[:])
                    last.then_inc(tr_ready, 1)

            for i, (u, kind, j, s) in enumerate(outs):
                b, width = u % 2, UNITS[u][2]
                pe.wait_ge(lo_done, u + 1)
                if i >= 3:
                    pe.wait_ge(main_out, i - 2)
                if kind == "lr":
                    if j == 0:
                        pe.wait_ge(rt_out, 3)
                        pe.wait_ge(ld_s, 64)
                    pe.matmul(ps_main[:, i % 3, :], raT[0:RANK + 1, j * P:(j + 1) * P], wlr[:], start=True,
                              stop=True).then_inc(main_ready, 1)
                elif kind in ("small", "va", "gate"):
                    ts = slice(j * P, (j + 1) * P)
                    for k in range(KT):
                        last = mm3(pe, ps_main[:, i % 3, :width], K.hhi[:, k, ts], K.hlo[:, k, ts],
                                   whi[:, b, k, :width], wlo[:, b, k, :width], k == 0, k == KT - 1)
                    last.then_inc(main_ready, 1)
                    if kind == "small" and j == NT - 1:
                        ranks()
                else:
                    t0, n = SEG[s]
                    cs = slice(j * P, (j + 1) * P)
                    for k in range(KT):
                        last = mm3(pe, ps_main[:, i % 3, :n], whi[:, b, k, cs], wlo[:, b, k, cs],
                                   K.hhi[:, k, t0:t0 + n], K.hlo[:, k, t0:t0 + n], k == 0, k == KT - 1)
                    last.then_inc(main_ready, 1)
                    cn = conv_no.get((u, j), len(conv_tiles) if (kind, j) == ("ka", 0) else 0)
                    if cn >= 1 and s == 0:
                        sums(cn - 1)
                    if cn >= 1 and s == (1 if kind == "q" else 2):
                        turn(cn - 1)


def mix_phase(nc, A, K, S):
    LAST_LEVEL = LEVELS - 1
    SM_STEPS = 5
    with ExitStack() as ctx:
        m = Alloc(nc, ctx, "mix_")
        R2 = range(2)
        both = lambda name, shape: [m.sb(f"{name}{d}", shape) for d in R2]
        tri, trix = m.sb("tri", [P, 2, P]), m.sb("trix", [P, 2, P])
        negmask, levmask = m.sb("negmask", [P, 2, 2, P]), m.sb("levmask", [P, 2, LEVELS, P])
        smask = m.sb("smask", [P, LEVELS + 1, C])
        kc, qc = both("kc", [P, NH, P]), both("qc", [P, NH, P])
        kt, vt = both("kt", [P, NH, P]), both("vt", [P, NH, P])
        coef = both("coef", [P, 5, NH])
        rows = both("rows", [P, 2, NH, C])
        lmat = both("lmat", [P, NH, P])
        dec = both("dec", [P, 2, NH, P])
        xx = both("xx", [P, 2, NH, P])
        yy = both("yy", [P, NH, P])
        atp = both("atp", [P, NH, P])
        bv, bk, kd, qd = (both(n, [P, NH, P]) for n in ("bv", "bk", "kd", "qd"))
        wtn, delta = both("wtn", [P, NH, P]), both("delta", [P, NH, P])
        st, sta = both("st", [P, NH, P]), both("sta", [P, NH, P])
        sm = m.sb("sm", [P, 2, NT, 5, NH])
        gqk = m.sb("gqk", [P, 2, 2, P])
        gva, gla = m.sb("gva", [P, NH, P]), m.sb("gla", [P, 512])
        bs = m.sb("bs", [P, 2, 2, P])
        wl = m.sb("wl", [P, LEVELS, 2, 2, P])
        kin, qin = m.sb("kin", [P, 2, 2, P]), m.sb("qin", [P, 2, 2, P])
        msc = m.sb("msc", [P, 2, LEVELS + 1, C])
        atg = m.sb("atg", [P, NH, P])
        kint = m.sb("kint", [P, 2, 2, P])
        pa = [m.ps(f"pa{d}", [P, 512]) for d in R2]
        pb = [m.ps(f"pb{d}", [P, 512]) for d in R2]
        pc = [m.ps(f"pc{d}", [P, 512]) for d in R2]
        px = [m.ps(f"px{d}", [P, 512]) for d in R2]

        ld_mask, ld_la, scan = m.sem("ld_mask"), m.sem("ld_la"), m.sem("gla_scan")
        two = lambda name: [m.sem(f"{name}{d}") for d in R2]
        init_done, g_ready, sm_step = m.sem("mx_init"), m.sem("g_ready"), m.sem("sm_step")
        ld_k, ld_q, ld_t = two("ld_k"), two("ld_q"), two("ld_t")
        coef_done, tri_la_done = two("coef_done"), two("tri_la_done")
        gr_ready, kq_ready = two("gr_ready"), two("kq_ready")
        diff_done, dec_in, dec_done, eg_done = two("diff_done"), two("dec_in"), two("dec_done"), two("eg_done")
        kkd_done, l_done, at_done = two("kkd_done"), two("l_done"), two("at_done")
        lt_ready, y_ready, y_done, p_ready, pt_ready = (two("lt_ready"), two("y_ready"), two("y_done"),
                                                        two("p_ready"), two("pt_ready"))
        x0_step, xt_done, x_done = two("x0_step"), two("xt_done"), two("x_done")
        scaled_done, qd_done = two("scaled_done"), two("qd_done")
        uw_ready, wt_done, ws_ready, delta_done = two("uw_ready"), two("wt_done"), two("ws_ready"), two("delta_done")
        ds_ready, sta_done, st_done = two("ds_ready"), two("sta_done"), two("st_done")
        o_ready, o_done = two("o_ready"), two("o_done")
        ld_g, ld_gq, st_qin, qin_done = m.sem("ld_g"), m.sem("ld_gq"), m.sem("st_qin"), m.sem("qin_done")
        b_ready, b_done, sub_done, exp_done = m.sem("b_ready"), m.sem("b_done"), m.sem("sub_done"), m.sem("exp_done")
        kin_exp, wl_exp = m.sem("kin_exp"), m.sem("wl_exp")
        wl_done, io_done = m.sem("wl_done"), m.sem("io_done")
        sc_ready, msc_done, atg_done = m.sem("sc_ready"), m.sem("msc_done"), m.sem("atg_done")
        kt_ready, kt_out, gs_ready, gs_out = m.sem("kt_ready"), m.sem("kt_out"), m.sem("gs_ready"), m.sem("gs_out")
        og_ready, og_out = m.sem("og_ready"), m.sem("og_out")

        def after(eng, sem, n):
            if not isinstance(n, int) or n > 0:
                eng.wait_ge(sem, n)

        def pos(d, s, lat):
            if d == 0:
                return s
            return 11 - s if lat else 1 - s

        def steps(eng, body):
            body(0, False)
            body(1, False)
            for i in range(TL):
                body(i + TC, True)

        def chunk_order(d):
            return ((0, 1), (1, 0))[d]

        half = lambda c: slice(c * C, (c + 1) * C)
        block = ctx.enter_context(nc.Block())

        @block.sync
        def _(sp):
            for dst, n in ((tri, "k_tri"), (trix, "k_trix"), (negmask, "k_negmask"), (levmask, "k_levmask"), (smask, "k_smask")):
                sp.dma_start(dst[:], A[n]).then_inc(ld_mask, 16)

            def step(s, lat):
                after(sp, b_ready, s)
                sp.dma_start(gla[:], S["la"][s]).then_inc(ld_la, 16)
                for d in R2:
                    p = pos(d, s, lat)
                    after(sp, kq_ready[d], s)
                    sp.dma_start(kc[d][:], S["k"][p]).then_inc(ld_k[d], 16)
                    if lat:
                        sp.wait_ge(sta_done[d], 2 * s)
                        sp.dma_start(qc[d][:], S["q"][p]).then_inc(ld_q[d], 16)
                    if not isinstance(s, int) or s > 0:
                        sp.wait_ge(scaled_done[d], s * 3)
                    sp.dma_start(kt[d][:], S["kt"][p]).then_inc(ld_t[d], 16)
                    sp.dma_start(vt[d][:], S["vt"][p]).then_inc(ld_t[d], 16)
                    if d == 0:
                        after(sp, gs_ready, 2 * s)
                        if lat:
                            sp.wait_ge(og_out, s - TC + 1)
                        sp.dma_start(gqk[:, 1], S["ga_k"][s]).then_inc(ld_g, 16)
                        sp.dma_start(gva[:], S["va"][s].rearrange("p (h n) -> p h n", h=NH)).then_inc(ld_g, 16)
                        if lat:
                            sp.dma_start(gqk[:, 0], S["ga_q"][s]).then_inc(ld_gq, 16)
                if lat:
                    sp.wait_ge(qin_done, s - TC + 1)
                    sp.dma_start(S["qin"][s - TC], qin[:]).then_inc(st_qin, 16)
            sp.sem_inc(st_qin, 16)
            steps(sp, step)
            sp.wait_ge(st_qin, 16 * (TL + 1))

        @block.gpsimd
        def _(pool):
            for d in R2:
                pool.memset(st[d][:], 0.0)
            pool.memset(K.xo[:, :, V_A:], 0.0)
            pool.memset(atg[:], 0.0).then_inc(init_done, 1)

            pool.wait_ge(ld_mask, 5 * 16)

            def step(s, lat):
                for d in R2:
                    after(pool, l_done[d], s)
                    after(pool, diff_done[d], s)
                    if isinstance(s, int) and s == 0:
                        pool.wait_ge(sm_step, SM_STEPS)
                    pool.tensor_copy(coef[d][:], sm[:, d, pos(d, s, lat)]).then_inc(coef_done[d], 1)
                    pool.wait_ge(coef_done[d], s + 1)
                    after(pool, sta_done[d], 2 * s)
                    pool.tensor_tensor(rows[d][:], tri[:, d].rearrange("p (c j) -> p c j", c=2).unsqueeze(2)
                                       .broadcast_to([P, 2, NH, C]),
                                       coef[d][:, 0].unsqueeze(1).unsqueeze(3).broadcast_to([P, 2, NH, C]),
                                       ALU.mult).then_inc(tri_la_done[d], 1)
                for d in R2:
                    pool.wait_ge(l_done[d], s + 1)
                    pool.tensor_tensor(xx[d][:, 1], lmat[d][:], levmask[:, d, 0].unsqueeze(1).broadcast_to([P, NH, P]),
                                       ALU.mult).then_inc(x0_step[d], 1)
                    pool.wait_ge(x0_step[d], 2 * s + 1)
                    pool.tensor_tensor(xx[d][:, 1], K.ident[:].unsqueeze(1).broadcast_to([P, NH, P]), xx[d][:, 1],
                                       ALU.subtract).then_inc(x0_step[d], 1)
                if lat:
                    pool.wait_ge(wl_exp, s - TC + 1)
                    pool.wait_ge(ld_gq, 16 * (s - TC + 1))
                    pool.wait_ge(ld_g, 32 * (s + 1))
                    pool.tensor_tensor(wl[:].rearrange("p l x a n -> p l (x a n)"),
                                       wl[:].rearrange("p l x a n -> p l (x a n)"),
                                       gqk[:].rearrange("p x a n -> p (x a n)").unsqueeze(1).broadcast_to([P, LEVELS, 512]),
                                       ALU.mult).then_inc(wl_done, 1)
                if lat:
                    pool.wait_ge(exp_done, s - TC + 1)
                    pool.wait_ge(ld_gq, 16 * (s - TC + 1))
                    pool.tensor_tensor(qin[:].rearrange("p z a n -> p z (a n)"), qin[:].rearrange("p z a n -> p z (a n)"),
                                       gqk[:, 0].rearrange("p a n -> p (a n)").unsqueeze(1).broadcast_to([P, 2, 256]),
                                       ALU.mult).then_inc(qin_done, 1)
                for d in R2:
                    pool.wait_ge(ld_t[d], 32 * (s + 1))
                    after(pool, ds_ready[d], 2 * s)
                    for out_, in_, kind in ((bv, vt, 2), (bk, kt, 3), (kd, kt, 4)):
                        pool.tensor_tensor(out_[d][:], in_[d][:],
                                           coef[d][:, kind].unsqueeze(2).broadcast_to([P, NH, P]),
                                           ALU.mult).then_inc(scaled_done[d], 1)
                for d in R2:
                    pool.wait_ge(eg_done[d], s + 1)
                    if lat:
                        pool.wait_ge(ld_q[d], 16 * (s - TC + 1))
                        pool.tensor_tensor(qd[d][:].rearrange("p h (c j) -> p c h j", c=2),
                                           qc[d][:].rearrange("p h (c j) -> p c h j", c=2), rows[d][:],
                                           ALU.mult).then_inc(qd_done[d], 1)
                for n in R2:
                    for d in R2:
                        c = chunk_order(d)[n]
                        last = (C - 1, 0)[d]
                        after(pool, st_done[d], 2 * s + n)
                        pool.tensor_tensor(sta[d][:], st[d][:], rows[d][:, c, :, last:last + 1]
                                           .broadcast_to([P, NH, P]), ALU.mult).then_inc(sta_done[d], 1)
            steps(pool, step)

        @block.scalar
        def _(act):
            act.wait_ge(g_ready, 1)
            act.activation(sm[:, :, :, 1, :], px[0][:, 0:80].rearrange("p (d t h) -> p d t h", d=2, t=NT),
                           ACT.Copy).then_inc(sm_step, 1)
            act.activation(sm[:, :, :, 3, :], px[0][:, 0:80].rearrange("p (d t h) -> p d t h", d=2, t=NT),
                           ACT.Exp).then_inc(sm_step, 1)
            act.activation(sm[:, :, :, 4, :], px[0][:, 80:160].rearrange("p (d t h) -> p d t h", d=2, t=NT),
                           ACT.Exp).then_inc(og_out, 1)

            def step(s, lat):
                act.wait_ge(b_ready, s + 1)
                after(act, sub_done, s)
                act.activation(bs[:].rearrange("p z a n -> p (z a n)"), px[0][:], ACT.Copy,
                               scale=GLA_DECAY).then_inc(b_done, 1)
                act.wait_ge(b_done, s + 1)
                for z in R2:
                    end = (C - 1, 0)[z]
                    act.activation(K.ga_a[:, bass.ds(2 * s, 2), z, :].rearrange("p c a -> p a c"),
                                   bs[:, z].rearrange("p a (c j) -> p a c j", c=2)[:, :, :, end], ACT.Exp)
                if lat:
                    act.wait_ge(st_qin, 16 * (s - TC + 1))
                    act.activation(qin[:], bs[:], ACT.Exp).then_inc(exp_done, 1)
                for d in R2:
                    act.wait_ge(dec_in[d], 2 * (s + 1))
                    act.activation(dec[d][:], dec[d][:], ACT.Exp).then_inc(dec_done[d], 1)
                    act.activation(rows[d][:].rearrange("p c h j -> p (c h j)"), pa[d][:], ACT.Exp).then_inc(eg_done[d], 1)
                act.wait_ge(sub_done, s + 1)
                act.activation(kin[:], kin[:], ACT.Exp).then_inc(kin_exp, 1)
                if lat:
                    act.activation(wl[:], wl[:], ACT.Exp).then_inc(wl_exp, 1)
                act.wait_ge(kt_ready, s + 1)
                act.activation(kint[:].rearrange("p z a n -> p (z a n)"), px[0][:], ACT.Copy).then_inc(kt_out, 1)
                for c in R2:
                    act.wait_ge(gs_ready, 2 * s + c + 1)
                    act.activation(K.ga_st[:, bass.ds(2 * s + c, 1)].rearrange("p o z a n -> p (o z a n)"), px[c][:],
                                   ACT.Copy).then_inc(gs_out, 1)
                for d in R2:
                    act.wait_ge(uw_ready[d], s + 1)
                    act.activation(wtn[d][:].rearrange("p h j -> p (h j)"), pa[d][:], ACT.Copy, scale=-1.0).then_inc(wt_done[d], 1)
                if lat:
                    act.wait_ge(og_ready, s - TC + 1)
                    act.activation(K.xo[:, bass.ds(s - TC, 1), 0:V_A].rearrange("p o n -> p (o n)"), px[0][:],
                                   ACT.Copy).then_inc(og_out, 1)
            steps(act, step)

        @block.vector
        def _(dve):
            dve.tensor_copy(sm[:, :, :, 0, :], K.gdn_la[:]).then_inc(sm_step, 1)
            dve.tensor_copy(sm[:, :, :, 2, :], K.beta[:]).then_inc(sm_step, 1)
            dve.wait_ge(sm_step, SM_STEPS - 1)
            dve.wait_ge(og_out, 1)
            dve.tensor_tensor(sm[:, :, :, 3, :], sm[:, :, :, 3, :], K.beta[:], ALU.mult).then_inc(sm_step, 1)
            dve.wait_ge(init_done, 1)
            dve.wait_ge(ld_mask, 5 * 16)
            for d in R2:
                dve.sem_inc(o_done[d], 1)

            def step(s, lat):
                for d in R2:
                    dve.wait_ge(gr_ready[d], s + 1)
                    dve.tensor_tensor(lmat[d][:].rearrange("p h (c j) -> p h c j", c=2),
                                      pa[d][:].rearrange("p (c h j) -> p h c j", c=2, h=NH),
                                      coef[d][:, 1].unsqueeze(2).unsqueeze(3).broadcast_to([P, NH, 2, C]),
                                      ALU.subtract).then_inc(diff_done[d], 1)
                    dve.wait_ge(diff_done[d], s + 1)
                    dve.scalar_tensor_tensor(dec[d][:, 0], lmat[d][:], -1.0,
                                             negmask[:, d, 0].unsqueeze(1).broadcast_to([P, NH, P]),
                                             ALU.mult, ALU.min).then_inc(dec_in[d], 1)
                    dve.tensor_tensor(dec[d][:, 1], lmat[d][:], negmask[:, d, 1].unsqueeze(1).broadcast_to([P, NH, P]),
                                      ALU.min).then_inc(dec_in[d], 1)
                for d in R2:
                    dve.wait_ge(kq_ready[d], s + 1)
                    dve.wait_ge(dec_done[d], s + 1)
                    dve.tensor_tensor(lmat[d][:], dec[d][:, 0], pb[d][:].rearrange("p (h j) -> p h j", h=NH),
                                      ALU.mult).then_inc(kkd_done[d], 1)
                    if lat:
                        dve.tensor_tensor(atp[d][:], dec[d][:, 1], pc[d][:].rearrange("p (h j) -> p h j", h=NH),
                                          ALU.mult).then_inc(at_done[d], 1)
                    dve.wait_ge(kkd_done[d], s + 1)
                    dve.tensor_tensor(lmat[d][:], lmat[d][:], coef[d][:, 2].unsqueeze(2).broadcast_to([P, NH, P]),
                                      ALU.mult).then_inc(l_done[d], 1)
                dve.wait_ge(b_done, s + 1)
                bf = bs[:, 0].rearrange("p a n -> p (a n)")
                br = bs[:, 1].rearrange("p a n -> p (a n)")
                for z, (b, end) in enumerate(((bf, C - 1), (br, 0))):
                    bb = b.rearrange("p (m j) -> p m j", j=C)
                    last = dve.tensor_tensor(kin[:, z].rearrange("p a (c j) -> p (a c) j", j=C),
                                             bb[:, :, end:end + 1].broadcast_to([P, 4, C]), bb, ALU.subtract)
                if lat:
                    for lev in range(LEVELS):
                        h = 1 << lev
                        n = 256 // (2 * h)
                        f, r = (b.rearrange("p (m u j) -> p m u j", u=2, j=h) for b in (bf, br))
                        wq, wk = (wl[:, lev, x].rearrange("p a (m u j) -> p (a m) u j", u=2, j=h) for x in R2)
                        mid_f = f[:, :, 0, h - 1:h].broadcast_to([P, n, h])
                        mid_r = r[:, :, 1, 0:1].broadcast_to([P, n, h])
                        dve.tensor_tensor(wq[:, :, 1, :], f[:, :, 1, :], mid_f, ALU.subtract)
                        dve.tensor_tensor(wq[:, :, 0, :], r[:, :, 0, :], mid_r, ALU.subtract)
                        dve.tensor_tensor(wk[:, :, 0, :], mid_f, f[:, :, 0, :], ALU.subtract)
                        last = dve.tensor_tensor(wk[:, :, 1, :], mid_r, r[:, :, 1, :], ALU.subtract)
                last.then_inc(sub_done, 1)
                id4 = K.ident[:].unsqueeze(1).broadcast_to([P, NH, P])
                bank = lambda b: b[:].rearrange("p (h j) -> p h j", h=NH)
                mask = lambda d, lev: levmask[:, 1 - d, lev].unsqueeze(1).broadcast_to([P, NH, P])
                for d in R2:
                    dve.wait_ge(lt_ready[d], s + 1)
                    dve.tensor_tensor(yy[d][:], mask(d, 0), bank(pa[d]), ALU.mult).then_inc(y_done[d], 1)
                for d in R2:
                    dve.wait_ge(y_done[d], LEVELS * s + 1)
                    dve.tensor_tensor(xx[d][:, 0], id4, yy[d][:], ALU.subtract).then_inc(xt_done[d], 1)
                for lev in range(1, LEVELS):
                    for d in R2:
                        dve.wait_ge(y_ready[d], LAST_LEVEL * s + lev)
                        dve.tensor_tensor(yy[d][:], mask(d, lev), bank(pa[d]), ALU.mult).then_inc(y_done[d], 1)
                    for d in R2:
                        dve.wait_ge(p_ready[d], LAST_LEVEL * s + lev)
                        dve.tensor_tensor(xx[d][:, 0], xx[d][:, 0], bank(pb[d]), ALU.subtract).then_inc(xt_done[d], 1)
                        if lev < LAST_LEVEL:
                            dve.wait_ge(pt_ready[d], (LAST_LEVEL - 1) * s + lev)
                            dve.tensor_tensor(xx[d][:, 1], xx[d][:, 1], bank(pc[d]), ALU.subtract).then_inc(x_done[d], 1)
                    if lev == 1:
                        dve.wait_ge(kin_exp, s + 1)
                        dve.wait_ge(ld_g, 32 * (s + 1))
                        dve.tensor_tensor(kin[:].rearrange("p z a n -> p z (a n)"), kin[:].rearrange("p z a n -> p z (a n)"),
                                          gqk[:, 1].rearrange("p a n -> p (a n)").unsqueeze(1).broadcast_to([P, 2, 256]),
                                          ALU.mult).then_inc(io_done, 1)
                    if lat and lev >= 2:
                        hd = lev - 2
                        dve.wait_ge(sc_ready, NH * (s - TC) + hd + 1)
                        dve.tensor_tensor(msc[:, hd % 2].rearrange("p l j -> p (l j)"), px[1][:, :(LEVELS + 1) * C],
                                          smask[:].rearrange("p l j -> p (l j)"), ALU.mult).then_inc(msc_done, 1)
                        dve.wait_ge(msc_done, NH * (s - TC) + hd + 1)
                        for c in R2:
                            dve.tensor_reduce(atg[half(c), hd, half(c)], msc[half(c), hd % 2].rearrange("p l j -> p j l"),
                                              AX.X, ALU.add).then_inc(atg_done, 1)
                for n in R2:
                    for d in R2:
                        c = chunk_order(d)[n]
                        dve.wait_ge(ws_ready[d], 2 * s + n + 1)
                        dve.tensor_copy(delta[d][half(c)].rearrange("p h j -> p (h j)"), pc[d][half(c)]).then_inc(delta_done[d], 1)
                    for d in R2:
                        dve.wait_ge(ds_ready[d], 2 * s + n + 1)
                        dve.wait_ge(sta_done[d], 2 * s + n + 1)
                        dve.tensor_tensor(st[d][:].rearrange("p h j -> p (h j)"), sta[d][:].rearrange("p h j -> p (h j)"),
                                          pa[d][:], ALU.add).then_inc(st_done[d], 1)
                dve.wait_ge(gs_out, 2 * (s + 1))
                for c in R2:
                    if s + c == 0:
                        continue
                    if s + c > 1:
                        dve.wait_ge(scan, 2 * (2 * s + c - 1))
                    to = 2 * s + c
                    for a in R2:
                        dve.scalar_tensor_tensor(K.ga_st[:, to, 0, a], K.ga_st[:, to - 1, 0, a], K.ga_a[:, to, 0, a:a + 1],
                                                 K.ga_st[:, to, 0, a], ALU.mult, ALU.add).then_inc(scan, 1)
                if lat:
                    for d in R2:
                        o = K.xo[:, bass.ds(s - TC if d == 0 else 9 - s, 1), V_A:].rearrange("p o n -> p (o n)")
                        dve.wait_ge(o_ready[d], s - TC + 1)
                        dve.wait_ge(o_done[1 - d], s - TC + 1 + d)
                        dve.tensor_tensor(o, o, pb[d][:], ALU.add).then_inc(o_done[d], 1)
            steps(dve, step)

        @block.tensor
        def _(pe):
            pe.wait_ge(ld_mask, 5 * 16)
            for x, mask in enumerate((tri, trix)):
                for d in R2:
                    last = pe.matmul(px[0][:, 80 * x + 40 * d:80 * x + 40 * d + 40], mask[:, d],
                                     K.gdn_la[:, d].rearrange("p t h -> p (t h)"), start=True, stop=True)
            last.then_inc(g_ready, 1)
            pe.wait_ge(init_done, 1)

            def level_y(d, s, lev):
                pe.wait_ge(xt_done[d], LEVELS * s + lev)
                for h in range(NH):
                    last = pe.matmul(pa[d][:, h * P:(h + 1) * P], lmat[d][:, h], xx[d][:, 0, h], start=True, stop=True)
                last.then_inc(y_ready[d], 1)

            def level_p(d, s, lev, lat):
                pe.wait_ge(y_done[d], LEVELS * s + lev + 1)
                if lev == 1:
                    pe.wait_ge(x0_step[d], 2 * (s + 1))
                else:
                    pe.wait_ge(x_done[d], (LAST_LEVEL - 1) * s + lev - 1)
                for h in range(NH):
                    last = pe.matmul(pb[d][:, h * P:(h + 1) * P], xx[d][:, 1, h], yy[d][:, h], start=True, stop=True)
                last.then_inc(p_ready[d], 1)
                if lev < LAST_LEVEL:
                    if lat and lev == 1:
                        pe.wait_ge(at_done[d], s - TC + 1)
                    for h in range(NH):
                        last = pe.matmul(pc[d][:, h * P:(h + 1) * P], yy[d][:, h], xx[d][:, 1, h], start=True, stop=True)
                    last.then_inc(pt_ready[d], 1)

            def scores(s, hd):
                a, r = hd // 2, half(hd % 2)
                if hd == 0:
                    pe.wait_ge(wl_done, s - TC + 1)
                    after(pe, gs_out, 2 * s)
                else:
                    pe.wait_ge(msc_done, NH * (s - TC) + hd)
                for c in R2:
                    for lev in range(LEVELS + 1):
                        kk, qq = ((wl[r, lev, 1, a, half(c)], wl[r, lev, 0, a, half(c)]) if lev < LEVELS
                                  else (gqk[r, 1, a, half(c)], gqk[r, 0, a, half(c)]))
                        last = pe.matmul(px[1][half(c), lev * C:(lev + 1) * C], kk, qq, start=True, stop=True)
                last.then_inc(sc_ready, 1)

            def step(s, lat):
                for d in R2:
                    pe.wait_ge(tri_la_done[d], s + 1)
                    after(pe, st_done[d], 2 * s)
                    pe.matmul(pa[d][:], K.ones[:], rows[d][:].rearrange("p c h j -> p (c h j)"), start=True,
                              stop=True).then_inc(gr_ready[d], 1)
                pe.wait_ge(ld_la, 16 * (s + 1))
                after(pe, gs_out, 2 * s)
                pe.wait_ge(og_out, s - TC + 1 if lat else 1)
                for z in R2:
                    for a in R2:
                        last = pe.matmul(px[0][:, (2 * z + a) * P:(2 * z + a + 1) * P],
                                         gla[:, (2 * z + a) * P:(2 * z + a + 1) * P], tri[:, z], start=True, stop=True)
                last.then_inc(b_ready, 1)
                for d in R2:
                    pe.wait_ge(ld_k[d], 16 * (s + 1))
                    if lat:
                        pe.wait_ge(ld_q[d], 16 * (s - TC + 1))
                        pe.wait_ge(o_done[d], s - TC + 1)
                    after(pe, xt_done[d], LEVELS * s)
                    for h in range(NH):
                        last = pe.matmul(pb[d][:, h * P:(h + 1) * P], kc[d][:, h], kc[d][:, h], start=True, stop=True)
                    if lat:
                        pe.wait_ge(delta_done[d], 2 * s)
                        for h in range(NH):
                            last = pe.matmul(pc[d][:, h * P:(h + 1) * P], kc[d][:, h], qc[d][:, h], start=True, stop=True)
                    last.then_inc(kq_ready[d], 1)
                for d in R2:
                    pe.wait_ge(l_done[d], s + 1)
                    pe.wait_ge(eg_done[d], s + 1)
                    for h in range(NH):
                        last = pe.transpose(pa[d][:, h * P:(h + 1) * P], lmat[d][:, h], K.ident[:])
                    last.then_inc(lt_ready[d], 1)
                for lev in range(1, LEVELS):
                    for d in R2:
                        level_y(d, s, lev)
                    if lat and lev >= 2:
                        scores(s, lev - 2)
                    if lev == 2:
                        pe.wait_ge(ld_g, 32 * (s + 1))
                        pe.wait_ge(io_done, s + 1)
                        pe.wait_ge(b_done, s + 1)
                        for z in R2:
                            for a in R2:
                                last = pe.transpose(px[0][:, (2 * z + a) * P:(2 * z + a + 1) * P], kin[:, z, a], K.ident[:])
                        last.then_inc(kt_ready, 1)
                    for d in R2:
                        level_p(d, s, lev, lat)
                for c in R2:
                    pe.wait_ge(kt_out, s + 1)
                    if lat and c == 1:
                        pe.wait_ge(msc_done, NH * (s - TC + 1))
                    for z in R2:
                        for hd in range(NH):
                            a, x = hd // 2, hd % 2
                            last = pe.matmul(px[c][half(x), (2 * z + a) * P:(2 * z + a + 1) * P],
                                             kint[half(c), z, a, half(x)], gva[half(c), hd], start=True, stop=True)
                    last.then_inc(gs_ready, 1)
                for d in R2:
                    pe.wait_ge(xt_done[d], LEVELS * (s + 1))
                    pe.wait_ge(x_done[d], (LAST_LEVEL - 1) * (s + 1))
                    pe.wait_ge(scaled_done[d], 3 * (s + 1))
                    after(pe, delta_done[d], 2 * s)
                    for h in range(NH):
                        pe.matmul(pc[d][:, h * P:(h + 1) * P], xx[d][:, 0, h], bv[d][:, h], start=(h == 0), stop=False,
                                  skip_group_check=True)
                    for h in range(NH):
                        last = pe.matmul(pa[d][:, h * P:(h + 1) * P], bk[d][:, h], xx[d][:, 0, h], start=True, stop=True)
                    last.then_inc(uw_ready[d], 1)
                for n in R2:
                    for d in R2:
                        c = chunk_order(d)[n]
                        pe.wait_ge(wt_done[d], s + 1)
                        after(pe, st_done[d], 2 * s + n)
                        for h in range(NH):
                            last = pe.matmul(pc[d][half(c), h * P:(h + 1) * P], wtn[d][:, h, half(c)], st[d][:, h],
                                             start=False, stop=True, skip_group_check=True)
                        last.then_inc(ws_ready[d], 1)
                        if lat:
                            pe.wait_ge(qd_done[d], s - TC + 1)
                            for h in range(NH):
                                pe.matmul(pb[d][half(c), h * P:(h + 1) * P], qd[d][:, h, half(c)], st[d][:, h],
                                          start=(h == 0), stop=False, skip_group_check=True)
                    for d in R2:
                        c = chunk_order(d)[n]
                        pe.wait_ge(delta_done[d], 2 * s + n + 1)
                        if n == 1:
                            pe.wait_ge(st_done[d], 2 * s + 1)
                        for h in range(NH):
                            last = pe.matmul(pa[d][:, h * P:(h + 1) * P], kd[d][half(c), h], delta[d][half(c), h],
                                             start=True, stop=True)
                        last.then_inc(ds_ready[d], 1)
                if lat:
                    for d in R2:
                        pe.wait_ge(at_done[d], s - TC + 1)
                        for h in range(NH):
                            last = pe.matmul(pb[d][:, h * P:(h + 1) * P], atp[d][:, h], delta[d][:, h],
                                             start=False, stop=True, skip_group_check=True)
                        last.then_inc(o_ready[d], 1)
                    pe.wait_ge(atg_done, 2 * NH * (s - TC + 1))
                    pe.wait_ge(gs_out, 2 * s + 1)
                    for hd in range(NH):
                        last = pe.matmul(px[0][:, hd * P:(hd + 1) * P], atg[:, hd], gva[:, hd], start=True, stop=True)
                    last.then_inc(og_ready, 1)
            steps(pe, step)


def merge_phase(nc, A, K, S):
    with ExitStack() as ctx:
        m = Alloc(nc, ctx, "merge_")
        wraw = m.sb("wraw", [P, 2, D])
        whi, wlo = m.sb("wohi", [P, KT, D], F32R), m.sb("wolo", [P, KT, D], F32R)
        gt1 = m.sb("gt1", [P, D])
        diag = m.sb("diag", [P, 2, P])
        gains = m.sb("gains", [P, 2, P])
        qs = m.sb("qs", [P, 2, 2, 2, P])
        gates = m.sb("gates", [P, 2, D])
        xs = m.sb("mxs", [P, D])
        sq = m.sb("msq", [P, D])
        ss, var, lnv, rs = (m.sb(n, [P, 8]) for n in ("mss", "mvar", "mlnv", "mrs"))
        yhi, ylo = m.sb("yhi", [P, 2, KT, P], F32R), m.sb("ylo", [P, 2, KT, P], F32R)
        ps_o = m.ps("mps_o", [P, 2, 2, 512])
        ps_t = m.ps("mps_t", [P, 2, 512])
        ps_p = m.ps("mps_p", [P, 2, 512])
        row_bank = [ps_p[:, 0], ps_p[:, 1], ps_o[:, 1, 0], ps_o[:, 1, 1]]
        ld_wo, ld_gain = [m.sem("ld_wo0"), m.sem("ld_wo1")], m.sem("ld_gain")
        ld_qs, ld_gates = ([m.sem(f"{n}{b}") for b in range(2)] for n in ("ld_qs", "ld_gates"))
        ld_xs = m.sem("ld_xs")
        diag_done, diag_used, row_out = m.sem("diag_done"), m.sem("diag_used"), m.sem("mrow_out")
        wo_hi, wo_lo, gated = m.sem("wo_hi"), m.sem("wo_lo"), m.sem("gated")
        inter_ready, o_done, sq_done, ss_done = m.sem("inter_ready"), m.sem("mo_done"), m.sem("msq_done"), m.sem("mss_done")
        var_done, ln_done, rs_done = m.sem("mvar_done"), m.sem("mln_done"), m.sem("mrs_done")
        gain_done, norm_done, y_done = m.sem("gain_done"), m.sem("norm_done"), m.sem("my_done")
        t_ready, hi_done, lo_done = m.sem("mt_ready"), m.sem("mhi_done"), m.sem("mlo_done")
        p_ready, x1_done, scan = m.sem("mp_ready"), m.sem("x1_done"), m.sem("gla_scan")
        CTX_SCANS = 2 * (2 * TC - 1) + 1


        def tile(t):
            return TL - 1 - t

        block = ctx.enter_context(nc.Block())

        @block.sync
        def _(sp):
            for i, n in enumerate(("gla_norm_g", "gdn_norm_g")):
                sp.dma_start(gains[:, i], A[n].partition_broadcast(P).rearrange("p a n -> p (a n)")).then_inc(ld_gain, 16)

            def states_query(t):
                b = t % 2
                if t >= 2:
                    sp.wait_ge(inter_ready, t - 1)
                sp.dma_start(qs[:, b], S["qin"][tile(t)]).then_inc(ld_qs[b], 16)

            def gate(t):
                b = t % 2
                if t >= 2:
                    sp.wait_ge(y_done, t - 1)
                sp.dma_start(gates[:, b], S["gate"][tile(t)]).then_inc(ld_gates[b], 16)

            states_query(0)
            states_query(1)
            gate(0)
            for k in range(KT):
                if k >= 2:
                    sp.wait_ge(wo_lo, k - 1)
                sp.dma_start(wraw[:, k % 2], A["w_out"][k * P:(k + 1) * P]).then_inc(ld_wo[k % 2], 16)
            for t in range(TL):
                if t + 2 < TL:
                    states_query(t + 2)
                if t + 1 < TL:
                    gate(t + 1)
                if t:
                    sp.wait_ge(x1_done, 2 * t)
                sp.dma_start(xs[:], A["x"][tile(t) * P:(tile(t) + 1) * P]).then_inc(ld_xs, 16)

        @block.gpsimd
        def _(pool):
            def gain(t):
                pool.wait_ge(ld_gates[t % 2], 16 * (t // 2 + 1))
                g = gates[:, t % 2].rearrange("p (g h n) -> p g h n", g=2, h=NH)
                pool.tensor_tensor(g, g, gains[:].unsqueeze(2).broadcast_to([P, 2, NH, P]), ALU.mult).then_inc(gain_done, 1)

            pool.wait_ge(ld_gain, 32)
            gain(0)
            for k in range(KT):
                pool.wait_ge(wo_hi, k + 1)
                pool.tensor_tensor(wlo[:, k], wraw[:, k % 2], whi[:, k].bitcast(F32), ALU.subtract).then_inc(wo_lo, 1)
            for t in range(TL):
                pool.wait_ge(o_done, 2 * (t + 1))
                if t:
                    pool.wait_ge(ss_done, t)
                pool.tensor_tensor(sq[:], K.xo[:, tile(t)], K.xo[:, tile(t)], ALU.mult).then_inc(sq_done, 1)
                pool.wait_ge(norm_done, t + 1)
                pool.wait_ge(gain_done, t + 1)
                pool.tensor_tensor(K.xo[:, tile(t)], K.xo[:, tile(t)], gates[:, t % 2], ALU.mult).then_inc(y_done, 1)
                if t + 1 < TL:
                    gain(t + 1)

        @block.scalar
        def _(act):
            for r in range(4):
                act.wait_ge(diag_used, 4 * (r + 1))
                dst = gt1 if r < 2 else K.gt2
                act.activation(dst[:, (r % 2) * 512:(r % 2 + 1) * 512], row_bank[r], ACT.Copy).then_inc(row_out, 1)
            for k in range(KT):
                act.wait_ge(ld_wo[k % 2], 16 * (k // 2 + 1))
                act.activation(whi[:, k], wraw[:, k % 2], ACT.Copy).then_inc(wo_hi, 1)
            for t in range(TL):
                act.wait_ge(var_done, t + 1)
                act.activation(lnv[:], var[:], ACT.Ln).then_inc(ln_done, 1)
                act.wait_ge(ln_done, t + 1)
                act.activation(rs[:], lnv[:], ACT.Exp, scale=-0.5).then_inc(rs_done, 1)
                for i in range(2):
                    act.wait_ge(t_ready, 2 * t + i + 1)
                    if t >= 2:
                        act.wait_ge(p_ready, 2 * (t - 1))
                    act.activation(yhi[:, t % 2, 4 * i:4 * i + 4].rearrange("p k n -> p (k n)"), ps_t[:, i],
                                   ACT.Copy).then_inc(hi_done, 1)

        @block.vector
        def _(dve):
            for i in range(2 * KT):
                if i >= 2:
                    dve.wait_ge(diag_used, i - 1)
                dve.tensor_scalar(diag[:, i % 2], K.ident[:], K.mod[:, (16 if i < KT else 40) + i % KT, 0:1], None,
                                  ALU.mult).then_inc(diag_done, 1)

            def outputs(t):
                for i in range(2):
                    cs = slice(i * 512, (i + 1) * 512)
                    dve.wait_ge(p_ready, 2 * t + i + 1)
                    dve.tensor_tensor(K.xo[:, tile(t), cs], gt1[:, cs], ps_p[:, i], ALU.mult).then_inc(gated, 1)
                dve.wait_ge(ld_xs, 16 * (t + 1))
                for i in range(2):
                    cs = slice(i * 512, (i + 1) * 512)
                    dve.wait_ge(gated, 2 * t + i + 1)
                    dve.tensor_tensor(K.xo[:, tile(t), cs], K.xo[:, tile(t), cs], xs[:, cs], ALU.add).then_inc(x1_done, 1)

            def norms(t):
                dve.wait_ge(inter_ready, t + 1)
                for x in range(2):
                    o = K.xo[:, tile(t), 0:V_A].rearrange("p (a x n) -> p a x n", a=2, x=2)[:, :, x]
                    dve.tensor_tensor(o, o, ps_o[:, t % 2, x, 0:2 * P].rearrange("p (a n) -> p a n", a=2),
                                      ALU.add).then_inc(o_done, 1)
                dve.wait_ge(sq_done, t + 1)
                dve.tensor_reduce(ss[:], sq[:].rearrange("p (h n) -> p h n", n=P), AX.X, ALU.add).then_inc(ss_done, 1)
                dve.wait_ge(ss_done, t + 1)
                dve.tensor_scalar(var[:], ss[:], 1.0 / P, EPS, ALU.mult, ALU.add).then_inc(var_done, 1)
                dve.wait_ge(rs_done, t + 1)
                o = K.xo[:, tile(t)].rearrange("p (h n) -> p h n", n=P)
                dve.tensor_tensor(o, o, rs[:].unsqueeze(2).broadcast_to([P, 8, P]), ALU.mult).then_inc(norm_done, 1)

            def low(t):
                for i in range(2):
                    dve.wait_ge(hi_done, 2 * t + i + 1)
                    hi = yhi[:, t % 2, 4 * i:4 * i + 4].rearrange("p k n -> p (k n)")
                    dve.tensor_tensor(ylo[:, t % 2, 4 * i:4 * i + 4].rearrange("p k n -> p (k n)"), ps_t[:, i], hi.bitcast(F32),
                                      ALU.subtract).then_inc(lo_done, 1)

            def advance(to, done):
                if done:
                    dve.wait_ge(scan, done)
                for a in range(2):
                    dve.scalar_tensor_tensor(K.ga_st[:, to, 1, a], K.ga_st[:, to + 1, 1, a], K.ga_a[:, to, 1, a:a + 1],
                                             K.ga_st[:, to, 1, a], ALU.mult, ALU.add).then_inc(scan, 1)

            def states(t):
                top = 2 * (tile(t) + TC) + 2
                for to in ((top, top - 1) if t else (top - 1,)):
                    advance(to, CTX_SCANS + 2 * (2 * NT - 1 - to))

            for i in range(2 * TC - 1):
                advance(2 * TC - 2 - i, 2 * i)
            dve.wait_ge(scan, CTX_SCANS - 1)
            dve.tensor_copy(K.ga_st[:, 2 * NT, 1], K.ga_st[:, 0, 1]).then_inc(scan, 1)
            for t in range(3):
                states(t)
            norms(0)
            norms(1)
            dve.wait_ge(row_out, 2)
            for t in range(TL):
                low(t)
                if t + 3 < TL:
                    states(t + 3)
                if t + 2 < TL:
                    norms(t + 2)
                outputs(t)

        @block.tensor
        def _(pe):
            for i in range(2 * KT):
                pe.wait_ge(diag_done, i + 1)
                last = pe.matmul(row_bank[i // 4][:, (i % 4) * P:(i % 4 + 1) * P], K.ones[:], diag[:, i % 2],
                                 start=True, stop=True)
                last.then_inc(diag_used, 1)

            def inter(t):
                pe.wait_ge(scan, CTX_SCANS + 2 * (2 * NT - 1 - 2 * (tile(t) + TC)))
                pe.wait_ge(ld_qs[t % 2], 16 * (t // 2 + 1))
                if t == 1:
                    pe.wait_ge(row_out, 4)
                if t >= 2:
                    pe.wait_ge(o_done, 2 * (t - 1))
                for c in range(2):
                    cc, toks = 2 * (tile(t) + TC) + c, slice(c * C, (c + 1) * C)
                    for hd in range(NH):
                        a, x = hd // 2, hd % 2
                        r = slice(x * C, (x + 1) * C)
                        for z in range(2):
                            last = pe.matmul(ps_o[toks, t % 2, x, a * P:(a + 1) * P], qs[r, t % 2, z, a, toks],
                                             K.ga_st[r, cc - 1 if z == 0 else cc + 1, z, a], start=(z == 0), stop=(z == 1))
                last.then_inc(inter_ready, 1)

            def turn(t):
                pe.wait_ge(y_done, t + 1)
                if t:
                    pe.wait_ge(lo_done, 2 * t)
                for i in range(2):
                    for j in range(4):
                        last = pe.transpose(ps_t[:, i, j * P:(j + 1) * P],
                                            K.xo[:, tile(t), (4 * i + j) * P:(4 * i + j + 1) * P], K.ident[:])
                    last.then_inc(t_ready, 1)

            inter(0)
            inter(1)
            turn(0)
            pe.wait_ge(wo_lo, KT)
            for t in range(TL):
                if t + 2 < TL:
                    inter(t + 2)
                pe.wait_ge(lo_done, 2 * (t + 1))
                if t:
                    pe.wait_ge(gated, 2 * t)
                for i in range(2):
                    cs = slice(i * 512, (i + 1) * 512)
                    for k in range(KT):
                        last = mm3(pe, ps_p[:, i], yhi[:, t % 2, k], ylo[:, t % 2, k], whi[:, k, cs], wlo[:, k, cs],
                                   k == 0, k == KT - 1)
                    last.then_inc(p_ready, 1)
                    if i == 0 and t + 1 < TL:
                        turn(t + 1)


def mlp_phase(nc, A, K, S, out):
    GJ = 4
    NG = FF // (GJ * P)
    with ExitStack() as ctx:
        m = Alloc(nc, ctx, "mlp_")
        h2hi, h2lo = m.sb("h2hi", [P, KT, NLAT], F32R), m.sb("h2lo", [P, KT, NLAT], F32R)
        ss, var, lnv, rstd = (m.sb(n, [P, TL]) for n in ("fss", "fvar", "flnv", "frstd"))
        sc2 = m.sb("sc2", [P, KT])
        tmp = m.sb("ftmp", [P, 2, 512])
        with ExitStack() as ctx_in:
            mi = Alloc(nc, ctx_in, "mlp_in_")
            xn = mi.sb("fxn", [P, TL, D])
            junk = mi.sb("fjunk", [P, D])
            ps = mi.ps("fps_t", [P, 4, 512])
            ss_done, var_done, ln_done, rstd_done = (mi.sem(n) for n in ("fss_done", "fvar_done", "fln_done", "frstd_done"))
            sc_done, xn_done, t_ready = mi.sem("fsc_done"), mi.sem("fxn_done"), mi.sem("ft_ready")
            hf_done, hi_done, lo_done = mi.sem("fhf_done"), mi.sem("fhi_done"), mi.sem("flo_done")
            units = [(k, s) for s in range(2) for k in range(KT)]
            block = ctx_in.enter_context(nc.Block())

            @block.scalar
            def _(act):
                for t in range(TL):
                    if t:
                        act.wait_ge(ss_done, t)
                    act.activation(junk[:], K.xo[:, t], ACT.Square, accum_out=ss[:, t:t + 1]).then_inc(ss_done, 1)
                    if t % 4 == 3:
                        hs = slice(t - 3, t + 1)
                        act.wait_ge(var_done, t // 4 + 1)
                        act.activation(lnv[:, hs], var[:, hs], ACT.Ln).then_inc(ln_done, 1)
                        act.wait_ge(ln_done, t // 4 + 1)
                        act.activation(rstd[:, hs], lnv[:, hs], ACT.Exp, scale=-0.5).then_inc(rstd_done, 1)
                for u, (k, s) in enumerate(units):
                    act.wait_ge(hf_done, u + 1)
                    act.activation(h2hi[:, k, s * 512:(s + 1) * 512], tmp[:, u % 2], ACT.Copy).then_inc(hi_done, 1)

            @block.vector
            def _(dve):
                dve.tensor_scalar(sc2[:], K.mod[:, 32:40, 0], 1.0, None, ALU.add).then_inc(sc_done, 1)
                dve.wait_ge(sc_done, 1)
                dve.tensor_tensor(sc2[:], sc2[:], K.cols[:, 56:64], ALU.mult).then_inc(sc_done, 1)
                for hlf in range(2):
                    hs = slice(4 * hlf, 4 * hlf + 4)
                    dve.wait_ge(ss_done, 4 * hlf + 4)
                    dve.tensor_scalar(var[:, hs], ss[:, hs], 1.0 / D, EPS, ALU.mult, ALU.add).then_inc(var_done, 1)
                    dve.wait_ge(rstd_done, hlf + 1)
                    for t in range(4 * hlf, 4 * hlf + 4):
                        dve.tensor_scalar(xn[:, t], K.xo[:, t], rstd[:, t:t + 1], None, ALU.mult).then_inc(xn_done, 1)
                dve.wait_ge(sc_done, 2)
                for u, (k, s) in enumerate(units):
                    dve.wait_ge(t_ready, u + 1)
                    if u >= 2:
                        dve.wait_ge(lo_done, u - 1)
                    dve.tensor_scalar(tmp[:, u % 2], ps[:, u % 4], sc2[:, k:k + 1], K.mod[:, 24 + k, 0:1],
                                      ALU.mult, ALU.add).then_inc(hf_done, 1)

            @block.gpsimd
            def _(pool):
                for u, (k, s) in enumerate(units):
                    cs = slice(s * 512, (s + 1) * 512)
                    pool.wait_ge(hi_done, u + 1)
                    pool.tensor_tensor(h2lo[:, k, cs], tmp[:, u % 2], h2hi[:, k, cs].bitcast(F32),
                                       ALU.subtract).then_inc(lo_done, 1)

            @block.tensor
            def _(pe):
                for u, (k, s) in enumerate(units):
                    pe.wait_ge(xn_done, 4 * s + 4)
                    if u >= 4:
                        pe.wait_ge(hf_done, u - 3)
                    for i in range(4):
                        last = pe.transpose(ps[:, u % 4, i * P:(i + 1) * P], xn[:, 4 * s + i, k * P:(k + 1) * P], K.ident[:])
                    last.then_inc(t_ready, 1)

        hhi, hlo = m.sb("hidhi", [P, GJ, NLAT], F32R), m.sb("hidlo", [P, GJ, NLAT], F32R)
        w1raw = m.sb("w1raw", [P, 2, KT, P])
        w1hi, w1lo = m.sb("w1hi", [P, 2, KT, P], F32R), m.sb("w1lo", [P, 2, KT, P], F32R)
        w2raw = m.sb("w2raw", [P, D])
        w2hi, w2lo = m.sb("w2hi", [P, GJ, D], F32R), m.sb("w2lo", [P, GJ, D], F32R)
        ps_a = m.ps("fps_a", [P, 4, 512])
        ps_b = m.ps("fps_b", [P, 4, 512])
        ld_w1, ld_w2 = [m.sem("ld_w1_0"), m.sem("ld_w1_1")], m.sem("ld_w2")
        w1_hi, w1_lo, w2_scaled, w2_hi, w2_lo = (m.sem(n) for n in ("w1_hi", "w1_lo", "w2_scaled", "w2_hi", "w2_lo"))
        a_ready, relu_done, sq_done, hid_hi, hid_lo = (m.sem(n) for n in ("a_ready", "relu_done", "fsq_done", "hid_hi", "hid_lo"))
        b_ready, x2_done = m.sem("b_ready"), m.sem("x2_done")
        gss, gvar, glnv, grstd = (m.sb(n, [P, TL]) for n in ("gss", "gvar", "glnv", "grstd"))
        gain = w1raw[:, 0].rearrange("p k n -> p (k n)")
        ld_gain, gss_done, gvar_done, gln_done, grstd_done, y_done = (
            m.sem(n) for n in ("ld_fgain", "gss_done", "gvar_done", "gln_done", "grstd_done", "gy_done"))
        NO = 2 * TL

        def after(eng, sem, n):
            if not isinstance(n, int) or n > 0:
                eng.wait_ge(sem, n)

        def groups(eng, body):
            for g in range(NG):
                body(g, g == NG - 1)

        block = ctx.enter_context(nc.Block())

        @block.sync
        def _(sp):
            w1v = A["w_ff1"].rearrange("(k p) f -> p k f", p=P)

            def load_w1(g, j):
                f = GJ * g + j
                after(sp, w1_lo, f - 1)
                sp.dma_start(w1raw[:, j % 2], w1v[:, :, bass.ds(f * P, P)]).then_inc(ld_w1[j % 2], 16)

            def group(g, last):
                for j in range(GJ):
                    f = GJ * g + j
                    after(sp, w2_lo, f)
                    sp.dma_start(w2raw[:], A["w_ff2"][bass.ds(f * P, P)]).then_inc(ld_w2, 16)
                    if not (last and j == GJ - 1):
                        load_w1(g if j < GJ - 1 else g + 1, (j + 1) % GJ)

            load_w1(0, 0)
            groups(sp, group)
            sp.wait_ge(w1_lo, GJ * NG - 1)
            sp.dma_start(gain, A["final_norm_g"].partition_broadcast(P)).then_inc(ld_gain, 16)
            for t in range(TL):
                sp.wait_ge(y_done, t + 1)
                sp.dma_start(out[t * P:(t + 1) * P], K.xo[:, t]).then_inc(K.stored, 16)
            sp.wait_ge(K.stored, 16 * TL)

        @block.gpsimd
        def _(pool):
            def low_w1(g, j):
                f = GJ * g + j
                pool.wait_ge(w1_hi, f + 1)
                pool.tensor_tensor(w1lo[:, j % 2], w1raw[:, j % 2], w1hi[:, j % 2].bitcast(F32),
                                   ALU.subtract).then_inc(w1_lo, 1)

            def group(g, last):
                for j in range(GJ):
                    f = GJ * g + j
                    if not (last and j == GJ - 1):
                        low_w1(g if j < GJ - 1 else g + 1, (j + 1) % GJ)
                    for i in range(2):
                        cs = slice(i * 512, (i + 1) * 512)
                        pool.wait_ge(hid_hi, 2 * f + i + 1)
                        pool.tensor_tensor(hlo[:, j, cs], tmp[:, i], hhi[:, j, cs].bitcast(F32),
                                           ALU.subtract).then_inc(hid_lo, 1)

            low_w1(0, 0)
            groups(pool, group)

        @block.scalar
        def _(act):
            def high_w1(g, j):
                f = GJ * g + j
                after(act, a_ready, 2 * (f - 1))
                act.wait_ge(ld_w1[j % 2], 16 * (2 * g + j // 2 + 1))
                act.activation(w1hi[:, j % 2], w1raw[:, j % 2], ACT.Copy).then_inc(w1_hi, 1)

            def group(g, last):
                for j in range(GJ):
                    f = GJ * g + j
                    if not (last and j == GJ - 1):
                        high_w1(g if j < GJ - 1 else g + 1, (j + 1) % GJ)
                    for i in range(2):
                        after(act, hid_lo, 2 * f + i - 1)
                        act.wait_ge(a_ready, 2 * f + i + 1)
                        act.activation(tmp[:, i], ps_a[:, (2 * j + i) % 4], ACT.Relu).then_inc(relu_done, 1)
                    for i in range(2):
                        act.wait_ge(sq_done, 2 * f + i + 1)
                        if j == 0 and i == 0:
                            after(act, b_ready, NO * g)
                        act.activation(hhi[:, j, i * 512:(i + 1) * 512], tmp[:, i], ACT.Copy).then_inc(hid_hi, 1)
                    act.wait_ge(w2_scaled, f + 1)
                    act.activation(w2hi[:, j], w2raw[:], ACT.Copy).then_inc(w2_hi, 1)

            high_w1(0, 0)
            groups(act, group)
            act.wait_ge(hid_lo, 2 * GJ * NG)
            for t in range(TL):
                act.wait_ge(x2_done, NO * (NG - 1) + 2 * (t + 1))
                if t:
                    act.wait_ge(gss_done, t)
                act.activation(tmp[:].rearrange("p i n -> p (i n)"), K.xo[:, t], ACT.Square,
                               accum_out=gss[:, t:t + 1]).then_inc(gss_done, 1)
                act.wait_ge(gvar_done, t + 1)
                act.activation(glnv[:, t:t + 1], gvar[:, t:t + 1], ACT.Ln).then_inc(gln_done, 1)
                act.wait_ge(gln_done, t + 1)
                act.activation(grstd[:, t:t + 1], glnv[:, t:t + 1], ACT.Exp, scale=-0.5).then_inc(grstd_done, 1)

        @block.vector
        def _(dve):
            def variance(t):
                dve.wait_ge(gss_done, t + 1)
                dve.tensor_scalar(gvar[:, t:t + 1], gss[:, t:t + 1], 1.0 / D, EPS, ALU.mult, ALU.add).then_inc(gvar_done, 1)

            def final(t):
                dve.wait_ge(grstd_done, t + 1)
                dve.scalar_tensor_tensor(K.xo[:, t], K.xo[:, t], grstd[:, t:t + 1], gain, ALU.mult,
                                         ALU.mult).then_inc(y_done, 1)

            def group(g, last):
                for j in range(GJ):
                    f = GJ * g + j
                    dve.wait_ge(ld_w2, 16 * (f + 1))
                    dve.tensor_tensor(w2raw[:], w2raw[:], K.gt2[:], ALU.mult).then_inc(w2_scaled, 1)
                    for i in range(2):
                        dve.wait_ge(relu_done, 2 * f + i + 1)
                        dve.tensor_tensor(tmp[:, i], tmp[:, i], tmp[:, i], ALU.mult).then_inc(sq_done, 1)
                    dve.wait_ge(w2_hi, f + 1)
                    dve.tensor_tensor(w2lo[:, j], w2raw[:], w2hi[:, j].bitcast(F32), ALU.subtract).then_inc(w2_lo, 1)
                for o in range(NO):
                    x = K.xo[:, o // 2, (o % 2) * 512:(o % 2 + 1) * 512]
                    dve.wait_ge(b_ready, NO * g + o + 1)
                    if o == 0:
                        after(dve, x2_done, NO * g)
                    dve.tensor_tensor(x, x, ps_b[:, o % 4], ALU.add).then_inc(x2_done, 1)
                    if last and o % 4 == 3:
                        if o == 3:
                            dve.wait_ge(ld_gain, 16)
                        for t in (o // 2 - 1, o // 2):
                            if t >= 2:
                                final(t - 2)
                            variance(t)
            groups(dve, group)
            final(TL - 2)
            final(TL - 1)

        @block.tensor
        def _(pe):
            def group(g, last):
                for j in range(GJ):
                    f = GJ * g + j
                    pe.wait_ge(w1_lo, f + 1)
                    for i in range(2):
                        after(pe, relu_done, 2 * f + i - 3)
                        for k in range(KT):
                            done = mm3(pe, ps_a[:, (2 * j + i) % 4], w1hi[:, j % 2, k], w1lo[:, j % 2, k],
                                       h2hi[:, k, i * 512:(i + 1) * 512], h2lo[:, k, i * 512:(i + 1) * 512],
                                       k == 0, k == KT - 1)
                        done.then_inc(a_ready, 1)
                for q in range(NO // 4):
                    for part in (range(GJ - 1), range(GJ - 1, GJ)):
                        for o in range(4 * q, 4 * q + 4):
                            t, cs = o // 2, slice((o % 2) * 512, (o % 2 + 1) * 512)
                            if part[0] == 0:
                                after(pe, x2_done, NO * g + o - 3)
                            for j in part:
                                f = GJ * g + j
                                if o == 4 * q:
                                    pe.wait_ge(w2_lo, f + 1)
                                    pe.wait_ge(hid_lo, 2 * f + (1 if t < 4 else 2))
                                done = mm3(pe, ps_b[:, o % 4], hhi[:, j, t * P:(t + 1) * P], hlo[:, j, t * P:(t + 1) * P],
                                           w2hi[:, j, cs], w2lo[:, j, cs], j == 0, j == GJ - 1)
                            if part[0]:
                                done.then_inc(b_ready, 1)
            groups(pe, group)



def masks():
    t = np.arange(P)
    same = t[:, None] // C == t[None, :] // C
    tri = np.stack([same & (t[:, None] <= t[None, :]), same & (t[:, None] >= t[None, :])], 1)
    trix = np.stack([same & (t[:, None] > t[None, :]), same & (t[:, None] < t[None, :])], 1)
    p, f = (t % C)[:, None], np.arange(C)[None, :]
    neg = np.float32(-1e30)
    below, above = same & (t[None, :] <= t[:, None]), same & (t[None, :] >= t[:, None])
    valid = np.stack([np.stack([below, above], 1), np.stack([above, below], 1)], 1)
    lev, smask = [], []
    for h in (1, 2, 4, 8, 16, 32):
        block = p // (2 * h) == f // (2 * h)
        up_p, up_f = p % (2 * h) >= h, f % (2 * h) >= h
        up = t % (2 * h) >= h
        pair = t[:, None] // (2 * h) == t[None, :] // (2 * h)
        lev.append(np.stack([pair & up[:, None] & ~up[None, :], pair & ~up[:, None] & up[None, :]], 1))
        smask.append(block & (up_p != up_f))
    smask = [x.astype(np.float32) for x in smask] + [2.0 * (p == f).astype(np.float32)]
    f32 = lambda x: np.ascontiguousarray(x, dtype=np.float32)
    return {"k_ident": np.eye(P, dtype=np.float32), "k_tri": f32(tri), "k_trix": f32(trix),
            "k_negmask": f32(np.where(valid, np.float32(0), neg)),
            "k_levmask": f32(np.stack(lev, 2)), "k_smask": f32(np.stack(smask, 1))}


class Kept:
    pass


def hybrid_block(nc, A, out):
    dram = {"k": [NT, P, NH, P], "q": [NT, P, NH, P], "kt": [NT, P, NH, P], "vt": [NT, P, NH, P],
            "ga_k": [NT, P, 2, P], "ga_q": [NT, P, 2, P], "va": [NT, P, V_A], "la": [NT, P, 512],
            "gate": [TL, P, 2 * V_A], "qin": [TL, P, 2, 2, P]}
    S = {n: nc.dram_tensor("s_" + n, s, F32, kind=SCRATCH).ap() for n, s in dram.items()}
    K = Kept()
    with ExitStack() as ctx:
        m = Alloc(nc, ctx)
        K.stored = ctx.enter_context(nc.semaphore("stored"))
        K.ident = m.sb("ident", [P, P])
        K.ones = m.sb("ones", [P, P])
        K.cols = m.sb("cols", [P, 100])
        K.mod = m.sb("mod", [P, 48, 2])
        K.gdn_la = m.sb("gdn_la", [P, 2, NT, NH])
        K.beta = m.sb("beta", [P, 2, NT, NH])
        with ExitStack() as ctx_h:
            mh = Alloc(nc, ctx_h)
            K.hhi = mh.sb("hhi", [P, KT, NTOK], F32R)
            K.hlo = mh.sb("hlo", [P, KT, NTOK], F32R)
            modulate_phase(nc, A, K, S)
            project_phase(nc, A, K, S)
        K.xo = m.sb("xo", [P, TL, D])
        K.gt2 = m.sb("gt2", [P, D])
        with ExitStack() as ctx_s:
            ms = Alloc(nc, ctx_s)
            K.ga_st = ms.sb("ga_st", [P, 2 * NT + 1, 2, 2, P])
            K.ga_a = ms.sb("ga_a", [P, 2 * NT, 2, 2])
            mix_phase(nc, A, K, S)
            merge_phase(nc, A, K, S)
        mlp_phase(nc, A, K, S, out)


def kernel(**inputs):
    import concourse.bacc as bacc
    from concourse.bass_utils import run_bass_kernel_spmd

    nc = bacc.Bacc("TRN2", target_bir_lowering=False, num_devices=1)
    arrays = {n: np.ascontiguousarray(a) for n, a in inputs.items()}
    arrays["x"] = arrays["x"].reshape(NLAT, D)
    arrays["ctx"] = arrays["ctx"].reshape(NCTX, D)
    for n in ("w_ada", "w_in", "gla_w_lr", "gla_b_lr", "gdn_a_log", "gdn_dt_bias", "w_out", "w_ff1", "w_ff2"):
        arrays[n] = arrays[n].reshape(arrays[n].shape[1:])
    arrays.update(masks())
    A = {n: nc.dram_tensor("in_" + n, a.shape, F32, kind="ExternalInput").ap() for n, a in arrays.items()}
    out = nc.dram_tensor("out", (NLAT, D), F32, kind="ExternalOutput").ap()
    hybrid_block(nc, A, out)
    got = run_bass_kernel_spmd(nc, [{"in_" + n: a for n, a in arrays.items()}], core_ids=[0])
    res = got.results[0]
    y = res["out"].reshape(1, NLAT, D)
    return y
```
